# Optimizing a Trainium2 kernel written in Bass

```python
import math
import jax, jax.numpy as jnp
from jax import lax
import numpy as np

D_MODEL = 1024
BATCH = 1
SEQ = 128
DEPTH = 1
DEC_BATCH = 1
DEC_SEQ = 1024
PAST_LEN = 128

GRID_W = 64
D_MIX = D_MODEL
D_POOL = D_MIX // 2
D_LRU = D_MIX - D_POOL
D_IN = D_POOL + 2 * D_LRU
POOL_WINDOWS = (2, 4, 8, 16)
N_POOL_GROUPS = len(POOL_WINDOWS)
POOL_GROUP_W = D_POOL // N_POOL_GROUPS
N_LRU_HEADS = 8
LRU_HEAD_DIM = D_LRU // N_LRU_HEADS
CONV_W = 4
CONV_LEFT = CONV_W // 2
LRU_C = 8.0
N_EXPERTS = 16
EC_FACTOR = 2
D_EXPERT = 1024
N_MOD = 6
EPS = 1e-6

kernel_name = "hybrid_pool_rglru_ec_diffusion_step"

def _rmsnorm(x, g):
    xf = x.astype(jnp.float32)
    y = xf * lax.rsqrt(jnp.mean(xf * xf, axis=-1, keepdims=True) + EPS)
    return (y * g.astype(jnp.float32)).astype(x.dtype)

def _window_mean(u, w, axis):
    u0 = jnp.moveaxis(u, axis, 0)
    L = u0.shape[0]
    uf = u0.astype(jnp.float32)
    cs = jnp.concatenate([jnp.zeros_like(uf[:1]), jnp.cumsum(uf, axis=0)], axis=0)
    t = jnp.arange(L)
    lo = jnp.clip(t - w // 2, 0, L)
    hi = jnp.clip(t + (w - w // 2), 0, L)
    cnt = (hi - lo).astype(jnp.float32).reshape((L,) + (1,) * (u0.ndim - 1))
    m = (cs[hi] - cs[lo]) / cnt
    return jnp.moveaxis(m.astype(u.dtype), 0, axis)

def _pool_mixer(u, rows, w_pool, pool_scale):
    B, L, _ = u.shape
    ug = u.reshape(B, L, N_POOL_GROUPS, POOL_GROUP_W)
    outs = []
    for g, w in enumerate(POOL_WINDOWS):
        x_g = ug[:, :, g, :]
        if rows is None:
            m = _window_mean(x_g, w, 1)
        else:
            grid = x_g.reshape(B, rows, GRID_W, POOL_GROUP_W)
            m = _window_mean(_window_mean(grid, w, 2), w, 1).reshape(B, L, POOL_GROUP_W)
        outs.append(m - x_g)
    d = jnp.stack(outs, axis=2)
    y = jnp.einsum('blgc,gcd->blgd', d, w_pool).reshape(B, L, D_POOL)
    return y * pool_scale

def _conv_centred(x, w_conv, b_conv):
    L = x.shape[1]
    xp = jnp.pad(x, ((0, 0), (CONV_LEFT, CONV_W - 1 - CONV_LEFT), (0, 0)))
    y = b_conv
    for k in range(CONV_W):
        y = y + w_conv[k] * xp[:, k:k + L, :]
    return y

def _lin_combine(e1, e2):
    a1, b1 = e1
    a2, b2 = e2
    return a1 * a2, a2 * b1 + b2

def _rglru(xc, w_a, b_a, w_x, b_x, lam, h0, reverse):
    B, L, C = xc.shape
    xh = xc.reshape(B, L, N_LRU_HEADS, LRU_HEAD_DIM)
    r = jax.nn.sigmoid(jnp.einsum('blhi,hij->blhj', xh, w_a) + b_a).reshape(B, L, C)
    i = jax.nn.sigmoid(jnp.einsum('blhi,hij->blhj', xh, w_x) + b_x).reshape(B, L, C)
    log_a = -LRU_C * r.astype(jnp.float32) * jax.nn.softplus(-lam.astype(jnp.float32))
    a = jnp.exp(log_a)
    mult = jnp.sqrt(jnp.maximum(-jnp.expm1(2.0 * log_a), 0.0))
    b = mult * (i * xc).astype(jnp.float32)
    A, Bc = lax.associative_scan(_lin_combine, (a, b), axis=1, reverse=reverse)
    return A * h0.astype(jnp.float32)[:, None, :] + Bc

def _ec_moe(h, w_router, w_exp_gate, w_exp_up, w_exp_down):
    B, L, D = h.shape
    N = B * L
    flat = h.reshape(N, D)
    aff = jax.nn.softmax(jnp.einsum('nd,de->ne', flat, w_router).astype(jnp.float32), axis=-1)
    cap = EC_FACTOR * N // N_EXPERTS
    g, idx = lax.top_k(aff.T, cap)
    xs = flat[idx]
    hid = jax.nn.silu(jnp.einsum('ecd,edf->ecf', xs, w_exp_gate)) * jnp.einsum('ecd,edf->ecf', xs, w_exp_up)
    out = jnp.einsum('ecf,efd->ecd', hid, w_exp_down) * g[..., None].astype(h.dtype)
    y = jnp.zeros((N, D), h.dtype).at[idx.reshape(-1)].add(out.reshape(-1, D))
    return y.reshape(B, L, D)

def _layer(x, mod, h0, rows, p, want_state):
    shift1, scale1, gate1, shift2, scale2, gate2 = jnp.split(mod, N_MOD, axis=-1)
    hn = _rmsnorm(x, p['g_norm_mix']) * (1 + scale1) + shift1
    proj = jnp.einsum('bld,dk->blk', hn, p['w_in'])
    u_pool = proj[..., :D_POOL]
    u_lru = proj[..., D_POOL:D_POOL + D_LRU]
    u_gate = proj[..., D_POOL + D_LRU:]
    y_pool = _pool_mixer(u_pool, rows, p['w_pool'], p['pool_scale'])
    xc = _conv_centred(u_lru, p['w_conv'], p['b_conv'])
    hf = _rglru(xc, p['w_gate_a'][0], p['b_gate_a'][0], p['w_gate_x'][0], p['b_gate_x'][0], p['lru_lambda'][0], h0[:, 0], False)
    hb = _rglru(xc, p['w_gate_a'][1], p['b_gate_a'][1], p['w_gate_x'][1], p['b_gate_x'][1], p['lru_lambda'][1], h0[:, 1], True)
    y_lru = jax.nn.gelu(u_gate) * (hf + hb).astype(x.dtype)
    mix = jnp.einsum('blk,kd->bld', jnp.concatenate([y_pool, y_lru], axis=-1), p['w_out'])
    x = x + gate1 * mix
    hn2 = _rmsnorm(x, p['g_norm_ffn']) * (1 + scale2) + shift2
    x = x + gate2 * _ec_moe(hn2, p['w_router'], p['w_exp_gate'], p['w_exp_up'], p['w_exp_down'])
    if want_state:
        st = jnp.stack([hf[:, -1], hb[:, 0]], axis=1).astype(x.dtype)
        return x, st
    return x, None

def setup_inputs(seed: int = 0) -> dict:
    key = jax.random.key(seed)
    ks = jax.random.split(key, 32)
    f32 = jnp.float32
    nrm = lambda k, shape, s: jax.random.normal(k, shape, f32) * s
    u = jax.random.uniform(ks[20], (DEPTH, 2, D_LRU), f32, 0.9, 0.999)
    sig = u ** (1.0 / LRU_C)
    lam = jnp.log(sig) - jnp.log1p(-sig)
    return {
        'x_prompt': nrm(ks[0], (BATCH, SEQ, D_MODEL), 1.0),
        'x_sample': nrm(ks[1], (DEC_BATCH, DEC_SEQ, D_MODEL), 1.0),
        'state_rglru': nrm(ks[2], (DEC_BATCH, DEPTH, 2, D_LRU), 0.5),
        'c': nrm(ks[3], (DEC_BATCH, D_MODEL), 1.0),
        'c_ctx': nrm(ks[4], (D_MODEL,), 1.0),
        'w_mod': nrm(ks[5], (DEPTH, D_MODEL, N_MOD * D_MODEL), 0.5 * D_MODEL ** -0.5),
        'b_mod': nrm(ks[6], (DEPTH, N_MOD * D_MODEL), 0.01),
        'g_norm_mix': 1.0 + nrm(ks[7], (DEPTH, D_MODEL), 0.02),
        'g_norm_ffn': 1.0 + nrm(ks[8], (DEPTH, D_MODEL), 0.02),
        'w_in': nrm(ks[9], (DEPTH, D_MODEL, D_IN), D_MODEL ** -0.5),
        'w_pool': nrm(ks[10], (DEPTH, N_POOL_GROUPS, POOL_GROUP_W, POOL_GROUP_W), POOL_GROUP_W ** -0.5),
        'pool_scale': 0.5 + nrm(ks[11], (DEPTH, D_POOL), 0.1),
        'w_conv': nrm(ks[12], (DEPTH, CONV_W, D_LRU), CONV_W ** -0.5),
        'b_conv': nrm(ks[13], (DEPTH, D_LRU), 0.01),
        'w_gate_a': nrm(ks[14], (DEPTH, 2, N_LRU_HEADS, LRU_HEAD_DIM, LRU_HEAD_DIM), LRU_HEAD_DIM ** -0.5),
        'b_gate_a': nrm(ks[15], (DEPTH, 2, N_LRU_HEADS, LRU_HEAD_DIM), 0.01),
        'w_gate_x': nrm(ks[16], (DEPTH, 2, N_LRU_HEADS, LRU_HEAD_DIM, LRU_HEAD_DIM), LRU_HEAD_DIM ** -0.5),
        'b_gate_x': nrm(ks[17], (DEPTH, 2, N_LRU_HEADS, LRU_HEAD_DIM), 0.01),
        'lru_lambda': lam,
        'w_out': nrm(ks[18], (DEPTH, D_MIX, D_MODEL), D_MIX ** -0.5),
        'w_router': nrm(ks[19], (DEPTH, D_MODEL, N_EXPERTS), D_MODEL ** -0.5),
        'w_exp_gate': nrm(ks[21], (DEPTH, N_EXPERTS, D_MODEL, D_EXPERT), D_MODEL ** -0.5),
        'w_exp_up': nrm(ks[22], (DEPTH, N_EXPERTS, D_MODEL, D_EXPERT), D_MODEL ** -0.5),
        'w_exp_down': nrm(ks[23], (DEPTH, N_EXPERTS, D_EXPERT, D_MODEL), D_EXPERT ** -0.5),
        'g_final': 1.0 + nrm(ks[24], (D_MODEL,), 0.02),
    }

def reference(x_prompt, x_sample, state_rglru, c, c_ctx, w_mod, b_mod, g_norm_mix, g_norm_ffn, w_in, w_pool, pool_scale, w_conv, b_conv, w_gate_a, b_gate_a, w_gate_x, b_gate_x, lru_lambda, w_out, w_router, w_exp_gate, w_exp_up, w_exp_down, g_final):
    B = x_prompt.shape[0]
    rows = x_sample.shape[1] // GRID_W
    h0_ctx = jnp.zeros((B, 2, D_LRU), x_prompt.dtype)
    xp = x_prompt
    xs = x_sample
    states = []
    for l in range(DEPTH):
        p = {
            'g_norm_mix': g_norm_mix[l], 'g_norm_ffn': g_norm_ffn[l], 'w_in': w_in[l],
            'w_pool': w_pool[l], 'pool_scale': pool_scale[l], 'w_conv': w_conv[l], 'b_conv': b_conv[l],
            'w_gate_a': w_gate_a[l], 'b_gate_a': b_gate_a[l], 'w_gate_x': w_gate_x[l], 'b_gate_x': b_gate_x[l],
            'lru_lambda': lru_lambda[l], 'w_out': w_out[l], 'w_router': w_router[l],
            'w_exp_gate': w_exp_gate[l], 'w_exp_up': w_exp_up[l], 'w_exp_down': w_exp_down[l],
        }
        mod_ctx = (jnp.einsum('d,dk->k', jax.nn.silu(c_ctx), w_mod[l]) + b_mod[l])[None, None, :]
        mod_lat = (jnp.einsum('bd,dk->bk', jax.nn.silu(c), w_mod[l]) + b_mod[l])[:, None, :]
        xp, st = _layer(xp, mod_ctx, h0_ctx, None, p, True)
        xs, _ = _layer(xs, mod_lat, state_rglru[:, l], rows, p, False)
        states.append(st)
    y_prompt = _rmsnorm(xp, g_final)
    y_sample = _rmsnorm(xs, g_final)
    new_state_rglru = jnp.stack(states, axis=1)
    return (y_prompt, y_sample, new_state_rglru)


_drawn_inputs = setup_inputs


def setup_inputs(seed=0):
    import zlib

    import numpy as np

    out = dict(_drawn_inputs(seed))
    spreads = {}
    factors = {'state_rglru': 2.879,
     'g_norm_mix': 5.114,
     'g_norm_ffn': 8.0,
     'pool_scale': 2.851,
     'b_gate_a': 8.0,
     'b_gate_x': 8.0,
     'g_final': 2.857}
    for name, (base, spread) in spreads.items():
        noise = np.random.default_rng([zlib.crc32(name.encode()), seed]).standard_normal(out[name].shape)
        drawn = base * np.exp(spread * noise) if base else spread * noise
        out[name] = __import__('jax').numpy.asarray(drawn.astype(out[name].dtype))
    for name, factor in factors.items():
        out[name] = (out[name] * factor).astype(out[name].dtype)
    return out
```

```python
from contextlib import ExitStack

import numpy as np
import concourse.bass as bass
from concourse import mybir

D = 1024
P = 128
KC = D // P
N_LAT, N_CTX = 1024, 128
T = N_LAT + N_CTX
NT = T // P
CTX_TILE = NT - 1
SEG = T // 3
GRID_W, GRID_H = 64, N_LAT // 64
PAD = 8
PW = GRID_W + 2 * PAD
PH = GRID_H + 2 * PAD
NG = 4
LC = 4
CONV_W = 4
NE, CAP_L, CAP_C = 16, 128, 16
CAP = CAP_L + CAP_C
EPS = 1e-6
UW = 256
UN = KC * UW
RAW = 6
SPLIT = 4
POOL_KC = 1
UPE = 12

ROWS = {}
_at = 0
for _name, _n in (("b_mod", 48), ("g_mix", 8), ("g_ffn", 8), ("c", 8), ("c_ctx", 8), ("pool_scale", 4),
                  ("w_conv", 16), ("b_conv", 4), ("b_gate_a", 8), ("b_gate_x", 8), ("lam", 8)):
    ROWS[_name] = (_at, _at + _n)
    _at += _n
assert _at == P

SHIFT1, SCALE1, GATE1, SHIFT2, SCALE2, GATE2 = (8 * i for i in range(6))
NMOD1, NMOD2 = 8, 16


def hybrid_step_kernel(nc, x_prompt, x_sample, state_rglru, c, c_ctx, w_mod, b_mod, g_norm_mix, g_norm_ffn,
                       w_in, w_pool, pool_scale, w_conv, b_conv, w_gate_a, b_gate_a, w_gate_x, b_gate_x,
                       lru_lambda, w_out, w_router, w_exp_gate, w_exp_up, w_exp_down, g_final,
                       identity, inv_count, y_prompt, y_sample, new_state):
    f32, f32r, u32 = mybir.dt.float32, mybir.dt.float32r, mybir.dt.uint32
    ACT = mybir.ActivationFunctionType
    ALU = mybir.AluOpType
    AX = mybir.AxisListType

    order = ([("x", k) for k in range(KC)]
             + [("L", 0), ("L", 1), ("M", 0, 3), ("G", 0, 0, 0), ("G", 0, 0, 1), ("P", 3),
                ("G", 0, 1, 0), ("G", 0, 1, 1), ("P", 2), ("M", 3, 6), ("G", 1, 0, 0), ("G", 1, 0, 1), ("L", 2),
                ("G", 1, 1, 0), ("G", 1, 1, 1), ("L", 3), ("M", 6, 9), ("G", 2, 0, 0), ("G", 2, 0, 1), ("P", 1),
                ("G", 2, 1, 0), ("G", 2, 1, 1), ("P", 0), ("M", 9, 12), ("G", 3, 0, 0), ("G", 3, 0, 1), ("E", 0),
                ("G", 3, 1, 0), ("G", 3, 1, 1), ("E", 1), ("M", 12, 14), ("E", 2), ("E", 3), ("M", 14, 16)]
             + [("O", g) for g in (3, 2, 1, 0)])
    JOB = {j: n for n, j in enumerate(j for j in order if j[0] != "M")}
    NJOBS = len(JOB)
    POOL_ORDER = (3, 2, 1, 0)

    IN_CHUNK = {"P": 0, "L": 4, "E": 8}
    units = [("mod", u) for u in range(NMOD1)]
    for j in order:
        if j[0] == "M":
            units += [("mod", NMOD1 + u) for u in range(j[1], j[2])]
        elif j[0] in IN_CHUNK:
            u = ("in", (IN_CHUNK[j[0]] + j[1]) // 2)
            if u not in units:
                units.append(u)
    units += [("out", u) for u in range(D // UW)]
    UNIT = {u: n for n, u in enumerate(units)}
    OUT0 = UNIT[("out", 0)]
    MOE0 = len(units)

    def slot(n):
        return n % RAW

    def loads(n):
        return 16 * (n // RAW + 1)

    h_rows = nc.dram_tensor("h_rows", [T, D], f32).ap()
    y_rows = nc.dram_tensor("y_rows", [T, D], f32).ap()

    ctx = ExitStack()
    phase1, phase2, moe, last = ExitStack(), ExitStack(), ExitStack(), ExitStack()

    def sb(name, shape, dt=f32, stack=ctx):
        return stack.enter_context(nc.sbuf_tensor(name, shape, dt))

    def sem(name):
        return ctx.enter_context(nc.semaphore(name))

    with ctx:
        ps = ctx.enter_context(nc.psum_tensor("ps", [P, 8, 512], f32))

        raw = sb("raw", [P, RAW, KC, UW])
        ident = sb("ident", [P, P])
        ones = sb("ones", [P, P])
        vecs = sb("vecs", [P, P])
        states = sb("states", [P, 8])
        silu_c = sb("silu_c", [P, KC, 2])
        mod = sb("mod", [P, 48, 2])
        scale_a = sb("scale_a", [P, KC, 2])
        half = sb("half", [P, 1])
        lam_t = sb("lam_t", [P, 6, 8])
        rate = sb("rate", [P, 2, 8])
        st_out, st_rows = sb("st_out", [P, 8]), sb("st_rows", [8, P])
        sumsq = sb("sumsq", [P, 3, NT])
        rstd = sb("rstd", [P, 3, NT])
        w_r = sb("w_r", [P, KC, NE])
        logit_max = sb("logit_max", [P, NT])
        prob_sum = sb("prob_sum", [P, NT])
        prob_inv = sb("prob_inv", [P, NT])
        probs = sb("probs", [P, NT, NE])
        top_l, top_li, top_lf = sb("top_l", [NE, CAP_L]), sb("top_li", [NE, CAP_L], u32), sb("top_lf", [NE, CAP_L])
        top_c, top_ci, top_cf = sb("top_c", [NE, CAP_C]), sb("top_ci", [NE, CAP_C], u32), sb("top_cf", [NE, CAP_C])
        g_lat, i_lat = sb("g_lat", [CAP_L, NE]), sb("i_lat", [CAP_L, NE], u32)
        g_ctx, i_ctx = sb("g_ctx", [CAP_C, NE]), sb("i_ctx", [CAP_C, NE], u32)
        gi_lat, gi_ctx = sb("gi_lat", [CAP_L, 1], u32), sb("gi_ctx", [CAP_C, 1], u32)
        si_lat, si_ctx = sb("si_lat", [CAP_L, 1], u32), sb("si_ctx", [CAP_C, 1], u32)
        sg_lat, sg_ctx = sb("sg_lat", [CAP_L, 1]), sb("sg_ctx", [CAP_C, 1])

        y_t = sb("y_t", [P, KC, T], stack=phase1)
        h_t = sb("h_t", [P, KC, T], stack=phase1)
        h_flat = h_t[:, :, :].rearrange("p k t -> p (k t)")
        bc = h_flat[:, 0:6 * D].rearrange("p (v s d) -> p v s d", v=3, s=2)
        g2 = h_flat[:, 7 * D:9 * D].rearrange("p (s d) -> p s d", s=2)
        x_in_stack = ExitStack()
        x_in = sb("x_in", [P, NT, D], stack=x_in_stack)
        junk0 = sb("junk0", [P, D], stack=x_in_stack)
        rows_in = sb("rows_in", [P, P], stack=x_in_stack)
        rows_st = sb("rows_st", [8, P], stack=x_in_stack)
        x_in_stack.close()
        lru = ExitStack()
        up = sb("up", [P, T + 6], stack=lru)
        UL, UC = 2, N_LAT + 5
        xc = sb("xc", [P, 2, T], stack=lru)
        r_a = sb("r_a", [P, T], stack=lru)
        i_b = sb("i_b", [P, T], stack=lru)
        tau = sb("tau", [P, T], stack=lru)
        pad_l = sb("pad_l", [P, 2, GRID_H, PW], stack=lru)
        pad_c = sb("pad_c", [P, 2, N_CTX + 2 * PAD], stack=lru)
        box = [sb(f"box{i}", [P, PH * GRID_W], stack=lru) for i in range(2)]
        box_c = [sb(f"box_c{i}", [P, N_CTX + 2 * PAD], stack=lru) for i in range(2)]
        tall = sb("tall", [P, PH, GRID_W], stack=lru)
        NI = GRID_W + GRID_H + N_CTX
        inv = sb("inv", [P, NG, NI], stack=lru)
        w_gates = sb("w_gates", [P, 2, 2, LC, P], stack=lru)
        w_p = sb("w_p", [P, NG, P], stack=lru)
        gelu = up
        lru.close()
        x_res = sb("x_res", [P, 2, D], stack=phase2)
        x1 = sb("x1", [P, 2, D], stack=phase2)
        hn2 = sb("hn2", [P, 2, D], stack=phase2)
        hn2_t = sb("hn2_t", [P, 2, KC, P], stack=phase2)
        junk1 = sb("junk1", [P, D], stack=phase2)
        aff_l = sb("aff_l", [NE, N_LAT], stack=phase2)
        aff_c = sb("aff_c", [NE, N_CTX], stack=phase2)
        aff_w = [sb(f"aff_w{i}", [NE, N_LAT], stack=phase2) for i in range(2)]
        phase2.close()
        phase1.close()

        split = sb("split", [P, SPLIT, 2, KC, UW], f32r, stack=moe)
        sb("g2_kept", [P, 2 * D], stack=moe)
        x_l = sb("x_l", [CAP_L, D], stack=moe)
        x_c = sb("x_c", [CAP_C, D], stack=moe)
        xt = sb("xt", [P, 2, KC, CAP], f32r, stack=moe)
        gate_s = sb("gate_s", [P, 2, 2 * CAP], stack=moe)
        hid_f = sb("hid_f", [P, 2, 2 * CAP], stack=moe)
        hid = sb("hid", [P, 2, KC, CAP], f32r, stack=moe)
        down = sb("down", [P, KC, CAP], stack=moe)
        o_l = sb("o_l", [CAP_L, D], stack=moe)
        o_c = sb("o_c", [CAP_C, D], stack=moe)
        moe.close()
        y_end = sb("y_end", [P, NT, D], stack=last)
        junk2 = sb("junk2", [P, D], stack=last)
        g_fin = sb("g_fin", [P, D], stack=last)
        last.close()

        loaded = [sem(f"unit_loaded_{i}") for i in range(RAW)]
        rows_loaded, ident_loaded = sem("rows_loaded"), sem("ident_loaded")
        x_loaded = [sem(f"x_loaded_{t}") for t in range(NT)]
        small_loaded = sem("small_loaded")
        res_loaded = [sem(f"res_loaded_{i}") for i in range(2)]
        ones_ready = sem("ones_ready")
        vecs_turned, vecs_ready, silu_ready = sem("vecs_turned"), sem("vecs_ready"), sem("silu_ready")
        mods_done, mod1_ready, mod2_ready = sem("mods_done"), sem("mod1_ready"), sem("mod2_ready")
        half_ready, sq_ready, rstd_ready, xn_ready = sem("half_ready"), sem("sq_ready"), sem("rstd_ready"), sem("xn_ready")
        job_done, job_read = sem("job_done"), sem("job_read")
        lam_act, lam_dve, rate_ready = sem("lam_act"), sem("lam_dve"), sem("rate_ready")
        pads_ready, up_ready, conv_done = sem("pads_ready"), sem("up_ready"), sem("conv_done")
        decay_ready, scan_done, gelu_used = sem("decay_ready"), sem("scan_done"), sem("gelu_used")
        box_ready, pooled = sem("box_ready"), sem("pooled")
        diag_ready, rows_spread, rows_kept = sem("diag_ready"), sem("rows_spread"), sem("rows_kept")
        state_turned, state_kept, state_stored = sem("state_turned"), sem("state_kept"), sem("state_stored")
        act_step, dve_step, pool_step = sem("act_step"), sem("dve_step"), sem("pool_step")
        mix_done, mix_read, x1_ready = sem("mix_done"), sem("mix_read"), sem("x1_ready")
        sq2_ready, rstd2_ready, xn2_ready, hn2_ready = sem("sq2_ready"), sem("rstd2_ready"), sem("xn2_ready"), sem("hn2_ready")
        h_stored = [sem(f"h_stored_{i}") for i in range(2)]
        y_stored = [sem(f"y_stored_{i}") for i in range(2)]
        hn2_turned, hn2_t_ready, logits_done = sem("hn2_turned"), sem("hn2_t_ready"), sem("logits_done")
        max_ready, exp_ready, probs_ready = sem("max_ready"), sem("exp_ready"), sem("probs_ready")
        probs_turned, aff_ready = sem("probs_turned"), sem("aff_ready")
        top_ready, top_turned, routed = sem("top_ready"), sem("top_turned"), sem("routed")
        gi_ready, gathered, x_turned, xt_hi, xt_lo = (sem("gather_index_ready"), sem("gathered"), sem("x_turned"),
                                                      sem("xt_hi"), sem("xt_lo"))
        hi_done, lo_dve, lo_pool, unit_done = sem("hi_done"), sem("lo_dve"), sem("lo_pool"), sem("unit_done")
        silu_done, mul_done, hid_hi, hid_lo = sem("silu_done"), sem("mul_done"), sem("hid_hi"), sem("hid_lo")
        down_read, rows_turned, out_scaled, scattered = (sem("down_read"), sem("rows_turned"), sem("out_scaled"),
                                                         sem("scattered"))
        si_ready = sem("scatter_index_ready")
        y_loaded = [sem(f"y_loaded_{t}") for t in range(NT)]
        g_fin_loaded = sem("g_fin_loaded")
        sq3_ready, rstd3_ready, end_ready, stored = sem("sq3_ready"), sem("rstd3_ready"), sem("end_ready"), sem("stored")

        SMALL = 16 * 11
        LAG = 3

        def vec(name):
            a, b = ROWS[name]
            return vecs[:, a:b]

        def stream(t):
            return 1 if t == CTX_TILE else 0

        def unit_source(kind, u):
            w = {"mod": w_mod, "in": w_in, "out": w_out}[kind]
            return w[0, :, u * UW:(u + 1) * UW].rearrange("(k p) n -> p k n", p=P)

        def x_tile(t):
            return x_prompt[0, :, :] if t == CTX_TILE else x_sample[0, t * P:(t + 1) * P, :]

        def out_tile(t):
            return y_prompt[0, :, :] if t == CTX_TILE else y_sample[0, t * P:(t + 1) * P, :]

        TILES = [CTX_TILE] + list(range(NT - 1))

        block = ctx.enter_context(nc.Block())

        @block.sync
        def _(sp):
            def wait_used(n):
                kind, u = units[n]
                if kind == "mod":
                    sp.wait_ge(mods_done, u + 1)
                elif kind == "in":
                    sp.wait_ge(job_done, 1 + max(JOB[(x, k)] for x, a in IN_CHUNK.items() for k in range(4)
                                                 if (a + k) // 2 == u))
                else:
                    sp.wait_ge(mix_done, NT)

            def load_unit(n):
                kind, u = units[n]
                if n >= RAW:
                    wait_used(n - RAW)
                sp.dma_start(raw[:, slot(n), :, :], unit_source(kind, u)).then_inc(loaded[slot(n)], 16)

            for n in range(MOE0):
                load_unit(n)

            def load_residual(s):
                if s >= 2:
                    sp.wait_ge(x1_ready, s - 1)
                else:
                    sp.wait_ge(scan_done, 2 * LC)
                    sp.wait_ge(job_read, NJOBS)
                    sp.wait_ge(gelu_used, LC)
                    sp.wait_ge(pooled, NG)
                sp.dma_start(x_res[:, s % 2, :], x_tile(TILES[s])).then_inc(res_loaded[s % 2], 16)

            EXPERTS = {"g": w_exp_gate, "u": w_exp_up, "d": w_exp_down}

            def load_expert(e, j):
                kind, k = ("gu"[j % 2], j // 2) if j < 8 else ("d", j - 8)
                first = not isinstance(e, int)
                w = EXPERTS[kind]
                src = w[0, bass.ds(e, 1), :, k * UW:(k + 1) * UW] if first else w[0, e:e + 1, :, k * UW:(k + 1) * UW]
                sp.dma_start(raw[:, slot(MOE0 + j), :, :], src.rearrange("o (k p) n -> p (o k) n", p=P))\
                  .then_inc(loaded[slot(MOE0 + j)], 16)

            free = [j for j in range(RAW) if MOE0 + j - RAW < OUT0]
            load_residual(0)
            load_residual(1)
            for j in free:
                wait_used(MOE0 + j - RAW)
                load_expert(0, j)
            for s in range(2, NT):
                load_residual(s)
            for j in range(len(free), UPE):
                if j < RAW:
                    wait_used(MOE0 + j - RAW)
                else:
                    sp.wait_ge(lo_dve, j - RAW + 1)
                    sp.wait_ge(lo_pool, j - RAW + 1)
                load_expert(0, j)
            with sp.Fori(1, NE) as e:
                for j in range(UPE):
                    sp.wait_ge(lo_dve, e * UPE + (j - RAW + 1))
                    sp.wait_ge(lo_pool, e * UPE + (j - RAW + 1))
                    load_expert(e, j)

            sp.wait_ge(scattered, 32 * NE)
            sp.wait_ge(unit_done, UPE * NE)
            sp.dma_start(g_fin[:, :], g_final.partition_broadcast(P)).then_inc(g_fin_loaded, 16)
            for t in range(NT):
                sp.dma_start(y_end[:, t, :], y_rows[t * P:(t + 1) * P, :]).then_inc(y_loaded[t], 16)
            for t in range(NT):
                sp.wait_ge(end_ready, t + 1)
                sp.dma_start(out_tile(t), y_end[:, t, :]).then_inc(stored, 16)
            sp.wait_ge(stored, 16 * NT)
            sp.wait_ge(state_stored, 16)

        @block.scalar
        def _(act):
            steps = [0]

            def link(ins):
                ins.then_inc(act_step, 1)
                steps[0] += 1
                act.wait_ge(act_step, steps[0])

            sources = {"b_mod": b_mod[0], "g_mix": g_norm_mix[0], "g_ffn": g_norm_ffn[0], "c": c[0], "c_ctx": c_ctx,
                       "pool_scale": pool_scale[0], "w_conv": w_conv[0].rearrange("k n -> (k n)"), "b_conv": b_conv[0],
                       "b_gate_a": b_gate_a[0].rearrange("r h i -> (r h i)"),
                       "b_gate_x": b_gate_x[0].rearrange("r h i -> (r h i)"),
                       "lam": lru_lambda[0].rearrange("r n -> (r n)")}
            act.dma_start(ident[:, :], identity).then_inc(ident_loaded, 16)
            for name, (a, b) in ROWS.items():
                act.dma_start(rows_in[a:b, :], sources[name].rearrange("(r n) -> r n", n=P)).then_inc(rows_loaded, 16)
            act.dma_start(rows_st[:, :], state_rglru[0, 0].rearrange("r (k n) -> (r k) n", n=P)).then_inc(rows_loaded, 16)
            for t in range(NT):
                act.dma_start(x_in[:, t, :], x_tile(t)).then_inc(x_loaded[t], 16)

            act.wait_ge(vecs_ready, 2)
            a = ROWS["c"][0]
            act.activation(silu_c[:, :, :], vecs[:, a:a + 16].rearrange("p (s k) -> p k s", s=2), ACT.Silu)\
               .then_inc(silu_ready, 1)
            for t in range(NT):
                act.wait_ge(x_loaded[t], 16)
                act.activation(junk0[:, :], x_in[:, t, :], ACT.Square, accum_out=sumsq[:, 0, t:t + 1]).then_inc(sq_ready, 1)
                act.wait_ge(sq_ready, t + 1)
            link(act.activation(lam_t[:, 0, :], vec("lam"), ACT.Abs))
            act.activation(lam_t[:, 1, :], lam_t[:, 0, :], ACT.Exp, scale=-1.0).then_inc(lam_act, 1)
            act.wait_ge(lam_dve, 1)
            act.activation(lam_t[:, 3, :], lam_t[:, 2, :], ACT.Ln).then_inc(lam_act, 1)

            def bank_parts(j, dst):
                for n in range(3):
                    yield ps[:, 3 * (j % 2) + n, 0:SEG], dst[:, n * SEG:(n + 1) * SEG]

            for job in order:
                if job[0] == "M":
                    continue
                j = JOB[job]
                kind, k = job[0], job[1]
                if kind == "x":
                    if k == 0:
                        act.wait_ge(mod1_ready, 1)
                    act.wait_ge(job_done, j + 1)
                    for n, (a, b, s) in enumerate(((0, 512, 0), (512, N_LAT, 0), (N_LAT, T, 1))):
                        last_i = act.activation(h_t[:, k, a:b], ps[:, 3 * (j % 2) + n, 0:b - a], ACT.Identity,
                                                scale=scale_a[:, k, s:s + 1], bias=mod[:, SHIFT1 + k, s:s + 1])
                    last_i.then_inc(job_read, 1)
                elif kind == "L":
                    if k == 0:
                        act.wait_ge(up_ready, 1)
                    else:
                        act.wait_ge(conv_done, k)
                    act.wait_ge(job_done, j + 1)
                    b = 3 * (j % 2)
                    act.activation(up[:, UL:UL + SEG], ps[:, b, 0:SEG], ACT.Copy)
                    act.activation(up[:, UL + SEG:UL + 2 * SEG], ps[:, b + 1, 0:SEG], ACT.Copy)
                    act.activation(up[:, UL + 2 * SEG:UL + N_LAT], ps[:, b + 2, 0:N_LAT - 2 * SEG], ACT.Copy)
                    act.activation(up[:, UC:UC + N_CTX], ps[:, b + 2, N_LAT - 2 * SEG:SEG], ACT.Copy).then_inc(job_read, 1)
                elif kind == "P":
                    q = POOL_ORDER.index(k)
                    act.wait_ge(pads_ready, 1)
                    if q >= 2:
                        act.wait_ge(pooled, q - 1)
                    act.wait_ge(job_done, j + 1)
                    for n in range(3):
                        rows = (SEG if n < 2 else N_LAT - 2 * SEG) // GRID_W
                        at = n * SEG // GRID_W
                        act.activation(pad_l[:, q % 2, at:at + rows, PAD:PAD + GRID_W],
                                       ps[:, 3 * (j % 2) + n, 0:rows * GRID_W].rearrange("p (r w) -> p r w", w=GRID_W),
                                       ACT.Copy)
                    act.activation(pad_c[:, q % 2, PAD:PAD + N_CTX], ps[:, 3 * (j % 2) + 2, N_LAT - 2 * SEG:SEG],
                                   ACT.Copy).then_inc(job_read, 1)
                elif kind == "E":
                    if k > 0:
                        act.wait_ge(gelu_used, k)
                    else:
                        act.wait_ge(conv_done, LC)
                    act.wait_ge(job_done, j + 1)
                    for src, dst in bank_parts(j, gelu):
                        last_i = act.activation(dst, src, ACT.Gelu_apprx_tanh)
                    last_i.then_inc(job_read, 1)
                elif kind == "G":
                    _, k, r, ax = job
                    d = 2 * k + r
                    m = r * LC + k
                    if ax == 0:
                        if d > 0:
                            act.wait_ge(scan_done, d)
                        act.wait_ge(job_done, j + 1)
                        for src, dst in bank_parts(j, r_a):
                            last_i = act.activation(dst, src, ACT.Sigmoid, bias=vec("b_gate_a")[:, m:m + 1])
                        last_i.then_inc(job_read, 1)
                    else:
                        act.wait_ge(job_done, j + 1)
                        for src, dst in bank_parts(j, i_b):
                            last_i = act.activation(dst, src, ACT.Sigmoid, bias=vec("b_gate_x")[:, m:m + 1])
                        last_i.then_inc(job_read, 1)
                        act.wait_ge(rate_ready, 1)
                        act.wait_ge(job_read, JOB[("G", k, r, 0)] + 1)
                        link(act.activation(tau[:, :], r_a[:, :], ACT.Tanh, scale=rate[:, 0, m:m + 1]))
                        act.activation(r_a[:, :], r_a[:, :], ACT.Exp, scale=rate[:, 1, m:m + 1])
                        act.activation(tau[:, :], tau[:, :], ACT.Sqrt).then_inc(decay_ready, 1)
                elif kind == "O":
                    act.wait_ge(job_done, j + 1)
                    for src, dst in bank_parts(j, y_t[:, k, :]):
                        last_i = act.activation(dst, src, ACT.Copy, scale=vec("pool_scale")[:, k:k + 1])
                    last_i.then_inc(job_read, 1)

            for q in range(16):
                v, s, h = q // 4, q // 2 % 2, q % 2
                dst = bc[:, v, s, :] if v < 3 else g2[:, s, :]
                act.wait_ge(rows_spread, q + 1)
                act.activation(dst[:, 512 * h:512 * h + 512], ps[:, 6 + q % 2, :], ACT.Copy).then_inc(rows_kept, 1)

            for s in range(NT + 4):
                if s < NT:
                    act.wait_ge(x1_ready, s + 1)
                    act.activation(junk1[:, :], x1[:, s % 2, :], ACT.Square, accum_out=sumsq[:, 1, s:s + 1])\
                       .then_inc(sq2_ready, 1)
                    act.wait_ge(rstd2_ready, s + 1)
                    if s >= 2:
                        act.wait_ge(h_stored[s % 2], 16 * (s // 2))
                        act.wait_ge(hn2_turned, s - 1)
                    act.activation(hn2[:, s % 2, :], x1[:, s % 2, :], ACT.Copy, scale=rstd[:, 1, s:s + 1])\
                       .then_inc(xn2_ready, 1)
                if 0 <= s - 1 < NT:
                    t = s - 1
                    act.wait_ge(hn2_turned, t + 1)
                    if t >= 2:
                        act.wait_ge(logits_done, t - 1)
                    for h in range(2):
                        last_i = act.activation(hn2_t[:, t % 2, 4 * h:4 * h + 4, :],
                                                ps[:, 4 + h, :].rearrange("p (k n) -> p k n", k=4), ACT.Copy)
                    last_i.then_inc(hn2_t_ready, 1)
                if 0 <= s - 2 < NT:
                    t = s - 2
                    act.wait_ge(max_ready, t + 1)
                    act.activation(probs[:, t, :], ps[:, 6, 0:NE], ACT.Exp, bias=logit_max[:, t:t + 1],
                                   accum_out=prob_sum[:, t:t + 1]).then_inc(exp_ready, 1)

            def split_high(e, j):
                m = e * UPE + j
                load_base = e * (16 * UPE // RAW)
                act.wait_ge(loaded[slot(MOE0 + j)], load_base + loads(MOE0 + j))
                if not (isinstance(e, int) and e == 0 and j < SPLIT):
                    act.wait_ge(unit_done, m + (1 - SPLIT))
                act.activation(split[:, j % SPLIT, 0, :, :], raw[:, slot(MOE0 + j), :, :], ACT.Copy).then_inc(hi_done, 1)

            def hidden_high(e, k):
                act.wait_ge(mul_done, e * 4 + (k + 1))
                if not (isinstance(e, int) and e == 0):
                    act.wait_ge(unit_done, e * UPE)
                act.activation(hid[:, 0, 2 * k:2 * k + 2, :], hid_f[:, k % 2, :].rearrange("p (c n) -> p c n", c=2),
                               ACT.Copy).then_inc(hid_hi, 1)

            def evict(e, j):
                if j < 8 and j % 2 == 0:
                    k = j // 2
                    act.wait_ge(unit_done, e * UPE + (j + 1))
                    if not (isinstance(e, int) and e == 0 and k < 2):
                        act.wait_ge(mul_done, e * 4 + (k - 1))
                    act.activation(gate_s[:, k % 2, :], ps[:, k % 2, 0:2 * CAP], ACT.Silu).then_inc(silu_done, 1)
                    if k > 0:
                        hidden_high(e, k - 1)
                elif j == 7:
                    hidden_high(e, 3)
                elif j >= 8:
                    k = j - 8
                    act.wait_ge(unit_done, e * UPE + (j + 1))
                    act.activation(down[:, 2 * k:2 * k + 2, :], ps[:, 4 + k % 2, 0:2 * CAP]
                                   .rearrange("p (c n) -> p c n", c=2), ACT.Copy).then_inc(down_read, 1)

            def input_high(e):
                act.wait_ge(x_turned, e + 1)
                for h in range(2):
                    act.activation(xt[:, 0, 4 * h:4 * h + 4, 0:CAP_L], ps[:, 6 + h, :].rearrange("p (k n) -> p k n", k=4),
                                   ACT.Copy)
                act.activation(xt[:, 0, :, CAP_L:CAP], ps[:, 0, 0:KC * CAP_C].rearrange("p (k n) -> p k n", k=KC),
                               ACT.Copy).then_inc(xt_hi, 1)

            def expert(e, is_first, is_last):
                for j in range(UPE):
                    if not (is_first and j < LAG):
                        split_high(e, j)
                    if j >= LAG:
                        evict(e, j - LAG)
                    elif not is_first:
                        evict(e - 1, j - LAG + UPE)
                    if j == 7 + LAG and not is_last:
                        input_high(e + 1)

            act.wait_ge(hn2_ready, NT)
            act.wait_ge(mix_done, NT)
            for j in range(LAG):
                split_high(0, j)
            input_high(0)
            expert(0, True, False)
            with act.Fori(1, NE - 1) as e:
                expert(e, False, False)
            expert(NE - 1, False, True)
            for j in range(UPE - LAG, UPE):
                evict(NE - 1, j)

            for t in range(NT):
                act.wait_ge(y_loaded[t], 16)
                act.activation(junk2[:, :], y_end[:, t, :], ACT.Square, accum_out=sumsq[:, 2, t:t + 1]).then_inc(sq3_ready, 1)
                act.wait_ge(sq3_ready, t + 1)

        @block.gpsimd
        def _(pool):
            steps = [0]

            def link(ins):
                ins.then_inc(pool_step, 1)
                steps[0] += 1
                pool.wait_ge(pool_step, steps[0])

            pool.memset(half[:, :], -0.5).then_inc(half_ready, 1)
            pool.wait_ge(half_ready, 1)

            def root(norm, t, ready, done):
                pool.wait_ge(ready, t + 1)
                link(pool.tensor_scalar(rstd[:, norm, t:t + 1], sumsq[:, norm, t:t + 1], 1.0 / D, EPS, ALU.mult, ALU.add))
                pool.tensor_tensor(rstd[:, norm, t:t + 1], rstd[:, norm, t:t + 1], half[:, :], ALU.pow).then_inc(done, 1)

            for t in range(NT):
                root(0, t, sq_ready, rstd_ready)

            pool.wait_ge(job_done, KC)
            pool.memset(w_gates[:, :, :, :, :], 0.0).then_inc(pool_step, 1)
            pool.memset(pad_l[:, :, :, :], 0.0).then_inc(pool_step, 1)
            pool.memset(pad_c[:, :, :], 0.0).then_inc(pool_step, 1)
            pool.memset(tall[:, :, :], 0.0).then_inc(pool_step, 1)
            steps[0] += 4
            pool.wait_ge(pool_step, steps[0])
            for ax, w in enumerate((w_gate_a, w_gate_x)):
                for h in range(2):
                    src = w[0].rearrange("r (k h) i j -> h i r k j", h=2)[h]
                    for r in range(2):
                        pool.dma_start(w_gates[64 * h:64 * h + 64, ax, r, :, 64 * h:64 * h + 64], src[:, r, :, :])\
                            .then_inc(small_loaded, 16)
            pool.dma_start(w_p[:, :, :], w_pool[0].rearrange("g c d -> c g d")).then_inc(small_loaded, 16)
            pool.dma_start(inv[:, :, :], inv_count.partition_broadcast(P)).then_inc(small_loaded, 16)
            pool.dma_start(w_r[:, :, :], w_router[0].rearrange("(k p) e -> p k e", p=P)).then_inc(small_loaded, 16)
            pool.nop().then_inc(pads_ready, 1)

            def doubling(g, first, middle, final, take, size):
                spans, a, b = [], 0, size
                for s in range(g, -1, -1):
                    spans.insert(0, (a, b))
                    h = max(1, 2 ** (s - 1))
                    a, b = a - h, b + h
                src = first
                for s, (a, b) in enumerate(spans):
                    left, right = (1, 0) if s == 0 else (2 ** (s - 1), 2 ** (s - 1))
                    dst = final if s == g else take(middle[s % 2], a, b)
                    link(pool.tensor_tensor(dst, take(src, a - left, b - left), take(src, a + right, b + right), ALU.add))
                    src = middle[s % 2]

            def along_row(buf, a, b):
                return buf[:, :, PAD + a:PAD + b]

            def along_column(buf, a, b):
                return buf[:, PAD + a:PAD + b, :]

            def along_line(buf, a, b):
                return buf[:, PAD + a:PAD + b]

            wide = [b[:, 0:GRID_H * PW].rearrange("p (r w) -> p r w", w=PW) for b in box]
            high = [b[:, :].rearrange("p (r w) -> p r w", w=GRID_W) for b in box]
            for q, g in enumerate(POOL_ORDER):
                if q > 0:
                    pool.wait_ge(pooled, q)
                pool.wait_ge(job_read, JOB[("P", g)] + 1)
                doubling(g, pad_c[:, q % 2, :], box_c, along_line(box_c[g % 2], 0, N_CTX), along_line, N_CTX)
                doubling(g, pad_l[:, q % 2, :, :], wide, tall[:, PAD:PAD + GRID_H, :], along_row, GRID_W)
                doubling(g, tall, high, along_column(high[g % 2], 0, GRID_H), along_column, GRID_H)
                pool.nop().then_inc(box_ready, 1)

            pool.wait_ge(state_kept, 1)
            pool.dma_start(new_state[0, 0].rearrange("r (k n) -> (r k) n", n=P), st_rows[:, :])\
                .then_inc(state_stored, 16)

            for s in range(NT):
                t = TILES[s]
                pool.wait_ge(x1_ready, s + 1)
                pool.dma_start(y_rows[t * P:(t + 1) * P, :], x1[:, s % 2, :]).then_inc(y_stored[s % 2], 16)
                root(1, s, sq2_ready, rstd2_ready)
                pool.wait_ge(hn2_ready, s + 1)
                pool.dma_start(h_rows[t * P:(t + 1) * P, :], hn2[:, s % 2, :]).then_inc(h_stored[s % 2], 16)
            pool.wait_ge(h_stored[0], 16 * ((NT + 1) // 2))
            pool.wait_ge(h_stored[1], 16 * (NT // 2))
            pool.wait_ge(y_stored[0], 16 * ((NT + 1) // 2))
            pool.wait_ge(y_stored[1], 16 * (NT // 2))
            pool.wait_ge(routed, 4)

            def split_low(e, j):
                pool.wait_ge(hi_done, e * UPE + (j + 1))
                a = KC - POOL_KC
                pool.tensor_tensor(split[:, j % SPLIT, 1, a:KC, :], raw[:, slot(MOE0 + j), a:KC, :],
                                   split[:, j % SPLIT, 0, a:KC, :].bitcast(f32), ALU.subtract).then_inc(lo_pool, 1)

            def gather_waits(e):
                if not (isinstance(e, int) and e == 0):
                    pool.wait_ge(x_turned, e)
                pool.wait_ge(gi_ready, e + 1)

            def gather():
                pool.indirect_dma_start(x_l[:, :], None, h_rows, bass.IndirectOffsetOnAxis(ap=gi_lat[:, :], axis=0))\
                    .then_inc(gathered, 16)
                pool.indirect_dma_start(x_c[:, :], None, h_rows, bass.IndirectOffsetOnAxis(ap=gi_ctx[:, :], axis=0))\
                    .then_inc(gathered, 16)

            def scatter_waits(e):
                pool.wait_ge(out_scaled, e + 1)

            def scatter():
                pool.indirect_dma_start(y_rows, bass.IndirectOffsetOnAxis(ap=si_lat[:, :], axis=0), o_l[:, :], None,
                                        compute_op=ALU.add).then_inc(scattered, 16)
                pool.indirect_dma_start(y_rows, bass.IndirectOffsetOnAxis(ap=si_ctx[:, :], axis=0), o_c[:, :], None,
                                        compute_op=ALU.add).then_inc(scattered, 16)

            def expert(e, is_first, is_last):
                for j in range(UPE):
                    if j == GATHER_AT and not is_last:
                        gather_waits(e + 1)
                    if j == SCATTER_AT and not is_first:
                        scatter_waits(e - 1)
                    if j == UPE - 1 and not is_first:
                        pool.wait_ge(scattered, e * 32)
                    if not (is_first and j < LAG):
                        split_low(e, j)
                    if j == GATHER_AT and not is_last:
                        gather()
                    if j == SCATTER_AT and not is_first:
                        scatter()

            GATHER_AT, SCATTER_AT = LAG, 6
            gather_waits(0)
            gather()
            for j in range(LAG):
                split_low(0, j)
            expert(0, True, False)
            with pool.Fori(1, NE - 1) as e:
                expert(e, False, False)
            expert(NE - 1, False, True)
            scatter_waits(NE - 1)
            scatter()
            for t in range(NT):
                root(2, t, sq3_ready, rstd3_ready)

        @block.vector
        def _(dve):
            steps = [0]

            def link(ins):
                ins.then_inc(dve_step, 1)
                steps[0] += 1
                dve.wait_ge(dve_step, steps[0])

            dve.memset(ones[:, :], 1.0).then_inc(ones_ready, 1)
            dve.wait_ge(vecs_turned, 2)
            dve.tensor_copy(vecs[:, :], ps[:, 7, 0:P]).then_inc(vecs_ready, 1)
            dve.tensor_copy(states[:, :], ps[:, 7, P:P + 8]).then_inc(vecs_ready, 1)
            dve.wait_ge(vecs_ready, 2)
            for t in range(NT):
                dve.wait_ge(rstd_ready, t + 1)
                dve.tensor_scalar(x_in[:, t, :], x_in[:, t, :], rstd[:, 0, t:t + 1], None, ALU.mult).then_inc(xn_ready, 1)

            dve.wait_ge(lam_act, 1)
            dve.tensor_scalar(lam_t[:, 2, :], lam_t[:, 1, :], 1.0, None, ALU.add).then_inc(lam_dve, 1)
            dve.wait_ge(lam_dve, 1)
            link(dve.tensor_scalar(lam_t[:, 4, :], lam_t[:, 2, :], -1.0, None, ALU.add))
            link(dve.tensor_scalar(lam_t[:, 5, :], lam_t[:, 4, :], 0.0, None, ALU.is_equal))
            link(dve.tensor_tensor(lam_t[:, 4, :], lam_t[:, 4, :], lam_t[:, 5, :], ALU.add))
            link(dve.reciprocal(lam_t[:, 4, :], lam_t[:, 4, :]))
            dve.wait_ge(lam_act, 2)
            link(dve.tensor_tensor(lam_t[:, 3, :], lam_t[:, 3, :], lam_t[:, 5, :], ALU.add))
            link(dve.tensor_tensor(lam_t[:, 3, :], lam_t[:, 3, :], lam_t[:, 4, :], ALU.mult))
            link(dve.tensor_tensor(lam_t[:, 3, :], lam_t[:, 3, :], lam_t[:, 1, :], ALU.mult))
            link(dve.tensor_scalar(lam_t[:, 0, :], vec("lam"), -1.0, 0.0, ALU.mult, ALU.max))
            link(dve.tensor_tensor(lam_t[:, 0, :], lam_t[:, 0, :], lam_t[:, 3, :], ALU.add))
            link(dve.tensor_scalar(rate[:, 0, :], lam_t[:, 0, :], 4.0, None, ALU.mult))
            dve.tensor_scalar(rate[:, 1, :], lam_t[:, 0, :], -8.0, None, ALU.mult).then_inc(rate_ready, 1)

            def add_bias(a, b):
                v = vecs[:, a:b].unsqueeze(2).broadcast_to([P, b - a, 2])
                link(dve.tensor_tensor(mod[:, a:b, :], ps[:, 6, 2 * a:2 * b].rearrange("p (k s) -> p k s", s=2), v, ALU.add))

            def one_plus_scale(a, g):
                return dve.scalar_tensor_tensor(out=scale_a[:, :, :], in0=mod[:, a:a + KC, :], scalar=1.0,
                                                in1=vec(g).unsqueeze(2).broadcast_to([P, KC, 2]),
                                                op0=ALU.add, op1=ALU.mult)

            dve.wait_ge(mods_done, NMOD1)
            add_bias(0, 2 * NMOD1)
            one_plus_scale(SCALE1, "g_mix").then_inc(mod1_ready, 1)

            dve.wait_ge(job_done, KC)
            link(dve.memset(up[:, 0:UL], 0.0))
            link(dve.memset(up[:, UL + N_LAT:UC], 0.0))
            dve.memset(up[:, UC + N_CTX:T + 6], 0.0).then_inc(up_ready, 1)

            SEQS = ((UL, 0, N_LAT), (UC, N_LAT, N_CTX))

            def conv(k):
                w0 = ROWS["w_conv"][0]
                dve.wait_ge(job_read, JOB[("L", k)] + 1)
                if k >= 2:
                    dve.wait_ge(job_done, JOB[("G", k - 2, 1, 1)] + 1)
                for o, a, n in SEQS:
                    u = up[:, o - 2:o - 2 + n]
                    link(dve.tensor_scalar(xc[:, k % 2, a:a + n], u, vecs[:, w0 + k:w0 + k + 1],
                                           vec("b_conv")[:, k:k + 1], ALU.mult, ALU.add))
                for tap in range(1, CONV_W):
                    for i, (o, a, n) in enumerate(SEQS):
                        u = up[:, o - 2 + tap:o - 2 + tap + n]
                        ins = dve.scalar_tensor_tensor(out=xc[:, k % 2, a:a + n], in0=u,
                                                       scalar=vecs[:, w0 + LC * tap + k:w0 + LC * tap + k + 1],
                                                       in1=xc[:, k % 2, a:a + n], op0=ALU.mult, op1=ALU.add)
                        if tap == CONV_W - 1 and i == 1:
                            ins.then_inc(conv_done, 1)
                        elif i == 1:
                            link(ins)

            def scan(k, r):
                d = 2 * k + r
                m = r * LC + k
                dve.wait_ge(decay_ready, d + 1)
                link(dve.tensor_tensor(i_b[:, :], i_b[:, :], xc[:, k % 2, :], ALU.mult))
                link(dve.scalar_tensor_tensor(out=tau[:, :], in0=r_a[:, :], scalar=1.0, in1=tau[:, :],
                                              op0=ALU.add, op1=ALU.mult))
                link(dve.tensor_tensor(i_b[:, :], i_b[:, :], tau[:, :], ALU.mult))
                dst = y_t[:, LC + k, :] if r == 0 else tau[:, :]
                for n, (a, b) in enumerate(((0, N_LAT), (N_LAT, T))):
                    def run(x):
                        x = x[:, a:b]
                        return x if r == 0 else x[:, ::-1]
                    start = states[:, m:m + 1] if n == 0 else 0.0
                    link(dve.tensor_tensor_scan(run(dst), run(r_a[:, :]), run(i_b[:, :]), start, ALU.mult, ALU.add))
                end = T - 1 if r == 0 else N_LAT
                link(dve.tensor_copy(st_out[:, m:m + 1], dst[:, end:end + 1]))
                if r == 1:
                    dve.tensor_tensor(y_t[:, LC + k, :], y_t[:, LC + k, :], tau[:, :], ALU.add).then_inc(scan_done, 1)
                    dve.wait_ge(scan_done, d + 1)
                else:
                    dve.nop().then_inc(scan_done, 1)

            def pooling(g):
                q = POOL_ORDER.index(g)
                dve.wait_ge(small_loaded, SMALL)
                dve.wait_ge(box_ready, q + 1)
                d = y_t[:, g, 0:N_LAT].rearrange("p (r w) -> p r w", w=GRID_W)
                s = box[g % 2][:, PAD * GRID_W:(PAD + GRID_H) * GRID_W].rearrange("p (r w) -> p r w", w=GRID_W)
                by_col = inv[:, g, 0:GRID_W].unsqueeze(1).broadcast_to([P, GRID_H, GRID_W])
                by_row = inv[:, g, GRID_W:GRID_W + GRID_H].unsqueeze(2).broadcast_to([P, GRID_H, GRID_W])
                link(dve.tensor_tensor(d, s, by_col, ALU.mult))
                link(dve.tensor_tensor(d, d, by_row, ALU.mult))
                link(dve.tensor_tensor(d, d, pad_l[:, q % 2, :, PAD:PAD + GRID_W], ALU.subtract))
                dc = y_t[:, g, N_LAT:T]
                link(dve.tensor_tensor(dc, box_c[g % 2][:, PAD:PAD + N_CTX], inv[:, g, GRID_W + GRID_H:NI], ALU.mult))
                dve.tensor_tensor(dc, dc, pad_c[:, q % 2, PAD:PAD + N_CTX], ALU.subtract).then_inc(pooled, 1)

            def gated(k):
                dve.wait_ge(job_read, JOB[("E", k)] + 1)
                dve.tensor_tensor(y_t[:, LC + k, :], y_t[:, LC + k, :], gelu[:, 0:T], ALU.mult).then_inc(gelu_used, 1)

            conv(0)
            conv(1)
            scan(0, 0)
            scan(0, 1)
            pooling(3)
            scan(1, 0)
            conv(2)
            scan(1, 1)
            conv(3)
            pooling(2)
            scan(2, 0)
            scan(2, 1)
            pooling(1)
            scan(3, 0)
            gated(0)
            scan(3, 1)
            pooling(0)
            for k in range(1, LC):
                gated(k)
            dve.wait_ge(state_turned, 1)
            dve.tensor_copy(st_rows[:, :], ps[0:8, 7, 0:P]).then_inc(state_kept, 1)

            dve.wait_ge(mods_done, NMOD1 + NMOD2)
            add_bias(2 * NMOD1, 48)
            link(one_plus_scale(SCALE2, "g_ffn"))
            dve.nop().then_inc(mod2_ready, 1)
            dve.wait_ge(pooled, NG)
            for q in range(16):
                v, s, h = q // 4, q // 2 % 2, q % 2
                src = (mod[:, GATE1:GATE1 + KC, s], scale_a[:, :, s], mod[:, SHIFT2:SHIFT2 + KC, s],
                       mod[:, GATE2:GATE2 + KC, s])[v]
                if q >= 2:
                    dve.wait_ge(rows_spread, q - 1)
                dve.tensor_tensor(box[q % 2][:, 0:512].rearrange("p (k n) -> p k n", k=4),
                                  ident[:, :].unsqueeze(1).broadcast_to([P, 4, P]),
                                  src[:, 4 * h:4 * h + 4].unsqueeze(2).broadcast_to([P, 4, P]), ALU.mult)\
                   .then_inc(diag_ready, 1)

            dve.wait_ge(rows_kept, 16)
            for s in range(NT + 5):
                if s < NT:
                    t = TILES[s]
                    dve.wait_ge(res_loaded[s % 2], 16 * (s // 2 + 1))
                    if s >= 2:
                        dve.wait_ge(y_stored[s % 2], 16 * (s // 2))
                        dve.wait_ge(xn2_ready, s - 1)
                    dve.wait_ge(mix_done, s + 1)
                    b = 2 * (s % 2)
                    dve.tensor_tensor(x1[:, s % 2, :], ps[:, b:b + 2, :].rearrange("p b n -> p (b n)"),
                                      bc[:, 0, stream(t), :], ALU.mult).then_inc(mix_read, 1)
                    dve.wait_ge(mix_read, s + 1)
                    dve.tensor_tensor(x1[:, s % 2, :], x1[:, s % 2, :], x_res[:, s % 2, :], ALU.add).then_inc(x1_ready, 1)
                    dve.wait_ge(xn2_ready, s + 1)
                    link(dve.tensor_tensor(hn2[:, s % 2, :], hn2[:, s % 2, :], bc[:, 1, stream(t), :], ALU.mult))
                    dve.tensor_tensor(hn2[:, s % 2, :], hn2[:, s % 2, :], bc[:, 2, stream(t), :], ALU.add)\
                       .then_inc(hn2_ready, 1)
                if 0 <= s - 2 < NT:
                    t = s - 2
                    dve.wait_ge(logits_done, t + 1)
                    dve.tensor_reduce(logit_max[:, t:t + 1], ps[:, 6, 0:NE], AX.X, ALU.max, negate=True)\
                       .then_inc(max_ready, 1)
                if 0 <= s - 3 < NT:
                    t = s - 3
                    dve.wait_ge(exp_ready, t + 1)
                    link(dve.reciprocal(prob_inv[:, t:t + 1], prob_sum[:, t:t + 1]))
                    dve.tensor_scalar(probs[:, t, :], probs[:, t, :], prob_inv[:, t:t + 1], None, ALU.mult)\
                       .then_inc(probs_ready, 1)
                if 0 <= s - 4 < NT:
                    t = s - 4
                    dve.wait_ge(probs_turned, t + 1)
                    dst = aff_c[:, :] if TILES[t] == CTX_TILE else aff_l[:, TILES[t] * P:(TILES[t] + 1) * P]
                    dve.tensor_copy(dst, ps[0:NE, 7, 0:P]).then_inc(aff_ready, 1)

            dve.wait_ge(aff_ready, NT)

            def top(aff, work, best, index, rounds):
                src = aff
                for r in range(rounds):
                    link(dve.max(best[:, 8 * r:8 * r + 8], src))
                    ins = dve.max_index(index[:, 8 * r:8 * r + 8], best[:, 8 * r:8 * r + 8], src)
                    if r < rounds - 1:
                        link(dve.match_replace(work[r % 2], best[:, 8 * r:8 * r + 8], src, -1.0))
                        src = work[r % 2]
                link(ins)

            top(aff_c[:, :], [w[:, 0:N_CTX] for w in aff_w], top_c, top_ci, CAP_C // 8)
            top(aff_l[:, :], [w[:, :] for w in aff_w], top_l, top_li, CAP_L // 8)
            link(dve.tensor_copy(top_lf[:, :], top_li[:, :]))
            link(dve.tensor_copy(top_cf[:, :], top_ci[:, :]))
            link(dve.tensor_scalar(top_cf[:, :], top_cf[:, :], float(N_LAT), None, ALU.add))
            dve.nop().then_inc(top_ready, 1)
            dve.wait_ge(top_turned, 4)
            dve.tensor_copy(g_lat[:, :], ps[:, 4, 0:NE]).then_inc(routed, 1)
            dve.tensor_copy(i_lat[:, :], ps[:, 4, NE:2 * NE]).then_inc(routed, 1)
            dve.tensor_copy(g_ctx[:, :], ps[0:CAP_C, 4, 2 * NE:3 * NE]).then_inc(routed, 1)
            dve.tensor_copy(i_ctx[:, :], ps[0:CAP_C, 4, 3 * NE:4 * NE]).then_inc(routed, 1)
            dve.wait_ge(routed, 4)

            def column(x, e):
                return x[:, e:e + 1] if isinstance(e, int) else x[:, bass.ds(e, 1)]

            def gather_index(e):
                dve.wait_ge(routed, 4)
                dve.tensor_copy(gi_lat[:, :], column(i_lat, e))
                dve.tensor_copy(gi_ctx[:, :], column(i_ctx, e)).then_inc(gi_ready, 1)

            def split_low(e, j):
                dve.wait_ge(hi_done, e * UPE + (j + 1))
                a = KC - POOL_KC
                dve.tensor_tensor(split[:, j % SPLIT, 1, 0:a, :], raw[:, slot(MOE0 + j), 0:a, :],
                                  split[:, j % SPLIT, 0, 0:a, :].bitcast(f32), ALU.subtract).then_inc(lo_dve, 1)

            def hidden_low(e, k):
                dve.wait_ge(hid_hi, e * 4 + (k + 1))
                dve.tensor_tensor(hid[:, 1, 2 * k:2 * k + 2, :], hid_f[:, k % 2, :].rearrange("p (c n) -> p c n", c=2),
                                  hid[:, 0, 2 * k:2 * k + 2, :].bitcast(f32), ALU.subtract).then_inc(hid_lo, 1)

            def after_up(e, k):
                if k > 0:
                    hidden_low(e, k - 1)
                dve.wait_ge(silu_done, e * 4 + (k + 1))
                dve.wait_ge(unit_done, e * UPE + (2 * k + 2))
                dve.tensor_tensor(hid_f[:, k % 2, :], ps[:, 2 + k % 2, 0:2 * CAP], gate_s[:, k % 2, :], ALU.mult)\
                   .then_inc(mul_done, 1)
                if k == 3:
                    hidden_low(e, 3)

            def input_low(e):
                dve.wait_ge(xt_hi, e + 1)
                for h in range(2):
                    dve.tensor_tensor(xt[:, 1, 4 * h:4 * h + 4, 0:CAP_L], ps[:, 6 + h, :].rearrange("p (k n) -> p k n", k=4),
                                      xt[:, 0, 4 * h:4 * h + 4, 0:CAP_L].bitcast(f32), ALU.subtract)
                dve.tensor_tensor(xt[:, 1, :, CAP_L:CAP], ps[:, 0, 0:KC * CAP_C].rearrange("p (k n) -> p k n", k=KC),
                                  xt[:, 0, :, CAP_L:CAP].bitcast(f32), ALU.subtract).then_inc(xt_lo, 1)

            def scatter_index(e):
                dve.wait_ge(routed, 4)
                dve.tensor_copy(si_lat[:, :], column(i_lat, e))
                dve.tensor_copy(si_ctx[:, :], column(i_ctx, e))
                dve.tensor_copy(sg_lat[:, :], column(g_lat, e))
                dve.tensor_copy(sg_ctx[:, :], column(g_ctx, e)).then_inc(si_ready, 1)

            def scale_rows(e):
                dve.wait_ge(si_ready, e + 1)
                dve.wait_ge(rows_turned, e + 1)
                for h in range(2):
                    a, b = 512 * h, 512 * h + 512
                    dve.scalar_tensor_tensor(out=o_l[:, a:b], in0=ps[:, 6 + h, :], scalar=sg_lat[:, 0:1],
                                             in1=g2[:, 0, a:b], op0=ALU.mult, op1=ALU.mult)
                    ins = dve.scalar_tensor_tensor(out=o_c[:, a:b], in0=ps[0:CAP_C, 4 + h, :], scalar=sg_ctx[:, 0:1],
                                                   in1=g2[0:CAP_C, 1, a:b], op0=ALU.mult, op1=ALU.mult)
                ins.then_inc(out_scaled, 1)

            def expert(e, is_first, is_last):
                for j in range(UPE):
                    if j == 1 and not is_last:
                        gather_index(e + 1)
                    if j == 1 and not is_first:
                        scatter_index(e - 1)
                    if j == UPE - 1 and not is_first:
                        dve.wait_ge(scattered, e * 32)
                    if not (is_first and j < LAG):
                        split_low(e, j)
                    if j >= LAG and (j - LAG) % 2 == 1 and j - LAG < 8:
                        after_up(e, (j - LAG) // 2)
                    if j == LAG + 1 and not is_first:
                        scale_rows(e - 1)
                    if j == 7 + LAG and not is_last:
                        input_low(e + 1)

            gather_index(0)
            for j in range(LAG):
                split_low(0, j)
            input_low(0)
            expert(0, True, False)
            with dve.Fori(1, NE - 1) as e:
                expert(e, False, False)
            expert(NE - 1, False, True)
            scatter_index(NE - 1)
            scale_rows(NE - 1)

            dve.wait_ge(g_fin_loaded, 16)
            for t in range(NT):
                dve.wait_ge(rstd3_ready, t + 1)
                dve.scalar_tensor_tensor(out=y_end[:, t, :], in0=y_end[:, t, :], scalar=rstd[:, 2, t:t + 1],
                                         in1=g_fin[:, :], op0=ALU.mult, op1=ALU.mult).then_inc(end_ready, 1)

        @block.tensor
        def _(pe):
            pe.wait_ge(ident_loaded, 16)
            pe.wait_ge(rows_loaded, 16 * (len(ROWS) + 1))
            pe.transpose(ps[:, 7, 0:P], rows_in[:, :], ident[:, :]).then_inc(vecs_turned, 1)
            pe.transpose(ps[:, 7, P:P + 8], rows_st[:, :], ident[0:8, 0:8]).then_inc(vecs_turned, 1)

            def modulate(u):
                n = UNIT[("mod", u)]
                pe.wait_ge(loaded[slot(n)], loads(n))
                for i in range(2):
                    for k in range(KC):
                        ins = pe.matmul(ps[:, 6, 2 * (2 * u + i):2 * (2 * u + i) + 2],
                                        raw[:, slot(n), k, i * P:(i + 1) * P], silu_c[:, k, :],
                                        start=(k == 0), stop=(k == KC - 1))
                ins.then_inc(mods_done, 1)

            pe.wait_ge(silu_ready, 1)
            for u in range(NMOD1):
                modulate(u)

            for job in order:
                if job[0] == "M":
                    if job[1] == 0:
                        pe.wait_ge(mod1_ready, 1)
                    for u in range(job[1], job[2]):
                        modulate(NMOD1 + u)
                    continue
                j = JOB[job]
                b = 3 * (j % 2)
                if j >= 2:
                    pe.wait_ge(job_read, j - 1)
                kind, k = job[0], job[1]
                if kind == "x":
                    if k == 0:
                        pe.wait_ge(xn_ready, NT)
                    for t in range(NT):
                        ins = pe.transpose(ps[:, b + t // 4, (t % 4) * P:(t % 4 + 1) * P], x_in[:, t, k * P:(k + 1) * P],
                                           ident[:, :])
                    ins.then_inc(job_done, 1)
                elif kind in IN_CHUNK:
                    ch = IN_CHUNK[kind] + k
                    n = UNIT[("in", ch // 2)]
                    if job == ("L", 0):
                        pe.wait_ge(job_read, KC)
                    pe.wait_ge(loaded[slot(n)], loads(n))
                    for kk in range(KC):
                        for seg in range(3):
                            ins = pe.matmul(ps[:, b + seg, 0:SEG], raw[:, slot(n), kk, (ch % 2) * P:(ch % 2 + 1) * P],
                                            h_t[:, kk, seg * SEG:(seg + 1) * SEG], start=(kk == 0), stop=(kk == KC - 1))
                    ins.then_inc(job_done, 1)
                elif kind == "G":
                    _, k, r, ax = job
                    pe.wait_ge(small_loaded, SMALL)
                    pe.wait_ge(conv_done, k + 1)
                    for seg in range(3):
                        ins = pe.matmul(ps[:, b + seg, 0:SEG], w_gates[:, ax, r, k, :],
                                        xc[:, k % 2, seg * SEG:(seg + 1) * SEG], start=True, stop=True)
                    ins.then_inc(job_done, 1)
                else:
                    pe.wait_ge(pooled, POOL_ORDER.index(k) + 1)
                    for seg in range(3):
                        ins = pe.matmul(ps[:, b + seg, 0:SEG], w_p[:, k, :], y_t[:, k, seg * SEG:(seg + 1) * SEG],
                                        start=True, stop=True)
                    ins.then_inc(job_done, 1)
            pe.wait_ge(scan_done, 2 * LC)
            pe.transpose(ps[0:8, 7, 0:P], st_out[:, :], ident[:, :]).then_inc(state_turned, 1)

            pe.wait_ge(mod2_ready, 1)
            pe.wait_ge(state_kept, 1)
            pe.wait_ge(ones_ready, 1)
            for q in range(16):
                pe.wait_ge(diag_ready, q + 1)
                if q >= 2:
                    pe.wait_ge(rows_kept, q - 1)
                pe.matmul(ps[:, 6 + q % 2, :], ones[:, :], box[q % 2][:, 0:512], start=True, stop=True)\
                  .then_inc(rows_spread, 1)

            pe.wait_ge(job_read, NJOBS)
            pe.wait_ge(gelu_used, LC)
            pe.wait_ge(rows_kept, 16)
            for u in range(D // UW):
                pe.wait_ge(loaded[slot(OUT0 + u)], loads(OUT0 + u))
            for s in range(NT + 4):
                if s < NT:
                    t = TILES[s]
                    if s >= 2:
                        pe.wait_ge(mix_read, s - 1)
                    for u in range(D // UW):
                        for k in range(KC):
                            ins = pe.matmul(ps[:, 2 * (s % 2) + u // 2, (u % 2) * UW:(u % 2 + 1) * UW],
                                            y_t[:, k, t * P:(t + 1) * P], raw[:, slot(OUT0 + u), k, :],
                                            start=(k == 0), stop=(k == KC - 1))
                    ins.then_inc(mix_done, 1)
                if 0 <= s - 1 < NT:
                    t = s - 1
                    pe.wait_ge(hn2_ready, t + 1)
                    if t >= 1:
                        pe.wait_ge(hn2_t_ready, t)
                    for k in range(KC):
                        ins = pe.transpose(ps[:, 4 + k // 4, (k % 4) * P:(k % 4 + 1) * P], hn2[:, t % 2, k * P:(k + 1) * P],
                                           ident[:, :])
                    ins.then_inc(hn2_turned, 1)
                if 0 <= s - 2 < NT:
                    t = s - 2
                    pe.wait_ge(hn2_t_ready, t + 1)
                    if t >= 1:
                        pe.wait_ge(exp_ready, t)
                    for k in range(KC):
                        ins = pe.matmul(ps[:, 6, 0:NE], hn2_t[:, t % 2, k, :], w_r[:, k, :],
                                        start=(k == 0), stop=(k == KC - 1))
                    ins.then_inc(logits_done, 1)
                if 0 <= s - 4 < NT:
                    t = s - 4
                    pe.wait_ge(probs_ready, t + 1)
                    if t >= 1:
                        pe.wait_ge(aff_ready, t)
                    pe.transpose(ps[0:NE, 7, 0:P], probs[:, t, :], ident[:, :]).then_inc(probs_turned, 1)

            pe.wait_ge(top_ready, 1)
            pe.transpose(ps[:, 4, 0:NE], top_l[:, :], ident[0:NE, 0:NE]).then_inc(top_turned, 1)
            pe.transpose(ps[:, 4, NE:2 * NE], top_lf[:, :], ident[0:NE, 0:NE]).then_inc(top_turned, 1)
            pe.transpose(ps[0:CAP_C, 4, 2 * NE:3 * NE], top_c[:, :], ident[0:NE, 0:NE]).then_inc(top_turned, 1)
            pe.transpose(ps[0:CAP_C, 4, 3 * NE:4 * NE], top_cf[:, :], ident[0:NE, 0:NE]).then_inc(top_turned, 1)

            def turn_input(e):
                pe.wait_ge(gathered, e * 32 + 32)
                if not (isinstance(e, int) and e == 0):
                    pe.wait_ge(silu_done, e * 4 - 1)
                    if not (isinstance(e, int) and e == 1):
                        pe.wait_ge(out_scaled, e - 1)
                for k in range(KC):
                    pe.transpose(ps[:, 6 + k // 4, (k % 4) * P:(k % 4 + 1) * P], x_l[:, k * P:(k + 1) * P], ident[:, :])
                for k in range(KC):
                    ins = pe.transpose(ps[:, 0, k * CAP_C:(k + 1) * CAP_C], x_c[:, k * P:(k + 1) * P],
                                       ident[0:CAP_C, 0:CAP_C])
                ins.then_inc(x_turned, 1)

            def turn_rows(e):
                pe.wait_ge(down_read, e * 4 + 4)
                if isinstance(e, int) and e == NE - 1:
                    pe.wait_ge(out_scaled, e)
                else:
                    pe.wait_ge(xt_lo, e + 2)
                for k in range(KC):
                    pe.transpose(ps[:, 6 + k // 4, (k % 4) * P:(k % 4 + 1) * P], down[:, k, 0:CAP_L], ident[:, :])
                for k in range(KC):
                    ins = pe.transpose(ps[0:CAP_C, 4 + k // 4, (k % 4) * P:(k % 4 + 1) * P], down[:, k, CAP_L:CAP],
                                       ident[:, :])
                ins.then_inc(rows_turned, 1)

            def product(e, j):
                pe.wait_ge(lo_dve, e * UPE + (j + 1))
                pe.wait_ge(lo_pool, e * UPE + (j + 1))
                some = not (isinstance(e, int) and e == 0)
                if j < 8:
                    k = j // 2
                    bank = 2 * (j % 2) + k % 2
                    if j == 0:
                        pe.wait_ge(xt_lo, e + 1)
                    if some or k >= 2:
                        pe.wait_ge((silu_done, mul_done)[j % 2], e * 4 + (k - 1))
                    rhs = xt
                else:
                    k = j - 8
                    bank = 4 + k % 2
                    if some or k >= 2:
                        pe.wait_ge(down_read, e * 4 + (k - 1))
                    if k == 0:
                        if some:
                            pe.wait_ge(out_scaled, e)
                        pe.wait_ge(hid_lo, e * 4 + 3)
                    rhs = hid
                w = split[:, j % SPLIT, :, :, :]
                for i in range(2):
                    for c in range(KC):
                        if j == 8 and i == 0 and c == KC - 2:
                            pe.wait_ge(hid_lo, e * 4 + 4)
                        for a, b in ((0, 0), (0, 1), (1, 0)):
                            ins = pe.matmul(ps[:, bank, i * CAP:(i + 1) * CAP], w[:, a, c, i * P:(i + 1) * P],
                                            rhs[:, b, c, :], start=(c == 0 and a == b == 0),
                                            stop=(c == KC - 1 and a == 1))
                ins.then_inc(unit_done, 1)

            def expert(e, is_first, is_last):
                for j in range(UPE):
                    product(e, j)
                    if j == 0 and not is_first:
                        turn_rows(e - 1)
                    if j == 7 and not is_last:
                        turn_input(e + 1)

            pe.wait_ge(routed, 4)
            turn_input(0)
            expert(0, True, False)
            with pe.Fori(1, NE - 1) as e:
                expert(e, False, False)
            expert(NE - 1, False, True)
            turn_rows(NE - 1)


_INS = ["x_prompt", "x_sample", "state_rglru", "c", "c_ctx", "w_mod", "b_mod", "g_norm_mix", "g_norm_ffn", "w_in",
        "w_pool", "pool_scale", "w_conv", "b_conv", "w_gate_a", "b_gate_a", "w_gate_x", "b_gate_x", "lru_lambda",
        "w_out", "w_router", "w_exp_gate", "w_exp_up", "w_exp_down", "g_final"]
_OUTS = [((1, N_CTX, D), "float32"), ((1, N_LAT, D), "float32"), ((1, 1, 2, LC * P), "float32")]


def window_counts():
    out = np.zeros((NG, GRID_W + GRID_H + N_CTX), np.float32)
    for g in range(NG):
        w, at = 2 ** (g + 1), 0
        for n in (GRID_W, GRID_H, N_CTX):
            t = np.arange(n)
            count = np.minimum(t + w - w // 2, n) - np.maximum(t - w // 2, 0)
            out[g, at:at + n] = 1.0 / count
            at += n
    return out


def kernel(**inputs):
    import concourse.bacc as _bacc
    from concourse import mybir as _mybir
    from concourse.bass_utils import run_bass_kernel_spmd as _run

    nc = _bacc.Bacc("TRN2", target_bir_lowering=False, num_devices=1)
    arrays, args = {}, []
    consts = {"identity": np.eye(P, dtype=np.float32), "inv_count": window_counts()}
    for name in _INS + list(consts):
        a = np.ascontiguousarray(inputs[name] if name in inputs else consts[name])
        arrays[f"in_{name}_dram"] = a
        args.append(nc.dram_tensor(f"in_{name}_dram", a.shape, _mybir.dt.from_np(a.dtype), kind="ExternalInput").ap())
    for i, (shape, dtype) in enumerate(_OUTS):
        args.append(nc.dram_tensor(f"out_{i}_dram", shape, _mybir.dt.from_np(np.dtype(dtype)),
                                   kind="ExternalOutput").ap())
    hybrid_step_kernel(nc, *args)
    r = _run(nc, [arrays], core_ids=[0])
    return tuple(r.results[0][f"out_{i}_dram"] for i in range(len(_OUTS)))
```

```python
from contextlib import ExitStack

import numpy as np
import concourse.bass as bass
from concourse import mybir

D = 1024
P = 128
KC = D // P
N_LAT, N_CTX = 1024, 128
T = N_LAT + N_CTX
NT = T // P
CTX_TILE = NT - 1
SEG = T // 3
GRID_W, GRID_H = 64, N_LAT // 64
PAD = 8
PW = GRID_W + 2 * PAD
PH = GRID_H + 2 * PAD
NG = 4
LC = 4
CONV_W = 4
NE, CAP_L, CAP_C = 16, 128, 16
CAP = CAP_L + CAP_C
EPS = 1e-6
UW = 256
UN = KC * UW
RAW = 6
TILES_A = 5
SPLIT = 4
UPE = 12

ROWS = {}
_at = 0
for _name, _n in (("b_mod", 48), ("g_mix", 8), ("g_ffn", 8), ("c", 8), ("c_ctx", 8), ("pool_scale", 4),
                  ("w_conv", 16), ("b_conv", 4), ("b_gate_a", 8), ("b_gate_x", 8), ("lam", 8)):
    ROWS[_name] = (_at, _at + _n)
    _at += _n
assert _at == P

SHIFT1, SCALE1, GATE1, SHIFT2, SCALE2, GATE2 = (8 * i for i in range(6))
NMOD1, NMOD2 = 8, 16


def hybrid_step_kernel(nc, x_prompt, x_sample, state_rglru, c, c_ctx, w_mod, b_mod, g_norm_mix, g_norm_ffn,
                       w_in, w_pool, pool_scale, w_conv, b_conv, w_gate_a, b_gate_a, w_gate_x, b_gate_x,
                       lru_lambda, w_out, w_router, w_exp_gate, w_exp_up, w_exp_down, g_final,
                       identity, inv_count, y_prompt, y_sample, new_state):
    f32, f32r, u32 = mybir.dt.float32, mybir.dt.float32r, mybir.dt.uint32
    ACT = mybir.ActivationFunctionType
    ALU = mybir.AluOpType
    AX = mybir.AxisListType

    order = [("x", k) for k in range(KC)]
    order += [("M", 0), ("L", 0), ("M", 1), ("M", 2), ("L", 1), ("M", 3), ("G", 0, 0, 0), ("G", 0, 0, 1),
              ("P", 3), ("M", 4), ("G", 0, 1, 0), ("G", 0, 1, 1), ("P", 2), ("M", 5), ("G", 1, 0, 0), ("G", 1, 0, 1),
              ("L", 2), ("M", 6), ("G", 1, 1, 0), ("G", 1, 1, 1), ("L", 3), ("M", 7), ("G", 2, 0, 0), ("G", 2, 0, 1),
              ("P", 1), ("M", 8), ("G", 2, 1, 0), ("G", 2, 1, 1), ("P", 0), ("M", 9), ("G", 3, 0, 0), ("G", 3, 0, 1),
              ("E", 0), ("M", 10), ("G", 3, 1, 0), ("G", 3, 1, 1), ("E", 1), ("M", 11), ("E", 2), ("M", 12),
              ("M", 13), ("E", 3), ("M", 14), ("M", 15)]
    order += [("O", g) for g in (3, 2, 1, 0)]
    JOB = {j: n for n, j in enumerate(j for j in order if j[0] != "M")}
    NJOBS = len(JOB)
    POOL_ORDER = (3, 2, 1, 0)

    IN_CHUNK = {"P": 0, "L": 4, "E": 8}
    units = [("mod", u) for u in range(NMOD1)]
    for j in order:
        if j[0] == "M":
            units.append(("mod", NMOD1 + j[1]))
        elif j[0] in IN_CHUNK:
            u = ("in", (IN_CHUNK[j[0]] + j[1]) // 2)
            if u not in units:
                units.append(u)
    units += [("out", u) for u in range(D // UW)]
    UNIT = {u: n for n, u in enumerate(units)}
    OUT0 = UNIT[("out", 0)]
    MOE0 = len(units)

    def slot(n):
        return n % RAW

    def loads(n):
        return 16 * (n // RAW + 1)

    h_rows = nc.dram_tensor("h_rows", [T, D], f32).ap()
    y_rows = nc.dram_tensor("y_rows", [T, D], f32).ap()

    ctx = ExitStack()
    phase1, phase2, moe, last = ExitStack(), ExitStack(), ExitStack(), ExitStack()

    def sb(name, shape, dt=f32, stack=ctx):
        return stack.enter_context(nc.sbuf_tensor(name, shape, dt))

    def sem(name):
        return ctx.enter_context(nc.semaphore(name))

    with ctx:
        ps = ctx.enter_context(nc.psum_tensor("ps", [P, 8, 512], f32))

        raw = sb("raw", [P, RAW, KC, UW])
        ident = sb("ident", [P, P])
        ones = sb("ones", [P, P])
        vecs = sb("vecs", [P, P])
        states = sb("states", [P, 8])
        silu_c = sb("silu_c", [P, KC, 2])
        mod = sb("mod", [P, 48, 2])
        scale_a = sb("scale_a", [P, KC, 2])
        spare = sb("spare", [P, 2])
        half = sb("half", [P, 1])
        lam_t = sb("lam_t", [P, 6, 8])
        rate = sb("rate", [P, 2, 8])
        st_out, st_rows = sb("st_out", [P, 8]), sb("st_rows", [8, P])
        sumsq = sb("sumsq", [P, 3, NT])
        rstd = sb("rstd", [P, 3, NT])
        w_r = sb("w_r", [P, KC, NE])
        logit_max = sb("logit_max", [P, NT])
        prob_sum = sb("prob_sum", [P, NT])
        prob_inv = sb("prob_inv", [P, NT])
        probs = sb("probs", [P, NT, NE])
        g_lat, i_lat = sb("g_lat", [CAP_L, NE]), sb("i_lat", [CAP_L, NE], u32)
        g_ctx, i_ctx = sb("g_ctx", [CAP_C, NE]), sb("i_ctx", [CAP_C, NE], u32)
        gi_lat, gi_ctx = sb("gi_lat", [CAP_L, 1], u32), sb("gi_ctx", [CAP_C, 1], u32)
        si_lat, si_ctx = sb("si_lat", [CAP_L, 1], u32), sb("si_ctx", [CAP_C, 1], u32)
        sg_lat, sg_ctx = sb("sg_lat", [CAP_L, 1]), sb("sg_ctx", [CAP_C, 1])

        y_t = sb("y_t", [P, KC, T], stack=phase1)
        h_t = sb("h_t", [P, KC, T], stack=phase1)
        h_flat = h_t[:, :, :].rearrange("p k t -> p (k t)")
        bc = h_flat[:, 0:6 * D].rearrange("p (v s d) -> p v s d", v=3, s=2)
        g2 = h_flat[:, 7 * D:9 * D].rearrange("p (s d) -> p s d", s=2)
        x_in_stack = ExitStack()
        x_in = sb("x_in", [P, NT, D], stack=x_in_stack)
        junk0 = sb("junk0", [P, D], stack=x_in_stack)
        rows_in = sb("rows_in", [P, P], stack=x_in_stack)
        rows_st = sb("rows_st", [8, P], stack=x_in_stack)
        mod_rows = sb("mod_rows", [2, NMOD1 * UW], stack=x_in_stack)
        x_in_stack.close()
        lru = ExitStack()
        up = sb("up", [P, T + 6], stack=lru)
        UL, UC = 2, N_LAT + 5
        xc = sb("xc", [P, 2, T], stack=lru)
        r_a = sb("r_a", [P, T], stack=lru)
        i_b = sb("i_b", [P, T], stack=lru)
        tau = sb("tau", [P, T], stack=lru)
        pad_l = sb("pad_l", [P, 2, GRID_H, PW], stack=lru)
        pad_c = sb("pad_c", [P, 2, N_CTX + 2 * PAD], stack=lru)
        box = [sb(f"box{i}", [P, PH * GRID_W], stack=lru) for i in range(2)]
        box_c = [sb(f"box_c{i}", [P, N_CTX + 2 * PAD], stack=lru) for i in range(2)]
        tall = sb("tall", [P, PH, GRID_W], stack=lru)
        NI = GRID_W + GRID_H + N_CTX
        inv = sb("inv", [P, NG, NI], stack=lru)
        w_gates = sb("w_gates", [P, 2, 2, LC, P], stack=lru)
        w_p = sb("w_p", [P, NG, P], stack=lru)
        part = sb("part", [P, 2, 2, UW], stack=lru)
        gelu = up
        lru.close()
        x_res = sb("x_res", [P, 2, D], stack=phase2)
        x1 = sb("x1", [P, 2, D], stack=phase2)
        hn2 = sb("hn2", [P, 2, D], stack=phase2)
        hn2_t = sb("hn2_t", [P, 2, KC, P], stack=phase2)
        junk1 = sb("junk1", [P, D], stack=phase2)
        aff_a = sb("aff_a", [NE, TILES_A * P], stack=phase2)
        aff_b = sb("aff_b", [NE, N_LAT - TILES_A * P], stack=phase2)
        aff_c = sb("aff_c", [NE, N_CTX], stack=phase2)
        aff_w = [sb(f"aff_w{i}", [NE, max(TILES_A * P, N_LAT - TILES_A * P)], stack=phase2) for i in range(2)]
        top_a, top_ai, top_af = sb("top_a", [NE, CAP_L], stack=phase2), sb("top_ai", [NE, CAP_L], u32, stack=phase2), sb("top_af", [NE, CAP_L], stack=phase2)
        top_b, top_bi = sb("top_b", [NE, CAP_L], stack=phase2), sb("top_bi", [NE, CAP_L], u32, stack=phase2)
        rev_b, rev_bf = sb("rev_b", [NE, CAP_L], stack=phase2), sb("rev_bf", [NE, CAP_L], stack=phase2)
        pair, pair_d = sb("pair", [CAP_L, 4, NE], stack=phase2), sb("pair_d", [CAP_L, 2, NE], stack=phase2)
        top_c, top_ci, top_cf = sb("top_c", [NE, CAP_C], stack=phase2), sb("top_ci", [NE, CAP_C], u32, stack=phase2), sb("top_cf", [NE, CAP_C], stack=phase2)
        phase2.close()
        phase1.close()

        split = sb("split", [P, SPLIT, 2, KC, UW], f32r, stack=moe)
        sb("g2_kept", [P, 2 * D], stack=moe)
        x_l = sb("x_l", [CAP_L, D], stack=moe)
        x_c = sb("x_c", [CAP_C, D], stack=moe)
        xt = sb("xt", [P, KC, 2, CAP], f32r, stack=moe)
        gate_f = sb("gate_f", [P, 2, 2, CAP], stack=moe)
        gate_s = sb("gate_s", [P, 2, 2, CAP], stack=moe)
        up_f = sb("up_f", [P, 2, CAP], stack=moe)
        hid_f = sb("hid_f", [P, 2, 2, CAP], stack=moe)
        hid = sb("hid", [P, KC, 2, CAP], f32r, stack=moe)
        down = sb("down", [P, KC, CAP], stack=moe)
        o_l = sb("o_l", [CAP_L, D], stack=moe)
        o_c = sb("o_c", [CAP_C, D], stack=moe)
        moe.close()
        y_end = sb("y_end", [P, NT, D], stack=last)
        junk2 = sb("junk2", [P, D], stack=last)
        g_fin = sb("g_fin", [P, D], stack=last)
        last.close()

        loaded = [sem(f"unit_loaded_{i}") for i in range(RAW)]
        rows_loaded, ident_loaded = sem("rows_loaded"), sem("ident_loaded")
        x_loaded = [sem(f"x_loaded_{t}") for t in range(NT)]
        small_loaded = sem("small_loaded")
        res_loaded = [sem(f"res_loaded_{i}") for i in range(2)]
        ones_ready = sem("ones_ready")
        vecs_turned, vecs_ready, silu_ready = sem("vecs_turned"), sem("vecs_ready"), sem("silu_ready")
        mods_done, mod1_ready, mod2_ready = sem("mods_done"), sem("mod1_ready"), sem("mod2_ready")
        mod_rows_ready, mod1_turned, part_ready = sem("mod_rows_ready"), sem("mod1_turned"), sem("part_ready")
        half_ready, sq_ready, rstd_ready, xn_ready = sem("half_ready"), sem("sq_ready"), sem("rstd_ready"), sem("xn_ready")
        job_done, job_read = sem("job_done"), sem("job_read")
        lam_act, lam_dve, rate_ready = sem("lam_act"), sem("lam_dve"), sem("rate_ready")
        pads_ready, up_ready, conv_done = sem("pads_ready"), sem("up_ready"), sem("conv_done")
        decay_ready, scan_done, gelu_used = sem("decay_ready"), sem("scan_done"), sem("gelu_used")
        box_ready, pooled = sem("box_ready"), sem("pooled")
        diag_ready, rows_spread, rows_kept = sem("diag_ready"), sem("rows_spread"), sem("rows_kept")
        state_turned, state_kept, state_stored = sem("state_turned"), sem("state_kept"), sem("state_stored")
        act_step, dve_step, pool_step = sem("act_step"), sem("dve_step"), sem("pool_step")
        mix_done, mix_read, x1_ready = sem("mix_done"), sem("mix_read"), sem("x1_ready")
        sq2_ready, rstd2_ready, xn2_ready, hn2_ready = sem("sq2_ready"), sem("rstd2_ready"), sem("xn2_ready"), sem("hn2_ready")
        h_stored = [sem(f"h_stored_{i}") for i in range(2)]
        y_stored = [sem(f"y_stored_{i}") for i in range(2)]
        hn2_turned, hn2_t_ready, logits_done = sem("hn2_turned"), sem("hn2_t_ready"), sem("logits_done")
        max_ready, exp_ready, probs_ready = sem("max_ready"), sem("exp_ready"), sem("probs_ready")
        probs_turned, aff_ready = sem("probs_turned"), sem("aff_ready")
        top_ready, top_turned, routed = sem("top_ready"), sem("top_turned"), sem("routed")
        gi_ready, gathered, x_turned, xt_hi, xt_lo = (sem("gather_index_ready"), sem("gathered"), sem("x_turned"),
                                                      sem("xt_hi"), sem("xt_lo"))
        hi_done, lo_done, unit_done = sem("hi_done"), sem("lo_done"), sem("unit_done")
        psum_read, silu_done, mul_done = sem("psum_read"), sem("silu_done"), sem("mul_done")
        hid_hi, hid_lo = sem("hid_hi"), sem("hid_lo")
        rows_turned, out_scaled, scattered = sem("rows_turned"), sem("out_scaled"), sem("scattered")
        si_ready, ctx_scaled = sem("scatter_index_ready"), sem("ctx_scaled")
        paused = sem("paused")
        y_loaded = [sem(f"y_loaded_{t}") for t in range(NT)]
        g_fin_loaded = sem("g_fin_loaded")
        sq3_ready, rstd3_ready, end_ready, stored = sem("sq3_ready"), sem("rstd3_ready"), sem("end_ready"), sem("stored")

        SMALL = 16 * 11
        LAG = 3

        def vec(name):
            a, b = ROWS[name]
            return vecs[:, a:b]

        def stream(t):
            return 1 if t == CTX_TILE else 0

        def unit_source(kind, u):
            w = {"mod": w_mod, "in": w_in, "out": w_out}[kind]
            return w[0, :, u * UW:(u + 1) * UW].rearrange("(k p) n -> p k n", p=P)

        def x_tile(t):
            return x_prompt[0, :, :] if t == CTX_TILE else x_sample[0, t * P:(t + 1) * P, :]

        def out_tile(t):
            return y_prompt[0, :, :] if t == CTX_TILE else y_sample[0, t * P:(t + 1) * P, :]

        TILES = list(range(NT - 1)) + [CTX_TILE]

        block = ctx.enter_context(nc.Block())

        @block.sync
        def _(sp):
            def wait_used(n):
                kind, u = units[n]
                if kind == "mod" and u < NMOD1:
                    sp.wait_ge(mods_done, u + 1)
                elif kind == "mod":
                    sp.wait_ge(part_ready, u - NMOD1 + 1)
                elif kind == "in":
                    sp.wait_ge(job_done, 1 + max(JOB[(x, k)] for x, a in IN_CHUNK.items() for k in range(4)
                                                 if (a + k) // 2 == u))
                else:
                    sp.wait_ge(mix_done, NT)

            def load_unit(n):
                kind, u = units[n]
                if n >= RAW:
                    wait_used(n - RAW)
                sp.dma_start(raw[:, slot(n), :, :], unit_source(kind, u)).then_inc(loaded[slot(n)], 16)

            for n in range(MOE0):
                load_unit(n)

            def load_residual(s):
                if s >= 2:
                    sp.wait_ge(x1_ready, s - 1)
                else:
                    sp.wait_ge(scan_done, 2 * LC)
                    sp.wait_ge(job_read, NJOBS)
                    sp.wait_ge(gelu_used, LC)
                    sp.wait_ge(pooled, NG)
                sp.dma_start(x_res[:, s % 2, :], x_tile(TILES[s])).then_inc(res_loaded[s % 2], 16)

            EXPERTS = {"g": w_exp_gate, "u": w_exp_up, "d": w_exp_down}

            def load_expert(e, j):
                kind, k = ("gu"[j % 2], j // 2) if j < 8 else ("d", j - 8)
                first = not isinstance(e, int)
                w = EXPERTS[kind]
                src = w[0, bass.ds(e, 1), :, k * UW:(k + 1) * UW] if first else w[0, e:e + 1, :, k * UW:(k + 1) * UW]
                sp.dma_start(raw[:, slot(MOE0 + j), :, :], src.rearrange("o (k p) n -> p (o k) n", p=P))\
                  .then_inc(loaded[slot(MOE0 + j)], 16)

            free = [j for j in range(RAW) if MOE0 + j - RAW < OUT0]
            load_residual(0)
            load_residual(1)
            for j in free:
                wait_used(MOE0 + j - RAW)
                load_expert(0, j)
            for s in range(2, NT):
                load_residual(s)
            for j in range(len(free), UPE):
                if j < RAW:
                    wait_used(MOE0 + j - RAW)
                else:
                    sp.wait_ge(lo_done, j - RAW + 1)
                load_expert(0, j)
            with sp.Fori(1, NE) as e:
                for j in range(UPE):
                    sp.wait_ge(lo_done, e * UPE + (j - RAW + 1))
                    load_expert(e, j)

            sp.wait_ge(scattered, 32 * NE)
            sp.wait_ge(unit_done, UPE * NE)
            sp.dma_start(g_fin[:, :], g_final.partition_broadcast(P)).then_inc(g_fin_loaded, 16)
            for t in range(NT):
                sp.dma_start(y_end[:, t, :], y_rows[t * P:(t + 1) * P, :]).then_inc(y_loaded[t], 16)
            for t in range(NT):
                sp.wait_ge(end_ready, t + 1)
                sp.dma_start(out_tile(t), y_end[:, t, :]).then_inc(stored, 16)
            sp.wait_ge(stored, 16 * NT)
            sp.wait_ge(state_stored, 16)

        @block.scalar
        def _(act):
            steps = [0]

            def link(ins):
                ins.then_inc(act_step, 1)
                steps[0] += 1
                act.wait_ge(act_step, steps[0])

            sources = {"b_mod": b_mod[0], "g_mix": g_norm_mix[0], "g_ffn": g_norm_ffn[0], "c": c[0], "c_ctx": c_ctx,
                       "pool_scale": pool_scale[0], "w_conv": w_conv[0].rearrange("k n -> (k n)"), "b_conv": b_conv[0],
                       "b_gate_a": b_gate_a[0].rearrange("r h i -> (r h i)"),
                       "b_gate_x": b_gate_x[0].rearrange("r h i -> (r h i)"),
                       "lam": lru_lambda[0].rearrange("r n -> (r n)")}
            act.dma_start(ident[:, :], identity).then_inc(ident_loaded, 16)
            for name, (a, b) in ROWS.items():
                act.dma_start(rows_in[a:b, :], sources[name].rearrange("(r n) -> r n", n=P)).then_inc(rows_loaded, 16)
            act.dma_start(rows_st[:, :], state_rglru[0, 0].rearrange("r (k n) -> (r k) n", n=P)).then_inc(rows_loaded, 16)
            for t in range(NT):
                act.dma_start(x_in[:, t, :], x_tile(t)).then_inc(x_loaded[t], 16)

            act.wait_ge(vecs_ready, 2)
            a = ROWS["c"][0]
            act.activation(silu_c[:, :, :], vecs[:, a:a + 16].rearrange("p (s k) -> p k s", s=2), ACT.Silu)\
               .then_inc(silu_ready, 1)
            for t in range(NT):
                act.wait_ge(x_loaded[t], 16)
                act.activation(junk0[:, :], x_in[:, t, :], ACT.Square, accum_out=sumsq[:, 0, t:t + 1]).then_inc(sq_ready, 1)
                act.wait_ge(sq_ready, t + 1)
            link(act.activation(lam_t[:, 0, :], vec("lam"), ACT.Abs))
            act.activation(lam_t[:, 1, :], lam_t[:, 0, :], ACT.Exp, scale=-1.0).then_inc(lam_act, 1)
            act.wait_ge(lam_dve, 1)
            act.activation(lam_t[:, 3, :], lam_t[:, 2, :], ACT.Ln).then_inc(lam_act, 1)

            def bank_parts(j, dst):
                for n in range(3):
                    yield ps[:, 3 * (j % 2) + n, 0:SEG], dst[:, n * SEG:(n + 1) * SEG]

            for job in order:
                if job[0] == "M":
                    continue
                j = JOB[job]
                kind, k = job[0], job[1]
                if kind == "x":
                    if k == 0:
                        act.wait_ge(mod1_ready, 1)
                    act.wait_ge(job_done, j + 1)
                    for n, (a, b, s) in enumerate(((0, 512, 0), (512, N_LAT, 0), (N_LAT, T, 1))):
                        last_i = act.activation(h_t[:, k, a:b], ps[:, 3 * (j % 2) + n, 0:b - a], ACT.Identity,
                                                scale=scale_a[:, k, s:s + 1], bias=mod[:, SHIFT1 + k, s:s + 1])
                    last_i.then_inc(job_read, 1)
                elif kind == "L":
                    if k == 0:
                        act.wait_ge(up_ready, 1)
                    else:
                        act.wait_ge(conv_done, k)
                    act.wait_ge(job_done, j + 1)
                    b = 3 * (j % 2)
                    act.activation(up[:, UL:UL + SEG], ps[:, b, 0:SEG], ACT.Copy)
                    act.activation(up[:, UL + SEG:UL + 2 * SEG], ps[:, b + 1, 0:SEG], ACT.Copy)
                    act.activation(up[:, UL + 2 * SEG:UL + N_LAT], ps[:, b + 2, 0:N_LAT - 2 * SEG], ACT.Copy)
                    act.activation(up[:, UC:UC + N_CTX], ps[:, b + 2, N_LAT - 2 * SEG:SEG], ACT.Copy).then_inc(job_read, 1)
                elif kind == "P":
                    q = POOL_ORDER.index(k)
                    act.wait_ge(pads_ready, 1)
                    if q >= 2:
                        act.wait_ge(pooled, q - 1)
                    act.wait_ge(job_done, j + 1)
                    for n in range(3):
                        rows = (SEG if n < 2 else N_LAT - 2 * SEG) // GRID_W
                        at = n * SEG // GRID_W
                        act.activation(pad_l[:, q % 2, at:at + rows, PAD:PAD + GRID_W],
                                       ps[:, 3 * (j % 2) + n, 0:rows * GRID_W].rearrange("p (r w) -> p r w", w=GRID_W),
                                       ACT.Copy)
                    act.activation(pad_c[:, q % 2, PAD:PAD + N_CTX], ps[:, 3 * (j % 2) + 2, N_LAT - 2 * SEG:SEG],
                                   ACT.Copy).then_inc(job_read, 1)
                elif kind == "E":
                    if k > 0:
                        act.wait_ge(gelu_used, k)
                    else:
                        act.wait_ge(conv_done, LC)
                    act.wait_ge(job_done, j + 1)
                    for src, dst in bank_parts(j, gelu):
                        last_i = act.activation(dst, src, ACT.Gelu_apprx_tanh)
                    last_i.then_inc(job_read, 1)
                elif kind == "G":
                    _, k, r, ax = job
                    d = 2 * k + r
                    m = r * LC + k
                    if ax == 0:
                        if d > 0:
                            act.wait_ge(scan_done, d)
                        act.wait_ge(job_done, j + 1)
                        for src, dst in bank_parts(j, r_a):
                            last_i = act.activation(dst, src, ACT.Sigmoid, bias=vec("b_gate_a")[:, m:m + 1])
                        last_i.then_inc(job_read, 1)
                    else:
                        act.wait_ge(job_done, j + 1)
                        for src, dst in bank_parts(j, i_b):
                            last_i = act.activation(dst, src, ACT.Sigmoid, bias=vec("b_gate_x")[:, m:m + 1])
                        last_i.then_inc(job_read, 1)
                        act.wait_ge(rate_ready, 1)
                        act.wait_ge(job_read, JOB[("G", k, r, 0)] + 1)
                        link(act.activation(tau[:, :], r_a[:, :], ACT.Tanh, scale=rate[:, 0, m:m + 1]))
                        act.activation(r_a[:, :], r_a[:, :], ACT.Exp, scale=rate[:, 1, m:m + 1])
                        act.activation(tau[:, :], tau[:, :], ACT.Sqrt).then_inc(decay_ready, 1)
                elif kind == "O":
                    act.wait_ge(job_done, j + 1)
                    for src, dst in bank_parts(j, y_t[:, k, :]):
                        last_i = act.activation(dst, src, ACT.Copy, scale=vec("pool_scale")[:, k:k + 1])
                    last_i.then_inc(job_read, 1)

            for q in range(16):
                v, s, h = q // 4, q // 2 % 2, q % 2
                dst = bc[:, v, s, :] if v < 3 else g2[:, s, :]
                act.wait_ge(rows_spread, q + 1)
                act.activation(dst[:, 512 * h:512 * h + 512], ps[:, 6 + q % 2, :], ACT.Copy).then_inc(rows_kept, 1)

            for s in range(NT + 1):
                if s < NT:
                    act.wait_ge(x1_ready, s + 1)
                    act.activation(junk1[:, :], x1[:, s % 2, :], ACT.Square, accum_out=sumsq[:, 1, s:s + 1])\
                       .then_inc(sq2_ready, 1)
                if 0 <= s - 1 < NT:
                    t = s - 1
                    act.wait_ge(max_ready, t + 1)
                    act.activation(probs[:, t, :], ps[:, 6, 0:NE], ACT.Exp, bias=logit_max[:, t:t + 1],
                                   accum_out=prob_sum[:, t:t + 1]).then_inc(exp_ready, 1)
                if s < NT:
                    act.wait_ge(rstd2_ready, s + 1)
                    if s >= 2:
                        act.wait_ge(h_stored[s % 2], 16 * (s // 2))
                        act.wait_ge(hn2_turned, s - 1)
                    act.activation(hn2[:, s % 2, :], x1[:, s % 2, :], ACT.Copy, scale=rstd[:, 1, s:s + 1])\
                       .then_inc(xn2_ready, 1)
                    act.wait_ge(hn2_turned, s + 1)
                    if s >= 2:
                        act.wait_ge(logits_done, s - 1)
                    for h in range(2):
                        last_i = act.activation(hn2_t[:, s % 2, 4 * h:4 * h + 4, :],
                                                ps[:, 4 + h, :].rearrange("p (k n) -> p k n", k=4), ACT.Copy)
                    last_i.then_inc(hn2_t_ready, 1)

            def split_high(e, j):
                m = e * UPE + j
                load_base = e * (16 * UPE // RAW)
                act.wait_ge(loaded[slot(MOE0 + j)], load_base + loads(MOE0 + j))
                if not (isinstance(e, int) and e == 0 and j < SPLIT):
                    act.wait_ge(unit_done, m + (1 - SPLIT))
                act.activation(split[:, j % SPLIT, 0, :, :], raw[:, slot(MOE0 + j), :, :], ACT.Copy).then_inc(hi_done, 1)

            def hidden_high(e, k):
                act.wait_ge(mul_done, e * 4 + (k + 1))
                if not (isinstance(e, int) and e == 0):
                    act.wait_ge(unit_done, e * UPE)
                act.activation(hid[:, 2 * k:2 * k + 2, 0, :], hid_f[:, k % 2, :, :], ACT.Copy).then_inc(hid_hi, 1)

            def after_product(e, j):
                if j < 8 and j % 2 == 0:
                    k = j // 2
                    act.wait_ge(psum_read, e * UPE + (j + 1))
                    if not (isinstance(e, int) and e == 0 and k < 2):
                        act.wait_ge(mul_done, e * 4 + (k - 1))
                    act.activation(gate_s[:, k % 2, :, :], gate_f[:, k % 2, :, :], ACT.Silu).then_inc(silu_done, 1)
                    if k > 0:
                        hidden_high(e, k - 1)
                elif j == 7:
                    hidden_high(e, 3)

            def input_high(e):
                act.wait_ge(x_turned, e + 1)
                for h in range(2):
                    act.activation(xt[:, 4 * h:4 * h + 4, 0, 0:CAP_L], ps[:, 6 + h, :].rearrange("p (k n) -> p k n", k=4),
                                   ACT.Copy)
                act.activation(xt[:, :, 0, CAP_L:CAP], ps[:, 0, 0:KC * CAP_C].rearrange("p (k n) -> p k n", k=KC),
                               ACT.Copy).then_inc(xt_hi, 1)

            def expert(e, is_first, is_last):
                for j in range(UPE):
                    if not (is_first and j < LAG):
                        split_high(e, j)
                    if j >= LAG:
                        after_product(e, j - LAG)
                    if j == 7 + LAG and not is_last:
                        input_high(e + 1)

            act.wait_ge(hn2_ready, NT)
            act.wait_ge(mix_done, NT)
            for j in range(LAG):
                split_high(0, j)
            input_high(0)
            expert(0, True, False)
            with act.Fori(1, NE - 1) as e:
                expert(e, False, False)
            expert(NE - 1, False, True)

            for t in range(NT):
                act.wait_ge(y_loaded[t], 16)
                act.activation(junk2[:, :], y_end[:, t, :], ACT.Square, accum_out=sumsq[:, 2, t:t + 1]).then_inc(sq3_ready, 1)
                act.wait_ge(sq3_ready, t + 1)

        @block.gpsimd
        def _(pool):
            steps = [0]

            def link(ins):
                ins.then_inc(pool_step, 1)
                steps[0] += 1
                pool.wait_ge(pool_step, steps[0])

            pool.memset(half[:, :], -0.5).then_inc(half_ready, 1)
            link(pool.memset(spare[:, :], 0.0))
            pool.wait_ge(half_ready, 1)

            def root(norm, t, ready, done):
                pool.wait_ge(ready, t + 1)
                link(pool.tensor_scalar(rstd[:, norm, t:t + 1], sumsq[:, norm, t:t + 1], 1.0 / D, EPS, ALU.mult, ALU.add))
                pool.tensor_tensor(rstd[:, norm, t:t + 1], rstd[:, norm, t:t + 1], half[:, :], ALU.pow).then_inc(done, 1)

            for t in range(NT):
                root(0, t, sq_ready, rstd_ready)

            pool.wait_ge(job_done, KC)
            pool.memset(w_gates[:, :, :, :, :], 0.0).then_inc(pool_step, 1)
            pool.memset(pad_l[:, :, :, :], 0.0).then_inc(pool_step, 1)
            pool.memset(pad_c[:, :, :], 0.0).then_inc(pool_step, 1)
            pool.memset(tall[:, :, :], 0.0).then_inc(pool_step, 1)
            steps[0] += 4
            pool.wait_ge(pool_step, steps[0])
            for ax, w in enumerate((w_gate_a, w_gate_x)):
                for h in range(2):
                    src = w[0].rearrange("r (k h) i j -> h i r k j", h=2)[h]
                    for r in range(2):
                        pool.dma_start(w_gates[64 * h:64 * h + 64, ax, r, :, 64 * h:64 * h + 64], src[:, r, :, :])\
                            .then_inc(small_loaded, 16)
            pool.dma_start(w_p[:, :, :], w_pool[0].rearrange("g c d -> c g d")).then_inc(small_loaded, 16)
            pool.dma_start(inv[:, :, :], inv_count.partition_broadcast(P)).then_inc(small_loaded, 16)
            pool.dma_start(w_r[:, :, :], w_router[0].rearrange("(k p) e -> p k e", p=P)).then_inc(small_loaded, 16)
            pool.nop().then_inc(pads_ready, 1)

            def doubling(g, first, middle, final, take, size):
                spans, a, b = [], 0, size
                for s in range(g, -1, -1):
                    spans.insert(0, (a, b))
                    h = max(1, 2 ** (s - 1))
                    a, b = a - h, b + h
                src = first
                for s, (a, b) in enumerate(spans):
                    left, right = (1, 0) if s == 0 else (2 ** (s - 1), 2 ** (s - 1))
                    dst = final if s == g else take(middle[s % 2], a, b)
                    link(pool.tensor_tensor(dst, take(src, a - left, b - left), take(src, a + right, b + right), ALU.add))
                    src = middle[s % 2]

            def along_row(buf, a, b):
                return buf[:, :, PAD + a:PAD + b]

            def along_column(buf, a, b):
                return buf[:, PAD + a:PAD + b, :]

            def along_line(buf, a, b):
                return buf[:, PAD + a:PAD + b]

            wide = [b[:, 0:GRID_H * PW].rearrange("p (r w) -> p r w", w=PW) for b in box]
            high = [b[:, :].rearrange("p (r w) -> p r w", w=GRID_W) for b in box]
            for q, g in enumerate(POOL_ORDER):
                if q > 0:
                    pool.wait_ge(pooled, q)
                pool.wait_ge(job_read, JOB[("P", g)] + 1)
                doubling(g, pad_c[:, q % 2, :], box_c, along_line(box_c[g % 2], 0, N_CTX), along_line, N_CTX)
                doubling(g, pad_l[:, q % 2, :, :], wide, tall[:, PAD:PAD + GRID_H, :], along_row, GRID_W)
                doubling(g, tall, high, along_column(high[g % 2], 0, GRID_H), along_column, GRID_H)
                pool.nop().then_inc(box_ready, 1)

            pool.wait_ge(state_kept, 1)
            pool.dma_start(new_state[0, 0].rearrange("r (k n) -> (r k) n", n=P), st_rows[:, :])\
                .then_inc(state_stored, 16)

            for s in range(NT):
                t = TILES[s]
                pool.wait_ge(x1_ready, s + 1)
                pool.dma_start(y_rows[t * P:(t + 1) * P, :], x1[:, s % 2, :]).then_inc(y_stored[s % 2], 16)
                root(1, s, sq2_ready, rstd2_ready)
                pool.wait_ge(hn2_ready, s + 1)
                pool.dma_start(h_rows[t * P:(t + 1) * P, :], hn2[:, s % 2, :]).then_inc(h_stored[s % 2], 16)
            pool.wait_ge(h_stored[0], 16 * ((NT + 1) // 2))
            pool.wait_ge(h_stored[1], 16 * (NT // 2))
            pool.wait_ge(y_stored[0], 16 * ((NT + 1) // 2))
            pool.wait_ge(y_stored[1], 16 * (NT // 2))
            pool.wait_ge(routed, 4)

            def pause(before):
                if not (isinstance(before, int) and before == 0):
                    pool.wait_ge(paused, before)
                pool.tensor_tensor(spare[:, 1:2], spare[:, 0:1], spare[:, 0:1], ALU.add).then_inc(paused, 1)

            def gather(e, paused_before):
                if not (isinstance(e, int) and e == 0):
                    pool.wait_ge(x_turned, e)
                pool.wait_ge(gi_ready, e + 1)
                pause(paused_before)
                pool.indirect_dma_start(x_l[:, :], None, h_rows, bass.IndirectOffsetOnAxis(ap=gi_lat[:, :], axis=0))\
                    .then_inc(gathered, 16)
                pool.indirect_dma_start(x_c[:, :], None, h_rows, bass.IndirectOffsetOnAxis(ap=gi_ctx[:, :], axis=0))\
                    .then_inc(gathered, 16)

            def scatter(e, paused_before):
                pool.wait_ge(out_scaled, e + 1)
                pause(paused_before)
                pool.indirect_dma_start(y_rows, bass.IndirectOffsetOnAxis(ap=si_lat[:, :], axis=0), o_l[:, :], None,
                                        compute_op=ALU.add).then_inc(scattered, 16)
                pool.indirect_dma_start(y_rows, bass.IndirectOffsetOnAxis(ap=si_ctx[:, :], axis=0), o_c[:, :], None,
                                        compute_op=ALU.add).then_inc(scattered, 16)
                pool.wait_ge(scattered, e * 32 + 32)

            gather(0, 0)
            gather(1, 1)
            with pool.Fori(1, NE - 1) as e:
                scatter(e - 1, 2 * e)
                gather(e + 1, 2 * e + 1)
            scatter(NE - 2, 2 * NE - 2)
            scatter(NE - 1, 2 * NE - 1)
            for t in range(NT):
                root(2, t, sq3_ready, rstd3_ready)

        @block.vector
        def _(dve):
            steps = [0]

            def link(ins):
                ins.then_inc(dve_step, 1)
                steps[0] += 1
                dve.wait_ge(dve_step, steps[0])

            dve.memset(ones[:, :], 1.0).then_inc(ones_ready, 1)
            dve.wait_ge(vecs_turned, 2)
            dve.tensor_copy(vecs[:, :], ps[:, 7, 0:P]).then_inc(vecs_ready, 1)
            dve.tensor_copy(states[:, :], ps[:, 7, P:P + 8]).then_inc(vecs_ready, 1)
            dve.wait_ge(vecs_ready, 2)
            for t in range(NT):
                dve.wait_ge(rstd_ready, t + 1)
                dve.tensor_scalar(x_in[:, t, :], x_in[:, t, :], rstd[:, 0, t:t + 1], None, ALU.mult).then_inc(xn_ready, 1)

            dve.wait_ge(lam_act, 1)
            dve.tensor_scalar(lam_t[:, 2, :], lam_t[:, 1, :], 1.0, None, ALU.add).then_inc(lam_dve, 1)
            dve.wait_ge(lam_dve, 1)
            link(dve.tensor_scalar(lam_t[:, 4, :], lam_t[:, 2, :], -1.0, None, ALU.add))
            link(dve.tensor_scalar(lam_t[:, 5, :], lam_t[:, 4, :], 0.0, None, ALU.is_equal))
            link(dve.tensor_tensor(lam_t[:, 4, :], lam_t[:, 4, :], lam_t[:, 5, :], ALU.add))
            link(dve.reciprocal(lam_t[:, 4, :], lam_t[:, 4, :]))
            dve.wait_ge(lam_act, 2)
            link(dve.tensor_tensor(lam_t[:, 3, :], lam_t[:, 3, :], lam_t[:, 5, :], ALU.add))
            link(dve.tensor_tensor(lam_t[:, 3, :], lam_t[:, 3, :], lam_t[:, 4, :], ALU.mult))
            link(dve.tensor_tensor(lam_t[:, 3, :], lam_t[:, 3, :], lam_t[:, 1, :], ALU.mult))
            link(dve.tensor_scalar(lam_t[:, 0, :], vec("lam"), -1.0, 0.0, ALU.mult, ALU.max))
            link(dve.tensor_tensor(lam_t[:, 0, :], lam_t[:, 0, :], lam_t[:, 3, :], ALU.add))
            link(dve.tensor_scalar(rate[:, 0, :], lam_t[:, 0, :], 4.0, None, ALU.mult))
            dve.tensor_scalar(rate[:, 1, :], lam_t[:, 0, :], -8.0, None, ALU.mult).then_inc(rate_ready, 1)

            def add_bias(a, b):
                v = vecs[:, a:b].unsqueeze(2).broadcast_to([P, b - a, 2])
                link(dve.tensor_tensor(mod[:, a:b, :], ps[:, 6, 2 * a:2 * b].rearrange("p (k s) -> p k s", s=2), v, ALU.add))

            def one_plus_scale(a, g):
                return dve.scalar_tensor_tensor(out=scale_a[:, :, :], in0=mod[:, a:a + KC, :], scalar=1.0,
                                                in1=vec(g).unsqueeze(2).broadcast_to([P, KC, 2]),
                                                op0=ALU.add, op1=ALU.mult)

            for u in range(0, NMOD1, 2):
                dve.wait_ge(mods_done, u + 2)
                dve.tensor_copy(mod_rows[:, u * UW:(u + 2) * UW], ps[0:2, u // 2, :]).then_inc(mod_rows_ready, 1)
            dve.wait_ge(mod1_turned, 1)
            add_bias(0, 2 * NMOD1)
            one_plus_scale(SCALE1, "g_mix").then_inc(mod1_ready, 1)

            SEQS = ((UL, 0, N_LAT), (UC, N_LAT, N_CTX))

            def conv(k):
                w0 = ROWS["w_conv"][0]
                dve.wait_ge(job_read, JOB[("L", k)] + 1)
                if k >= 2:
                    dve.wait_ge(job_done, JOB[("G", k - 2, 1, 1)] + 1)
                for o, a, n in SEQS:
                    u = up[:, o - 2:o - 2 + n]
                    link(dve.tensor_scalar(xc[:, k % 2, a:a + n], u, vecs[:, w0 + k:w0 + k + 1],
                                           vec("b_conv")[:, k:k + 1], ALU.mult, ALU.add))
                for tap in range(1, CONV_W):
                    for i, (o, a, n) in enumerate(SEQS):
                        u = up[:, o - 2 + tap:o - 2 + tap + n]
                        ins = dve.scalar_tensor_tensor(out=xc[:, k % 2, a:a + n], in0=u,
                                                       scalar=vecs[:, w0 + LC * tap + k:w0 + LC * tap + k + 1],
                                                       in1=xc[:, k % 2, a:a + n], op0=ALU.mult, op1=ALU.add)
                        if tap == CONV_W - 1 and i == 1:
                            ins.then_inc(conv_done, 1)
                        elif i == 1:
                            link(ins)

            def scan(k, r):
                d = 2 * k + r
                m = r * LC + k
                dve.wait_ge(decay_ready, d + 1)
                link(dve.tensor_tensor(i_b[:, :], i_b[:, :], xc[:, k % 2, :], ALU.mult))
                link(dve.scalar_tensor_tensor(out=tau[:, :], in0=r_a[:, :], scalar=1.0, in1=tau[:, :],
                                              op0=ALU.add, op1=ALU.mult))
                link(dve.tensor_tensor(i_b[:, :], i_b[:, :], tau[:, :], ALU.mult))
                dst = y_t[:, LC + k, :] if r == 0 else tau[:, :]
                for n, (a, b) in enumerate(((0, N_LAT), (N_LAT, T))):
                    def run(x):
                        x = x[:, a:b]
                        return x if r == 0 else x[:, ::-1]
                    start = states[:, m:m + 1] if n == 0 else 0.0
                    link(dve.tensor_tensor_scan(run(dst), run(r_a[:, :]), run(i_b[:, :]), start, ALU.mult, ALU.add))
                end = T - 1 if r == 0 else N_LAT
                link(dve.tensor_copy(st_out[:, m:m + 1], dst[:, end:end + 1]))
                if r == 1:
                    dve.tensor_tensor(y_t[:, LC + k, :], y_t[:, LC + k, :], tau[:, :], ALU.add).then_inc(scan_done, 1)
                    dve.wait_ge(scan_done, d + 1)
                else:
                    dve.nop().then_inc(scan_done, 1)

            def pooling(g):
                q = POOL_ORDER.index(g)
                dve.wait_ge(small_loaded, SMALL)
                dve.wait_ge(box_ready, q + 1)
                d = y_t[:, g, 0:N_LAT].rearrange("p (r w) -> p r w", w=GRID_W)
                s = box[g % 2][:, PAD * GRID_W:(PAD + GRID_H) * GRID_W].rearrange("p (r w) -> p r w", w=GRID_W)
                by_col = inv[:, g, 0:GRID_W].unsqueeze(1).broadcast_to([P, GRID_H, GRID_W])
                by_row = inv[:, g, GRID_W:GRID_W + GRID_H].unsqueeze(2).broadcast_to([P, GRID_H, GRID_W])
                link(dve.tensor_tensor(d, s, by_col, ALU.mult))
                link(dve.tensor_tensor(d, d, by_row, ALU.mult))
                link(dve.tensor_tensor(d, d, pad_l[:, q % 2, :, PAD:PAD + GRID_W], ALU.subtract))
                dc = y_t[:, g, N_LAT:T]
                link(dve.tensor_tensor(dc, box_c[g % 2][:, PAD:PAD + N_CTX], inv[:, g, GRID_W + GRID_H:NI], ALU.mult))
                dve.tensor_tensor(dc, dc, pad_c[:, q % 2, PAD:PAD + N_CTX], ALU.subtract).then_inc(pooled, 1)

            def gated(k):
                dve.wait_ge(job_read, JOB[("E", k)] + 1)
                dve.tensor_tensor(y_t[:, LC + k, :], y_t[:, LC + k, :], gelu[:, 0:T], ALU.mult).then_inc(gelu_used, 1)

            def modulate(u):
                n = UNIT[("mod", NMOD1 + u)]
                dve.wait_ge(loaded[slot(n)], loads(n))
                if u >= 2:
                    dve.wait_ge(mods_done, NMOD1 + u - 1)
                for k in range(KC):
                    for s in range(2):
                        w, dst = raw[:, slot(n), k, :], part[:, u % 2, s, :]
                        if k == 0:
                            ins = dve.tensor_scalar(dst, w, silu_c[:, k, s:s + 1], None, ALU.mult)
                        else:
                            dve.wait_ge(dve_step, steps[0] - 1)
                            ins = dve.scalar_tensor_tensor(out=dst, in0=w, scalar=silu_c[:, k, s:s + 1], in1=dst,
                                                           op0=ALU.mult, op1=ALU.add)
                        if k == KC - 1 and s == 1:
                            dve.wait_ge(dve_step, steps[0])
                            ins.then_inc(part_ready, 1)
                        else:
                            ins.then_inc(dve_step, 1)
                            steps[0] += 1

            modulate(0)
            modulate(1)
            dve.wait_ge(job_done, KC)
            link(dve.memset(up[:, 0:UL], 0.0))
            link(dve.memset(up[:, UL + N_LAT:UC], 0.0))
            dve.memset(up[:, UC + N_CTX:T + 6], 0.0).then_inc(up_ready, 1)
            conv(0)
            modulate(2)
            modulate(3)
            conv(1)
            scan(0, 0)
            modulate(4)
            scan(0, 1)
            modulate(5)
            scan(1, 0)
            pooling(3)
            modulate(6)
            conv(2)
            scan(1, 1)
            modulate(7)
            conv(3)
            scan(2, 0)
            modulate(8)
            pooling(2)
            scan(2, 1)
            modulate(9)
            scan(3, 0)
            pooling(1)
            modulate(10)
            gated(0)
            scan(3, 1)
            pooling(0)
            modulate(11)
            gated(1)
            modulate(12)
            modulate(13)
            gated(2)
            modulate(14)
            modulate(15)
            gated(3)
            dve.wait_ge(state_turned, 1)
            dve.tensor_copy(st_rows[:, :], ps[0:8, 7, 0:P]).then_inc(state_kept, 1)

            dve.wait_ge(mods_done, NMOD1 + NMOD2)
            add_bias(2 * NMOD1, 48)
            link(one_plus_scale(SCALE2, "g_ffn"))
            dve.nop().then_inc(mod2_ready, 1)
            dve.wait_ge(pooled, NG)
            for q in range(16):
                v, s, h = q // 4, q // 2 % 2, q % 2
                src = (mod[:, GATE1:GATE1 + KC, s], scale_a[:, :, s], mod[:, SHIFT2:SHIFT2 + KC, s],
                       mod[:, GATE2:GATE2 + KC, s])[v]
                if q >= 2:
                    dve.wait_ge(rows_spread, q - 1)
                dve.tensor_tensor(box[q % 2][:, 0:512].rearrange("p (k n) -> p k n", k=4),
                                  ident[:, :].unsqueeze(1).broadcast_to([P, 4, P]),
                                  src[:, 4 * h:4 * h + 4].unsqueeze(2).broadcast_to([P, 4, P]), ALU.mult)\
                   .then_inc(diag_ready, 1)

            dve.wait_ge(rows_kept, 16)
            def top_round(aff, work, best, index, n, rounds):
                src = aff if n == 0 else work[(n - 1) % 2]
                link(dve.max(best[:, 8 * n:8 * n + 8], src))
                ins = dve.max_index(index[:, 8 * n:8 * n + 8], best[:, 8 * n:8 * n + 8], src)
                if n < rounds - 1:
                    link(dve.match_replace(work[n % 2], best[:, 8 * n:8 * n + 8], src, -1.0))
                else:
                    link(ins)

            FIRST = CAP_L // 8
            first_done = [0]

            def first_rounds(n):
                for m in range(first_done[0], min(first_done[0] + n, FIRST)):
                    top_round(aff_a[:, :], [w[:, :] for w in aff_w], top_a, top_ai, m, FIRST)
                    first_done[0] += 1

            def softmax_max(t):
                dve.wait_ge(logits_done, t + 1)
                dve.tensor_reduce(logit_max[:, t:t + 1], ps[:, 6, 0:NE], AX.X, ALU.max, negate=True).then_inc(max_ready, 1)

            def softmax_rows(t):
                dve.wait_ge(exp_ready, t + 1)
                link(dve.reciprocal(prob_inv[:, t:t + 1], prob_sum[:, t:t + 1]))
                dve.tensor_scalar(probs[:, t, :], probs[:, t, :], prob_inv[:, t:t + 1], None, ALU.mult)\
                   .then_inc(probs_ready, 1)

            def affinities(t):
                dve.wait_ge(probs_turned, t + 1)
                a = TILES[t] * P
                dst = (aff_c[:, :] if TILES[t] == CTX_TILE else aff_a[:, a:a + P] if TILES[t] < TILES_A else
                       aff_b[:, a - TILES_A * P:a - TILES_A * P + P])
                dve.tensor_copy(dst, ps[0:NE, 7, 0:P]).then_inc(aff_ready, 1)
                dve.wait_ge(aff_ready, t + 1)

            for s in range(NT + 1):
                if s < NT:
                    t = TILES[s]
                    dve.wait_ge(res_loaded[s % 2], 16 * (s // 2 + 1))
                    if s >= 2:
                        dve.wait_ge(y_stored[s % 2], 16 * (s // 2))
                        dve.wait_ge(xn2_ready, s - 1)
                    dve.wait_ge(mix_done, s + 1)
                    b = 2 * (s % 2)
                    dve.tensor_tensor(x1[:, s % 2, :], ps[:, b:b + 2, :].rearrange("p b n -> p (b n)"),
                                      bc[:, 0, stream(t), :], ALU.mult).then_inc(mix_read, 1)
                    dve.wait_ge(mix_read, s + 1)
                    dve.tensor_tensor(x1[:, s % 2, :], x1[:, s % 2, :], x_res[:, s % 2, :], ALU.add).then_inc(x1_ready, 1)
                if s >= 1:
                    softmax_max(s - 1)
                if TILES_A < s < NT:
                    first_rounds(1)
                if s >= 1:
                    softmax_rows(s - 1)
                if s < NT:
                    dve.wait_ge(xn2_ready, s + 1)
                    link(dve.tensor_tensor(hn2[:, s % 2, :], hn2[:, s % 2, :], bc[:, 1, stream(t), :], ALU.mult))
                    dve.tensor_tensor(hn2[:, s % 2, :], hn2[:, s % 2, :], bc[:, 2, stream(t), :], ALU.add)\
                       .then_inc(hn2_ready, 1)
                if s >= 1:
                    affinities(s - 1)
                if s >= TILES_A:
                    first_rounds(3)
            first_rounds(FIRST)
            for n in range(FIRST):
                top_round(aff_b[:, :], [w[:, 0:N_LAT - TILES_A * P] for w in aff_w], top_b, top_bi, n, FIRST)
            for n in range(CAP_C // 8):
                top_round(aff_c[:, :], [w[:, 0:N_CTX] for w in aff_w], top_c, top_ci, n, CAP_C // 8)
            dve.tensor_copy(top_af[:, :], top_ai[:, :]).then_inc(top_ready, 1)
            dve.tensor_copy(rev_b[:, :], top_b[:, ::-1]).then_inc(top_ready, 1)
            link(dve.tensor_copy(rev_bf[:, :], top_bi[:, ::-1]))
            dve.tensor_scalar(rev_bf[:, :], rev_bf[:, :], float(TILES_A * P), None, ALU.add).then_inc(top_ready, 1)
            link(dve.tensor_copy(top_cf[:, :], top_ci[:, :]))
            dve.tensor_scalar(top_cf[:, :], top_cf[:, :], float(N_LAT), None, ALU.add).then_inc(top_ready, 1)
            dve.wait_ge(top_turned, 6)
            link(dve.tensor_copy(pair[:, :, :], ps[:, 4, 0:4 * NE].rearrange("p (n e) -> p n e", n=4)))
            dve.tensor_tensor(g_lat[:, :], pair[:, 0, :], pair[:, 2, :], ALU.max).then_inc(routed, 1)
            dve.tensor_tensor(pair_d[:, 0, :], pair[:, 0, :], pair[:, 2, :], ALU.is_ge).then_inc(dve_step, 1)
            dve.tensor_tensor(pair_d[:, 1, :], pair[:, 1, :], pair[:, 3, :], ALU.subtract).then_inc(dve_step, 1)
            steps[0] += 2
            dve.wait_ge(dve_step, steps[0])
            link(dve.tensor_tensor(pair_d[:, 0, :], pair_d[:, 0, :], pair_d[:, 1, :], ALU.mult))
            link(dve.tensor_tensor(pair_d[:, 0, :], pair_d[:, 0, :], pair[:, 3, :], ALU.add))
            dve.tensor_copy(i_lat[:, :], pair_d[:, 0, :]).then_inc(routed, 1)
            dve.tensor_copy(g_ctx[:, :], ps[0:CAP_C, 5, 0:NE]).then_inc(routed, 1)
            dve.tensor_copy(i_ctx[:, :], ps[0:CAP_C, 5, NE:2 * NE]).then_inc(routed, 1)
            dve.wait_ge(routed, 4)

            def column(x, e):
                return x[:, e:e + 1] if isinstance(e, int) else x[:, bass.ds(e, 1)]

            def gather_index(e):
                dve.wait_ge(routed, 4)
                dve.tensor_copy(gi_lat[:, :], column(i_lat, e))
                dve.tensor_copy(gi_ctx[:, :], column(i_ctx, e)).then_inc(gi_ready, 1)

            def split_low(e, j):
                dve.wait_ge(hi_done, e * UPE + (j + 1))
                dve.tensor_tensor(split[:, j % SPLIT, 1, :, :], raw[:, slot(MOE0 + j), :, :],
                                  split[:, j % SPLIT, 0, :, :].bitcast(f32), ALU.subtract).then_inc(lo_done, 1)

            def hidden_low(e, k):
                dve.wait_ge(hid_hi, e * 4 + (k + 1))
                dve.tensor_tensor(hid[:, 2 * k:2 * k + 2, 1, :], hid_f[:, k % 2, :, :],
                                  hid[:, 2 * k:2 * k + 2, 0, :].bitcast(f32), ALU.subtract).then_inc(hid_lo, 1)

            def after_product(e, j):
                if j < 8 and j % 2 and not (isinstance(e, int) and e == 0 and j == 1):
                    dve.wait_ge(mul_done, e * 4 + j // 2)
                dve.wait_ge(unit_done, e * UPE + (j + 1))
                k = j // 2 if j < 8 else j - 8
                dst = down[:, 2 * k:2 * k + 2, :] if j >= 8 else up_f[:, :, :] if j % 2 else gate_f[:, k % 2, :, :]
                b = 2 * (j % 3)
                dve.tensor_reduce(dst, ps[:, b:b + 2, 0:2 * CAP].rearrange("p c (h n) -> p c n h", h=2), AX.X, ALU.add)\
                   .then_inc(psum_read, 1)
                if j < 8 and j % 2:
                    if k > 0:
                        hidden_low(e, k - 1)
                    dve.wait_ge(silu_done, e * 4 + (k + 1))
                    dve.wait_ge(psum_read, e * UPE + (j + 1))
                    dve.tensor_tensor(hid_f[:, k % 2, :, :], up_f[:, :, :], gate_s[:, k % 2, :, :], ALU.mult)\
                       .then_inc(mul_done, 1)
                    if k == 3:
                        hidden_low(e, 3)

            def input_low(e):
                dve.wait_ge(xt_hi, e + 1)
                for h in range(2):
                    dve.tensor_tensor(xt[:, 4 * h:4 * h + 4, 1, 0:CAP_L], ps[:, 6 + h, :].rearrange("p (k n) -> p k n", k=4),
                                      xt[:, 4 * h:4 * h + 4, 0, 0:CAP_L].bitcast(f32), ALU.subtract)
                dve.tensor_tensor(xt[:, :, 1, CAP_L:CAP], ps[:, 0, 0:KC * CAP_C].rearrange("p (k n) -> p k n", k=KC),
                                  xt[:, :, 0, CAP_L:CAP].bitcast(f32), ALU.subtract).then_inc(xt_lo, 1)

            def scatter_index(e):
                dve.wait_ge(routed, 4)
                dve.tensor_copy(si_lat[:, :], column(i_lat, e))
                dve.tensor_copy(si_ctx[:, :], column(i_ctx, e))
                dve.tensor_copy(sg_lat[:, :], column(g_lat, e))
                dve.tensor_copy(sg_ctx[:, :], column(g_ctx, e)).then_inc(si_ready, 1)

            def scale_rows(e):
                dve.wait_ge(si_ready, e + 1)
                dve.wait_ge(rows_turned, e + 1)
                for h in range(2):
                    a, b = 512 * h, 512 * h + 512
                    ins = dve.scalar_tensor_tensor(out=o_c[:, a:b], in0=ps[0:CAP_C, 4 + h, :], scalar=sg_ctx[:, 0:1],
                                                   in1=g2[0:CAP_C, 1, a:b], op0=ALU.mult, op1=ALU.mult)
                ins.then_inc(ctx_scaled, 1)
                for h in range(2):
                    a, b = 512 * h, 512 * h + 512
                    ins = dve.scalar_tensor_tensor(out=o_l[:, a:b], in0=ps[:, 6 + h, :], scalar=sg_lat[:, 0:1],
                                                   in1=g2[:, 0, a:b], op0=ALU.mult, op1=ALU.mult)
                ins.then_inc(out_scaled, 1)

            def expert(e, is_first, is_last):
                for j in range(UPE):
                    if j == 1 and not is_last:
                        gather_index(e + 1)
                    if j == 1 and not is_first:
                        scatter_index(e - 1)
                    if j == UPE - 1 and not is_first:
                        dve.wait_ge(scattered, e * 32)
                    if j >= LAG:
                        after_product(e, j - LAG)
                    elif not is_first:
                        after_product(e - 1, j - LAG + UPE)
                    if not (is_first and j < LAG):
                        split_low(e, j)
                    if j == LAG and not is_first:
                        scale_rows(e - 1)
                    if j == 7 + LAG and not is_last:
                        input_low(e + 1)

            gather_index(0)
            for j in range(LAG):
                split_low(0, j)
            input_low(0)
            expert(0, True, False)
            with dve.Fori(1, NE - 1) as e:
                expert(e, False, False)
            expert(NE - 1, False, True)
            for j in range(UPE - LAG, UPE):
                after_product(NE - 1, j)
            scatter_index(NE - 1)
            scale_rows(NE - 1)

            dve.wait_ge(g_fin_loaded, 16)
            for t in range(NT):
                dve.wait_ge(rstd3_ready, t + 1)
                dve.scalar_tensor_tensor(out=y_end[:, t, :], in0=y_end[:, t, :], scalar=rstd[:, 2, t:t + 1],
                                         in1=g_fin[:, :], op0=ALU.mult, op1=ALU.mult).then_inc(end_ready, 1)

        @block.tensor
        def _(pe):
            pe.wait_ge(ident_loaded, 16)
            pe.wait_ge(rows_loaded, 16 * (len(ROWS) + 1))
            pe.transpose(ps[:, 7, 0:P], rows_in[:, :], ident[:, :]).then_inc(vecs_turned, 1)
            pe.transpose(ps[:, 7, P:P + 8], rows_st[:, :], ident[0:8, 0:8]).then_inc(vecs_turned, 1)

            pe.wait_ge(silu_ready, 1)
            for u in range(NMOD1):
                n = UNIT[("mod", u)]
                pe.wait_ge(loaded[slot(n)], loads(n))
                for k in range(KC):
                    ins = pe.matmul(ps[0:2, u // 2, (u % 2) * UW:(u % 2 + 1) * UW], silu_c[:, k, :], raw[:, slot(n), k, :],
                                    start=(k == 0), stop=(k == KC - 1))
                ins.then_inc(mods_done, 1)
            for ch in range(2 * NMOD1):
                pe.wait_ge(mod_rows_ready, ch // 4 + 1)
                ins = pe.transpose(ps[:, 6, 2 * ch:2 * ch + 2], mod_rows[:, ch * P:(ch + 1) * P], ident[0:2, 0:2])
            ins.then_inc(mod1_turned, 1)

            def modulate(u):
                pe.wait_ge(part_ready, u + 1)
                for i in range(2):
                    for s in range(2):
                        col = 2 * (2 * (NMOD1 + u) + i) + s
                        ins = pe.matmul(ps[:, 6, col:col + 1], part[:, u % 2, s, i * P:(i + 1) * P], ones[:, 0:1],
                                        start=True, stop=True)
                ins.then_inc(mods_done, 1)

            for job in order:
                if job[0] == "M":
                    if job[1] == 1:
                        pe.wait_ge(mod1_ready, 1)
                        pe.wait_ge(ones_ready, 1)
                    if job[1] > 0:
                        modulate(job[1] - 1)
                    continue
                j = JOB[job]
                b = 3 * (j % 2)
                if j >= 2:
                    pe.wait_ge(job_read, j - 1)
                kind, k = job[0], job[1]
                if kind == "x":
                    if k == 0:
                        pe.wait_ge(xn_ready, NT)
                    for t in range(NT):
                        ins = pe.transpose(ps[:, b + t // 4, (t % 4) * P:(t % 4 + 1) * P], x_in[:, t, k * P:(k + 1) * P],
                                           ident[:, :])
                    ins.then_inc(job_done, 1)
                elif kind in IN_CHUNK:
                    ch = IN_CHUNK[kind] + k
                    n = UNIT[("in", ch // 2)]
                    if job == ("L", 0):
                        pe.wait_ge(job_read, KC)
                    pe.wait_ge(loaded[slot(n)], loads(n))
                    for kk in range(KC):
                        for seg in range(3):
                            ins = pe.matmul(ps[:, b + seg, 0:SEG], raw[:, slot(n), kk, (ch % 2) * P:(ch % 2 + 1) * P],
                                            h_t[:, kk, seg * SEG:(seg + 1) * SEG], start=(kk == 0), stop=(kk == KC - 1))
                    ins.then_inc(job_done, 1)
                elif kind == "G":
                    _, k, r, ax = job
                    pe.wait_ge(small_loaded, SMALL)
                    pe.wait_ge(conv_done, k + 1)
                    for seg in range(3):
                        ins = pe.matmul(ps[:, b + seg, 0:SEG], w_gates[:, ax, r, k, :],
                                        xc[:, k % 2, seg * SEG:(seg + 1) * SEG], start=True, stop=True)
                    ins.then_inc(job_done, 1)
                else:
                    pe.wait_ge(pooled, POOL_ORDER.index(k) + 1)
                    for seg in range(3):
                        ins = pe.matmul(ps[:, b + seg, 0:SEG], w_p[:, k, :], y_t[:, k, seg * SEG:(seg + 1) * SEG],
                                        start=True, stop=True)
                    ins.then_inc(job_done, 1)
            modulate(NMOD2 - 1)
            pe.wait_ge(scan_done, 2 * LC)
            pe.transpose(ps[0:8, 7, 0:P], st_out[:, :], ident[:, :]).then_inc(state_turned, 1)

            pe.wait_ge(mod2_ready, 1)
            pe.wait_ge(state_kept, 1)
            pe.wait_ge(ones_ready, 1)
            for q in range(16):
                pe.wait_ge(diag_ready, q + 1)
                if q >= 2:
                    pe.wait_ge(rows_kept, q - 1)
                pe.matmul(ps[:, 6 + q % 2, :], ones[:, :], box[q % 2][:, 0:512], start=True, stop=True)\
                  .then_inc(rows_spread, 1)

            pe.wait_ge(job_read, NJOBS)
            pe.wait_ge(gelu_used, LC)
            pe.wait_ge(rows_kept, 16)
            for u in range(D // UW):
                pe.wait_ge(loaded[slot(OUT0 + u)], loads(OUT0 + u))
            def out_product(s, u):
                t = TILES[s]
                for k in range(KC):
                    ins = pe.matmul(ps[:, 2 * (s % 2) + u // 2, (u % 2) * UW:(u % 2 + 1) * UW],
                                    y_t[:, k, t * P:(t + 1) * P], raw[:, slot(OUT0 + u), k, :],
                                    start=(k == 0), stop=(k == KC - 1))
                if u == D // UW - 1:
                    ins.then_inc(mix_done, 1)

            for s in range(NT + 2):
                if s < NT:
                    if s >= 2:
                        pe.wait_ge(mix_read, s - 1)
                    for u in range(D // UW - 1):
                        out_product(s, u)
                if 0 <= s - 2 < NT:
                    t = s - 2
                    pe.wait_ge(probs_ready, t + 1)
                    if t >= 1:
                        pe.wait_ge(aff_ready, t)
                    pe.transpose(ps[0:NE, 7, 0:P], probs[:, t, :], ident[:, :]).then_inc(probs_turned, 1)
                if 0 <= s - 1 < NT:
                    t = s - 1
                    pe.wait_ge(hn2_ready, t + 1)
                    if t >= 1:
                        pe.wait_ge(hn2_t_ready, t)
                    for k in range(KC):
                        ins = pe.transpose(ps[:, 4 + k // 4, (k % 4) * P:(k % 4 + 1) * P], hn2[:, t % 2, k * P:(k + 1) * P],
                                           ident[:, :])
                    ins.then_inc(hn2_turned, 1)
                if s < NT:
                    out_product(s, D // UW - 1)
                if 0 <= s - 1 < NT:
                    t = s - 1
                    pe.wait_ge(hn2_t_ready, t + 1)
                    if t >= 1:
                        pe.wait_ge(exp_ready, t)
                    for k in range(KC):
                        ins = pe.matmul(ps[:, 6, 0:NE], hn2_t[:, t % 2, k, :], w_r[:, k, :],
                                        start=(k == 0), stop=(k == KC - 1))
                    ins.then_inc(logits_done, 1)

            pe.wait_ge(top_ready, 4)
            for n, best in enumerate((top_a, top_af, rev_b, rev_bf)):
                pe.transpose(ps[:, 4, n * NE:(n + 1) * NE], best[:, :], ident[0:NE, 0:NE]).then_inc(top_turned, 1)
            for n, best in enumerate((top_c, top_cf)):
                pe.transpose(ps[0:CAP_C, 5, n * NE:(n + 1) * NE], best[:, :], ident[0:NE, 0:NE]).then_inc(top_turned, 1)

            def turn_input(e):
                pe.wait_ge(gathered, e * 32 + 32)
                if not (isinstance(e, int) and e == 0):
                    pe.wait_ge(psum_read, e * UPE - 5)
                    if not (isinstance(e, int) and e == 1):
                        pe.wait_ge(out_scaled, e - 1)
                for k in range(KC):
                    pe.transpose(ps[:, 6 + k // 4, (k % 4) * P:(k % 4 + 1) * P], x_l[:, k * P:(k + 1) * P], ident[:, :])
                for k in range(KC):
                    ins = pe.transpose(ps[:, 0, k * CAP_C:(k + 1) * CAP_C], x_c[:, k * P:(k + 1) * P],
                                       ident[0:CAP_C, 0:CAP_C])
                ins.then_inc(x_turned, 1)

            def turn_rows(e):
                pe.wait_ge(psum_read, e * UPE + UPE)
                if isinstance(e, int) and e == NE - 1:
                    pe.wait_ge(out_scaled, e)
                else:
                    pe.wait_ge(xt_lo, e + 2)
                for k in range(KC):
                    pe.transpose(ps[:, 6 + k // 4, (k % 4) * P:(k % 4 + 1) * P], down[:, k, 0:CAP_L], ident[:, :])
                for k in range(KC):
                    ins = pe.transpose(ps[0:CAP_C, 4 + k // 4, (k % 4) * P:(k % 4 + 1) * P], down[:, k, CAP_L:CAP],
                                       ident[:, :])
                ins.then_inc(rows_turned, 1)

            def product(e, j, is_last):
                pe.wait_ge(lo_done, e * UPE + (j + 1))
                some = not (isinstance(e, int) and e == 0)
                if some or j >= 3:
                    pe.wait_ge(psum_read, e * UPE + (j - 2))
                if j == 0:
                    pe.wait_ge(xt_lo, e + 1)
                if j == 2 and some:
                    pe.wait_ge(ctx_scaled, e)
                if j == 8:
                    pe.wait_ge(hid_lo, e * 4 + 3)
                if j == 9 and not is_last:
                    pe.wait_ge(xt_lo, e + 2)
                src = xt if j < 8 else hid
                for i in range(2):
                    out = ps[:, 2 * (j % 3) + i, :]
                    for c in range(KC):
                        if j == 8 and i == 0 and c == KC - 2:
                            pe.wait_ge(hid_lo, e * 4 + 4)
                        pe.matmul(out[:, 0:2 * CAP], split[:, j % SPLIT, 0, c, i * P:(i + 1) * P],
                                  src[:, c, :, :].rearrange("p h n -> p (h n)"), start=(c == 0), stop=False)
                        ins = pe.matmul(out[:, 0:CAP], split[:, j % SPLIT, 1, c, i * P:(i + 1) * P], src[:, c, 0, :],
                                        start=False, stop=(c == KC - 1))
                ins.then_inc(unit_done, 1)

            def expert(e, is_first, is_last):
                for j in range(UPE):
                    product(e, j, is_last)
                    if j == 0 and not is_first:
                        turn_rows(e - 1)
                    if j == 7 and not is_last:
                        turn_input(e + 1)

            pe.wait_ge(routed, 4)
            turn_input(0)
            expert(0, True, False)
            with pe.Fori(1, NE - 1) as e:
                expert(e, False, False)
            expert(NE - 1, False, True)
            turn_rows(NE - 1)


_INS = ["x_prompt", "x_sample", "state_rglru", "c", "c_ctx", "w_mod", "b_mod", "g_norm_mix", "g_norm_ffn", "w_in",
        "w_pool", "pool_scale", "w_conv", "b_conv", "w_gate_a", "b_gate_a", "w_gate_x", "b_gate_x", "lru_lambda",
        "w_out", "w_router", "w_exp_gate", "w_exp_up", "w_exp_down", "g_final"]
_OUTS = [((1, N_CTX, D), "float32"), ((1, N_LAT, D), "float32"), ((1, 1, 2, LC * P), "float32")]


def window_counts():
    out = np.zeros((NG, GRID_W + GRID_H + N_CTX), np.float32)
    for g in range(NG):
        w, at = 2 ** (g + 1), 0
        for n in (GRID_W, GRID_H, N_CTX):
            t = np.arange(n)
            count = np.minimum(t + w - w // 2, n) - np.maximum(t - w // 2, 0)
            out[g, at:at + n] = 1.0 / count
            at += n
    return out


def kernel(**inputs):
    import concourse.bacc as _bacc
    from concourse import mybir as _mybir
    from concourse.bass_utils import run_bass_kernel_spmd as _run

    nc = _bacc.Bacc("TRN2", target_bir_lowering=False, num_devices=1)
    arrays, args = {}, []
    consts = {"identity": np.eye(P, dtype=np.float32), "inv_count": window_counts()}
    for name in _INS + list(consts):
        a = np.ascontiguousarray(inputs[name] if name in inputs else consts[name])
        arrays[f"in_{name}_dram"] = a
        args.append(nc.dram_tensor(f"in_{name}_dram", a.shape, _mybir.dt.from_np(a.dtype), kind="ExternalInput").ap())
    for i, (shape, dtype) in enumerate(_OUTS):
        args.append(nc.dram_tensor(f"out_{i}_dram", shape, _mybir.dt.from_np(np.dtype(dtype)),
                                   kind="ExternalOutput").ap())
    hybrid_step_kernel(nc, *args)
    r = _run(nc, [arrays], core_ids=[0])
    return tuple(r.results[0][f"out_{i}_dram"] for i in range(len(_OUTS)))
```

```python
from contextlib import ExitStack

import numpy as np
import concourse.bass as bass
from concourse import mybir

D = 1024
P = 128
KC = D // P
N_LAT, N_CTX = 1024, 128
T = N_LAT + N_CTX
NT = T // P
CTX_TILE = NT - 1
SEG = T // 3
GRID_W, GRID_H = 64, N_LAT // 64
PAD = 8
PW = GRID_W + 2 * PAD
PH = GRID_H + 2 * PAD
NG = 4
LC = 4
CONV_W = 4
NE, CAP_L, CAP_C = 16, 128, 16
CAP = CAP_L + CAP_C
EPS = 1e-6
UW = 256
UN = KC * UW
RAW = 6
TILES_A = 4
SPLIT = 4
UPE = 12

ROWS = {}
_at = 0
for _name, _n in (("b_mod", 48), ("g_mix", 8), ("g_ffn", 8), ("c", 8), ("c_ctx", 8), ("pool_scale", 4),
                  ("w_conv", 16), ("b_conv", 4), ("b_gate_a", 8), ("b_gate_x", 8), ("lam", 8)):
    ROWS[_name] = (_at, _at + _n)
    _at += _n
assert _at == P

SHIFT1, SCALE1, GATE1, SHIFT2, SCALE2, GATE2 = (8 * i for i in range(6))
NMOD1, NMOD2 = 8, 16


def hybrid_step_kernel(nc, x_prompt, x_sample, state_rglru, c, c_ctx, w_mod, b_mod, g_norm_mix, g_norm_ffn,
                       w_in, w_pool, pool_scale, w_conv, b_conv, w_gate_a, b_gate_a, w_gate_x, b_gate_x,
                       lru_lambda, w_out, w_router, w_exp_gate, w_exp_up, w_exp_down, g_final,
                       identity, inv_count, chunk_numbers, y_prompt, y_sample, new_state):
    f32, f32r, u32 = mybir.dt.float32, mybir.dt.float32r, mybir.dt.uint32
    ACT = mybir.ActivationFunctionType
    ALU = mybir.AluOpType
    AX = mybir.AxisListType

    order = [("x", k) for k in range(KC)]
    order += [("M", 0), ("L", 0), ("M", 1), ("M", 2), ("L", 1), ("M", 3), ("G", 0, 0, 0), ("G", 0, 0, 1),
              ("P", 3), ("M", 4), ("G", 0, 1, 0), ("G", 0, 1, 1), ("P", 2), ("M", 5), ("G", 1, 0, 0), ("G", 1, 0, 1),
              ("L", 2), ("M", 6), ("G", 1, 1, 0), ("G", 1, 1, 1), ("L", 3), ("M", 7), ("G", 2, 0, 0), ("G", 2, 0, 1),
              ("P", 1), ("M", 8), ("G", 2, 1, 0), ("G", 2, 1, 1), ("P", 0), ("M", 9), ("G", 3, 0, 0), ("G", 3, 0, 1),
              ("E", 0), ("M", 10), ("G", 3, 1, 0), ("G", 3, 1, 1), ("E", 1), ("M", 11), ("E", 2), ("M", 12),
              ("M", 13), ("E", 3), ("M", 14), ("M", 15)]
    order += [("O", g) for g in (3, 2, 1, 0)]
    JOB = {j: n for n, j in enumerate(j for j in order if j[0] != "M")}
    NJOBS = len(JOB)
    POOL_ORDER = (3, 2, 1, 0)

    IN_CHUNK = {"P": 0, "L": 4, "E": 8}
    units = [("mod", u) for u in range(NMOD1)]
    for j in order:
        if j[0] == "M":
            units.append(("mod", NMOD1 + j[1]))
        elif j[0] in IN_CHUNK:
            u = ("in", (IN_CHUNK[j[0]] + j[1]) // 2)
            if u not in units:
                units.append(u)
    units += [("out", u) for u in range(D // UW)]
    UNIT = {u: n for n, u in enumerate(units)}
    OUT0 = UNIT[("out", 0)]
    MOE0 = len(units)

    def slot(n):
        return n % RAW

    def loads(n):
        return 16 * (n // RAW + 1)

    h_rows = nc.dram_tensor("h_rows", [T, D], f32).ap()
    y_rows = nc.dram_tensor("y_rows", [T, D], f32).ap()

    ctx = ExitStack()
    phase1, phase2, moe = ExitStack(), ExitStack(), ExitStack()

    def sb(name, shape, dt=f32, stack=ctx):
        return stack.enter_context(nc.sbuf_tensor(name, shape, dt))

    def sem(name):
        return ctx.enter_context(nc.semaphore(name))

    with ctx:
        ps = ctx.enter_context(nc.psum_tensor("ps", [P, 8, 512], f32))

        with ExitStack() as over:
            w_lo = sb("w_lo", [P, D // UW, KC, UW], f32r, stack=over)
            y_hi = sb("y_hi", [P, RAW - D // UW, KC, UW], f32r, stack=over)
        assert slot(OUT0) == 0 and slot(MOE0) == D // UW
        raw = sb("raw", [P, RAW, KC, UW])
        ident = sb("ident", [P, P])
        ones = sb("ones", [P, P])
        vecs = sb("vecs", [P, P])
        states = sb("states", [P, 8])
        silu_c = sb("silu_c", [P, KC, 2])
        mod = sb("mod", [P, 48, 2])
        scale_a = sb("scale_a", [P, KC, 2])
        spare = sb("spare", [P, 2])
        half = sb("half", [P, 1])
        lam_t = sb("lam_t", [P, 6, 8])
        rate = sb("rate", [P, 2, 8])
        st_out, st_rows = sb("st_out", [P, 8]), sb("st_rows", [8, P])
        sumsq = sb("sumsq", [P, 4, NT])
        rstd = sb("rstd", [P, 4, NT])
        w_r = sb("w_r", [P, KC, NE])
        logit_max = sb("logit_max", [P, NT])
        prob_sum = sb("prob_sum", [P, NT])
        prob_inv = sb("prob_inv", [P, NT])
        probs = sb("probs", [P, NT, NE])
        g_lat, i_lat = sb("g_lat", [CAP_L, NE]), sb("i_lat", [CAP_L, NE], u32)
        g_ctx, i_ctx = sb("g_ctx", [CAP_C, NE]), sb("i_ctx", [CAP_C, NE], u32)
        last_ctx = sb("last_ctx", [CAP_C, 1], u32)
        gi_lat, gi_ctx = sb("gi_lat", [CAP_L, 1], u32), sb("gi_ctx", [CAP_C, 1], u32)
        si_lat, si_ctx = sb("si_lat", [CAP_L, 1], u32), sb("si_ctx", [P, 1], u32)
        sg_lat, sg_ctx = sb("sg_lat", [CAP_L, 1]), sb("sg_ctx", [P, 1])
        assert KC * CAP_C == P
        chunk_no = sb("chunk_no", [P, 1])
        spread = sb("spread", [CAP_C, P])
        row_data = sb("row_data", [CAP_C, 2 * NE])
        g_part, i_part = sb("g_part", [P, NE]), sb("i_part", [P, NE], u32)
        g2_cols, g2_part = sb("g2_cols", [P, P]), sb("g2_part", [P, P])

        with ExitStack() as over:
            y_lo = sb("y_lo", [P, KC, T], f32r, stack=over)
        y_t = sb("y_t", [P, KC, T], stack=phase1)
        h_t = sb("h_t", [P, KC, T], stack=phase1)
        h_flat = h_t[:, :, :].rearrange("p k t -> p (k t)")
        bc = h_flat[:, 0:6 * D].rearrange("p (v s d) -> p v s d", v=3, s=2)
        g2 = h_flat[:, 7 * D:9 * D].rearrange("p (s d) -> p s d", s=2)
        x_in_stack = ExitStack()
        x_in = sb("x_in", [P, NT, D], stack=x_in_stack)
        junk0 = sb("junk0", [P, D], stack=x_in_stack)
        rows_in = sb("rows_in", [P, P], stack=x_in_stack)
        rows_st = sb("rows_st", [8, P], stack=x_in_stack)
        mod_rows = sb("mod_rows", [2, NMOD1 * UW], stack=x_in_stack)
        x_in_stack.close()
        lru = ExitStack()
        up = sb("up", [P, T + 6], stack=lru)
        UL, UC = 2, N_LAT + 5
        xc = sb("xc", [P, 2, T], stack=lru)
        r_a = sb("r_a", [P, T], stack=lru)
        i_b = sb("i_b", [P, T], stack=lru)
        tau = sb("tau", [P, T], stack=lru)
        pad_l = sb("pad_l", [P, 2, GRID_H, PW], stack=lru)
        pad_c = sb("pad_c", [P, 2, N_CTX + 2 * PAD], stack=lru)
        box = [sb(f"box{i}", [P, PH * GRID_W], stack=lru) for i in range(2)]
        box_c = [sb(f"box_c{i}", [P, N_CTX + 2 * PAD], stack=lru) for i in range(2)]
        tall = sb("tall", [P, PH, GRID_W], stack=lru)
        NI = GRID_W + GRID_H + N_CTX
        inv = sb("inv", [P, NG, NI], stack=lru)
        w_gates = sb("w_gates", [P, 2, 2, LC, P], stack=lru)
        w_p = sb("w_p", [P, NG, P], stack=lru)
        part = sb("part", [P, 2, 2, UW], stack=lru)
        gelu = up
        lru.close()
        x_res = sb("x_res", [P, 2, D], stack=phase2)
        w_hi = sb("w_hi", [P, D // UW, KC, UW], f32r, stack=phase2)
        x1 = sb("x1", [P, 2, D], stack=phase2)
        hn2 = sb("hn2", [P, 2, D], stack=phase2)
        hn2_t = sb("hn2_t", [P, 2, KC, P], stack=phase2)
        aff_a = sb("aff_a", [NE, TILES_A * P], stack=phase2)
        aff_b = sb("aff_b", [NE, N_LAT - TILES_A * P], stack=phase2)
        aff_c = sb("aff_c", [NE, N_CTX], stack=phase2)
        aff_w = [sb(f"aff_w{i}", [NE, max(TILES_A * P, N_LAT - TILES_A * P)], stack=phase2) for i in range(2)]
        top_a, top_af = sb("top_a", [NE, CAP_L], stack=phase2), sb("top_af", [NE, CAP_L], stack=phase2)
        top_ai = sb("top_ai", [NE, CAP_L], u32, stack=phase2)
        top_b, top_bi = sb("top_b", [NE, CAP_L], stack=phase2), sb("top_bi", [NE, CAP_L], u32, stack=phase2)
        rev_b, rev_bf = sb("rev_b", [NE, CAP_L], stack=phase2), sb("rev_bf", [NE, CAP_L], stack=phase2)
        pair, pair_d = sb("pair", [CAP_L, 4, NE], stack=phase2), sb("pair_d", [CAP_L, 2, NE], stack=phase2)
        top_c, top_cf = sb("top_c", [NE, CAP_C], stack=phase2), sb("top_cf", [NE, CAP_C], stack=phase2)
        top_ci = sb("top_ci", [NE, CAP_C], u32, stack=phase2)
        phase2.close()
        phase1.close()

        split = sb("split", [P, SPLIT, 2, KC, UW], f32r, stack=moe)
        sb("g2_kept", [P, 2 * D], stack=moe)
        x_l = sb("x_l", [CAP_L, D], stack=moe)
        x_c = sb("x_c", [CAP_C, D], stack=moe)
        xt = sb("xt", [P, KC, 2, CAP], f32r, stack=moe)
        gate_f = sb("gate_f", [P, 2, 2, CAP], stack=moe)
        gate_s = sb("gate_s", [P, 2, 2, CAP], stack=moe)
        up_f = sb("up_f", [P, 2, CAP], stack=moe)
        hid_f = sb("hid_f", [P, 2, 2, CAP], stack=moe)
        hid = sb("hid", [P, KC, 2, CAP], f32r, stack=moe)
        down, down_c = sb("down", [P, KC, CAP_L], stack=moe), sb("down_c", [P, KC, CAP_C], stack=moe)
        o_l = sb("o_l", [CAP_L, D], stack=moe)
        o_c = sb("o_c", [CAP_C, D], stack=moe)
        o_part = sb("o_part", [P, P], stack=moe)
        junk2 = sb("junk2", [P, D], stack=moe)
        g_fin = sb("g_fin", [P, D], stack=moe)
        moe.close()

        loaded = [sem(f"unit_loaded_{i}") for i in range(RAW)]
        rows_loaded, ident_loaded = sem("rows_loaded"), sem("ident_loaded")
        x_loaded = [sem(f"x_loaded_{t}") for t in range(NT)]
        small_loaded = sem("small_loaded")
        res_loaded = [sem(f"res_loaded_{i}") for i in range(2)]
        ones_ready = sem("ones_ready")
        vecs_turned, vecs_ready, silu_ready = sem("vecs_turned"), sem("vecs_ready"), sem("silu_ready")
        mods_done, mod1_ready, mod2_ready = sem("mods_done"), sem("mod1_ready"), sem("mod2_ready")
        mod_rows_ready, mod1_turned, part_ready = sem("mod_rows_ready"), sem("mod1_turned"), sem("part_ready")
        half_ready, sq_ready, rstd_ready, xn_ready = sem("half_ready"), sem("sq_ready"), sem("rstd_ready"), sem("xn_ready")
        job_done, job_read = sem("job_done"), sem("job_read")
        lam_act, lam_dve, rate_ready = sem("lam_act"), sem("lam_dve"), sem("rate_ready")
        pads_ready, up_ready, conv_done = sem("pads_ready"), sem("up_ready"), sem("conv_done")
        decay_ready, scan_done, gelu_used = sem("decay_ready"), sem("scan_done"), sem("gelu_used")
        box_ready, pooled = sem("box_ready"), sem("pooled")
        diag_ready, rows_spread, rows_kept = sem("diag_ready"), sem("rows_spread"), sem("rows_kept")
        state_turned, state_kept, state_stored = sem("state_turned"), sem("state_kept"), sem("state_stored")
        act_step, dve_step, pool_step = sem("act_step"), sem("dve_step"), sem("pool_step")
        w_out_hi, w_out_lo, y_out_hi, y_out_lo = (sem("w_out_hi"), sem("w_out_lo"), sem("y_out_hi"), sem("y_out_lo"))
        mix_done, mix_read, x1_ready = sem("mix_done"), sem("mix_read"), sem("x1_ready")
        sq2_ready, rstd2_ready, xn2_ready, hn2_ready = sem("sq2_ready"), sem("rstd2_ready"), sem("xn2_ready"), sem("hn2_ready")
        h_stored = [sem(f"h_stored_{i}") for i in range(2)]
        y_stored = [sem(f"y_stored_{i}") for i in range(2)]
        hn2_turned, hn2_t_ready, logits_done = sem("hn2_turned"), sem("hn2_t_ready"), sem("logits_done")
        max_ready, exp_ready, probs_ready = sem("max_ready"), sem("exp_ready"), sem("probs_ready")
        probs_turned, aff_ready = sem("probs_turned"), sem("aff_ready")
        top_ready, top_turned, routed = sem("top_ready"), sem("top_turned"), sem("routed")
        gi_ready, gathered, x_turned, xt_hi, xt_lo = (sem("gather_index_ready"), sem("gathered"), sem("x_turned"),
                                                      sem("xt_hi"), sem("xt_lo"))
        xt_c_hi, xt_c_lo = sem("xt_c_hi"), sem("xt_c_lo")
        hi_done, lo_done, unit_done = sem("hi_done"), sem("lo_done"), sem("unit_done")
        psum_read, silu_done, mul_done = sem("psum_read"), sem("silu_done"), sem("mul_done")
        hid_hi, hid_lo = sem("hid_hi"), sem("hid_lo")
        rows_turned, out_scaled, scattered = sem("rows_turned"), sem("out_scaled"), sem("scattered")
        rows_copied, parts_spread = sem("rows_copied"), sem("parts_spread")
        si_ready, ctx_scaled = sem("scatter_index_ready"), sem("ctx_scaled")
        paused = sem("paused")
        y_loaded = [sem(f"y_loaded_{t}") for t in range(NT)]
        g_fin_loaded = sem("g_fin_loaded")
        rows_back, sum_ready = sem("rows_back"), sem("sum_ready")
        sq4_ready, rstd4_ready, last_ready, last_stored = (sem("sq4_ready"), sem("rstd4_ready"), sem("last_ready"),
                                                           sem("last_stored"))
        sq3_ready, rstd3_ready, end_ready, stored = sem("sq3_ready"), sem("rstd3_ready"), sem("end_ready"), sem("stored")

        SMALL = 16 * 12
        END_STEP = 8
        def tile(s):
            return slice(TILES[s] * P, (TILES[s] + 1) * P)

        LAG = 3

        def vec(name):
            a, b = ROWS[name]
            return vecs[:, a:b]

        def stream(t):
            return 1 if t == CTX_TILE else 0

        def unit_source(kind, u):
            w = {"mod": w_mod, "in": w_in, "out": w_out}[kind]
            return w[0, :, u * UW:(u + 1) * UW].rearrange("(k p) n -> p k n", p=P)

        def x_tile(t):
            return x_prompt[0, :, :] if t == CTX_TILE else x_sample[0, t * P:(t + 1) * P, :]

        def y_end(t):
            a = t % 2 * (KC // 2)
            return raw[:, slot(MOE0 + (UPE - RAW) + t // 2), a:a + KC // 2, :].rearrange("p k n -> p (k n)")

        def out_tile(t):
            return y_prompt[0, :, :] if t == CTX_TILE else y_sample[0, t * P:(t + 1) * P, :]

        TILES = list(range(NT - 1)) + [CTX_TILE]

        sources = {"b_mod": b_mod[0], "g_mix": g_norm_mix[0], "g_ffn": g_norm_ffn[0], "c": c[0], "c_ctx": c_ctx,
                   "pool_scale": pool_scale[0], "w_conv": w_conv[0].rearrange("k n -> (k n)"), "b_conv": b_conv[0],
                   "b_gate_a": b_gate_a[0].rearrange("r h i -> (r h i)"),
                   "b_gate_x": b_gate_x[0].rearrange("r h i -> (r h i)"),
                   "lam": lru_lambda[0].rearrange("r n -> (r n)")}
        EARLY_ROWS = ("c", "c_ctx", "g_mix", "g_ffn", "pool_scale")

        block = ctx.enter_context(nc.Block())

        @block.sync
        def _(sp):
            def wait_used(n):
                kind, u = units[n]
                if kind == "mod" and u < NMOD1:
                    sp.wait_ge(mods_done, u + 1)
                elif kind == "mod":
                    sp.wait_ge(part_ready, u - NMOD1 + 1)
                else:
                    sp.wait_ge(job_done, 1 + max(JOB[(x, k)] for x, a in IN_CHUNK.items() for k in range(4)
                                                 if (a + k) // 2 == u))

            def load_unit(n):
                kind, u = units[n]
                if n >= RAW:
                    wait_used(n - RAW)
                sp.dma_start(raw[:, slot(n), :, :], unit_source(kind, u)).then_inc(loaded[slot(n)], 16)

            for name, (a, b) in ROWS.items():
                if name not in EARLY_ROWS:
                    sp.dma_start(rows_in[a:b, :], sources[name].rearrange("(r n) -> r n", n=P)).then_inc(rows_loaded, 16)
            for n in range(MOE0):
                load_unit(n)

            def load_residual(s):
                if s >= 2:
                    sp.wait_ge(x1_ready, s - 1)
                else:
                    sp.wait_ge(scan_done, 2 * LC)
                    sp.wait_ge(job_read, NJOBS)
                    sp.wait_ge(gelu_used, LC)
                    sp.wait_ge(pooled, NG)
                sp.dma_start(x_res[:, s % 2, :], x_tile(TILES[s])).then_inc(res_loaded[s % 2], 16)

            EXPERTS = {"g": w_exp_gate, "u": w_exp_up, "d": w_exp_down}

            def load_expert(e, j):
                kind, k = ("gu"[j % 2], j // 2) if j < 8 else ("d", j - 8)
                which = slice(e, e + 1) if isinstance(e, int) else bass.ds(e, 1)
                src = EXPERTS[kind][0, which, :, k * UW:(k + 1) * UW]
                sp.dma_start(raw[:, slot(MOE0 + j), :, :], src.rearrange("o (k p) n -> p (o k) n", p=P))\
                  .then_inc(loaded[slot(MOE0 + j)], 16)

            for s in range(NT):
                load_residual(s)
            for j in range(UPE):
                if j < RAW:
                    sp.wait_ge(mix_done, NT)
                else:
                    sp.wait_ge(lo_done, j - RAW + 1)
                load_expert(0, j)
            with sp.Fori(1, NE) as e:
                for j in range(UPE):
                    sp.wait_ge(lo_done, e * UPE + (j - RAW + 1))
                    load_expert(e, j)

            sp.dma_start(g_fin[:, :], g_final.partition_broadcast(P)).then_inc(g_fin_loaded, 16)
            sp.wait_ge(scattered, 32 * (NE - 1))
            for t in range(NT + 4):
                if t < NT:
                    if t % 2 == 0:
                        sp.wait_ge(lo_done, (NE - 1) * UPE + (UPE - RAW) + t // 2 + 1)
                    sp.dma_start(y_end(t), y_rows[t * P:(t + 1) * P, :]).then_inc(y_loaded[t], 16)
                if t >= 4:
                    sp.wait_ge(end_ready, t - 3)
                    sp.dma_start(out_tile(t - 4), y_end(t - 4)).then_inc(stored, 16)
            sp.wait_ge(stored, 16 * NT)
            sp.wait_ge(last_stored, 32)
            sp.wait_ge(state_stored, 16)

        @block.scalar
        def _(act):
            steps = [0]

            def link(ins):
                ins.then_inc(act_step, 1)
                steps[0] += 1
                act.wait_ge(act_step, steps[0])

            act.dma_start(ident[:, :], identity).then_inc(ident_loaded, 16)
            for name in EARLY_ROWS:
                a, b = ROWS[name]
                act.dma_start(rows_in[a:b, :], sources[name].rearrange("(r n) -> r n", n=P)).then_inc(rows_loaded, 16)
            act.dma_start(rows_st[:, :], state_rglru[0, 0].rearrange("r (k n) -> (r k) n", n=P)).then_inc(rows_loaded, 16)
            for t in range(NT):
                act.dma_start(x_in[:, t, :], x_tile(t)).then_inc(x_loaded[t], 16)

            act.wait_ge(vecs_ready, 2)
            a = ROWS["c"][0]
            act.activation(silu_c[:, :, :], vecs[:, a:a + 16].rearrange("p (s k) -> p k s", s=2), ACT.Silu)\
               .then_inc(silu_ready, 1)
            for t in range(NT):
                act.wait_ge(x_loaded[t], 16)
                act.activation(junk0[:, :], x_in[:, t, :], ACT.Square, accum_out=sumsq[:, 0, t:t + 1]).then_inc(sq_ready, 1)
                act.wait_ge(sq_ready, t + 1)
            link(act.activation(lam_t[:, 0, :], vec("lam"), ACT.Abs))
            act.activation(lam_t[:, 1, :], lam_t[:, 0, :], ACT.Exp, scale=-1.0).then_inc(lam_act, 1)
            act.wait_ge(lam_dve, 1)
            act.activation(lam_t[:, 3, :], lam_t[:, 2, :], ACT.Ln).then_inc(lam_act, 1)

            def bank_parts(j, dst):
                for n in range(3):
                    yield ps[:, 3 * (j % 2) + n, 0:SEG], dst[:, n * SEG:(n + 1) * SEG]

            def out_weight_high(u):
                if u == 0:
                    act.wait_ge(scan_done, 2 * LC)
                    act.wait_ge(pooled, NG)
                act.wait_ge(loaded[slot(OUT0 + u)], loads(OUT0 + u))
                act.activation(w_hi[:, u, :, :], raw[:, slot(OUT0 + u), :, :], ACT.Copy).then_inc(w_out_hi, 1)

            for job in order:
                if job[0] == "M":
                    continue
                j = JOB[job]
                kind, k = job[0], job[1]
                if job == ("E", LC - 1):
                    out_weight_high(0)
                if kind == "x":
                    if k == 0:
                        act.wait_ge(mod1_ready, 1)
                    act.wait_ge(job_done, j + 1)
                    for n, (a, b, s) in enumerate(((0, 512, 0), (512, N_LAT, 0), (N_LAT, T, 1))):
                        last_i = act.activation(h_t[:, k, a:b], ps[:, 3 * (j % 2) + n, 0:b - a], ACT.Identity,
                                                scale=scale_a[:, k, s:s + 1], bias=mod[:, SHIFT1 + k, s:s + 1])
                    last_i.then_inc(job_read, 1)
                elif kind == "L":
                    if k == 0:
                        act.wait_ge(up_ready, 1)
                    else:
                        act.wait_ge(conv_done, k)
                    act.wait_ge(job_done, j + 1)
                    b = 3 * (j % 2)
                    act.activation(up[:, UL:UL + SEG], ps[:, b, 0:SEG], ACT.Copy)
                    act.activation(up[:, UL + SEG:UL + 2 * SEG], ps[:, b + 1, 0:SEG], ACT.Copy)
                    act.activation(up[:, UL + 2 * SEG:UL + N_LAT], ps[:, b + 2, 0:N_LAT - 2 * SEG], ACT.Copy)
                    act.activation(up[:, UC:UC + N_CTX], ps[:, b + 2, N_LAT - 2 * SEG:SEG], ACT.Copy).then_inc(job_read, 1)
                elif kind == "P":
                    q = POOL_ORDER.index(k)
                    act.wait_ge(pads_ready, 1)
                    if q >= 2:
                        act.wait_ge(pooled, q - 1)
                    act.wait_ge(job_done, j + 1)
                    for n in range(3):
                        rows = (SEG if n < 2 else N_LAT - 2 * SEG) // GRID_W
                        at = n * SEG // GRID_W
                        act.activation(pad_l[:, q % 2, at:at + rows, PAD:PAD + GRID_W],
                                       ps[:, 3 * (j % 2) + n, 0:rows * GRID_W].rearrange("p (r w) -> p r w", w=GRID_W),
                                       ACT.Copy)
                    act.activation(pad_c[:, q % 2, PAD:PAD + N_CTX], ps[:, 3 * (j % 2) + 2, N_LAT - 2 * SEG:SEG],
                                   ACT.Copy).then_inc(job_read, 1)
                elif kind == "E":
                    if k > 0:
                        act.wait_ge(gelu_used, k)
                    else:
                        act.wait_ge(conv_done, LC)
                    act.wait_ge(job_done, j + 1)
                    for src, dst in bank_parts(j, gelu):
                        last_i = act.activation(dst, src, ACT.Gelu_apprx_tanh)
                    last_i.then_inc(job_read, 1)
                elif kind == "G":
                    _, k, r, ax = job
                    d = 2 * k + r
                    m = r * LC + k
                    if ax == 0:
                        if d > 0:
                            act.wait_ge(scan_done, d)
                        act.wait_ge(job_done, j + 1)
                        for src, dst in bank_parts(j, r_a):
                            last_i = act.activation(dst, src, ACT.Sigmoid, bias=vec("b_gate_a")[:, m:m + 1])
                        last_i.then_inc(job_read, 1)
                    else:
                        act.wait_ge(job_done, j + 1)
                        for src, dst in bank_parts(j, i_b):
                            last_i = act.activation(dst, src, ACT.Sigmoid, bias=vec("b_gate_x")[:, m:m + 1])
                        last_i.then_inc(job_read, 1)
                        act.wait_ge(rate_ready, 1)
                        act.wait_ge(job_read, JOB[("G", k, r, 0)] + 1)
                        link(act.activation(tau[:, :], r_a[:, :], ACT.Tanh, scale=rate[:, 0, m:m + 1]))
                        act.activation(r_a[:, :], r_a[:, :], ACT.Exp, scale=rate[:, 1, m:m + 1])
                        act.activation(tau[:, :], tau[:, :], ACT.Sqrt).then_inc(decay_ready, 1)
                elif kind == "O":
                    act.wait_ge(job_done, j + 1)
                    for src, dst in bank_parts(j, y_t[:, k, :]):
                        last_i = act.activation(dst, src, ACT.Copy, scale=vec("pool_scale")[:, k:k + 1])
                    last_i.then_inc(job_read, 1)

            def mixer_high(s):
                if s >= 2:
                    act.wait_ge(mix_done, s - 1)
                act.activation(y_hi[:, s % 2, :, 0:P], y_t[:, :, tile(s)], ACT.Copy).then_inc(y_out_hi, 1)

            for q in range(16):
                v, s, h = q // 4, q // 2 % 2, q % 2
                dst = bc[:, v, s, :] if v < 3 else g2[:, s, :]
                act.wait_ge(rows_spread, q + 1)
                act.activation(dst[:, 512 * h:512 * h + 512], ps[:, 6 + q % 2, :], ACT.Copy).then_inc(rows_kept, 1)
                if q % 4 == 1 and q > 1:
                    out_weight_high(q // 4)
                if q == 7:
                    act.wait_ge(gelu_used, LC)
                    act.wait_ge(job_read, NJOBS)
                    act.wait_ge(part_ready, NMOD2)
                    mixer_high(0)

            mixer_high(1)

            for s in range(NT + 1):
                if s < NT:
                    act.wait_ge(x1_ready, s + 1)
                    if s >= 2:
                        act.wait_ge(h_stored[s % 2], 16 * (s // 2))
                        act.wait_ge(hn2_turned, s - 1)
                    act.activation(hn2[:, s % 2, :], x1[:, s % 2, :], ACT.Square, accum_out=sumsq[:, 1, s:s + 1])\
                       .then_inc(sq2_ready, 1)
                if 0 <= s - 1 < NT:
                    t = s - 1
                    act.wait_ge(max_ready, t + 1)
                    act.activation(probs[:, t, :], ps[:, 6, 0:NE], ACT.Exp, bias=logit_max[:, t:t + 1],
                                   accum_out=prob_sum[:, t:t + 1]).then_inc(exp_ready, 1)
                if s < NT:
                    act.wait_ge(rstd2_ready, s + 1)
                    act.activation(hn2[:, s % 2, :], x1[:, s % 2, :], ACT.Copy, scale=rstd[:, 1, s:s + 1])\
                       .then_inc(xn2_ready, 1)
                    if s + 2 < NT:
                        mixer_high(s + 2)
                    act.wait_ge(hn2_turned, s + 1)
                    if s >= 2:
                        act.wait_ge(logits_done, s - 1)
                    for h in range(2):
                        last_i = act.activation(hn2_t[:, s % 2, 4 * h:4 * h + 4, :],
                                                ps[:, 4 + h, :].rearrange("p (k n) -> p k n", k=4), ACT.Copy)
                    last_i.then_inc(hn2_t_ready, 1)
            def split_high(e, j):
                m = e * UPE + j
                act.wait_ge(loaded[slot(MOE0 + j)], e * (16 * UPE // RAW) + loads(MOE0 + j))
                if not (isinstance(e, int) and e == 0 and j < SPLIT):
                    act.wait_ge(unit_done, m + (1 - SPLIT))
                act.activation(split[:, j % SPLIT, 0, :, :], raw[:, slot(MOE0 + j), :, :], ACT.Copy).then_inc(hi_done, 1)

            def hidden_high(e, k):
                act.wait_ge(mul_done, e * 4 + (k + 1))
                if not (isinstance(e, int) and e == 0):
                    act.wait_ge(unit_done, e * UPE)
                act.activation(hid[:, 2 * k:2 * k + 2, 0, :], hid_f[:, k % 2, :, :], ACT.Copy).then_inc(hid_hi, 1)

            def after_product(e, j):
                if j < 8 and j % 2 == 0:
                    k = j // 2
                    act.wait_ge(psum_read, e * UPE + (j + 1))
                    if not (isinstance(e, int) and e == 0 and k < 2):
                        act.wait_ge(mul_done, e * 4 + (k - 1))
                    act.activation(gate_s[:, k % 2, :, :], gate_f[:, k % 2, :, :], ACT.Silu).then_inc(silu_done, 1)
                    if k > 0:
                        hidden_high(e, k - 1)
                elif j == 7:
                    hidden_high(e, 3)

            def input_high(e):
                act.wait_ge(x_turned, e + 1)
                act.activation(xt[:, :, 0, CAP_L:CAP], ps[:, 0, 0:KC * CAP_C].rearrange("p (k n) -> p k n", k=KC),
                               ACT.Copy).then_inc(xt_c_hi, 1)
                for h in range(2):
                    last_i = act.activation(xt[:, 4 * h:4 * h + 4, 0, 0:CAP_L],
                                            ps[:, 6 + h, :].rearrange("p (k n) -> p k n", k=4), ACT.Copy)
                last_i.then_inc(xt_hi, 1)

            def expert(e, is_first, is_last):
                for j in range(UPE):
                    if not (is_first and j < LAG):
                        split_high(e, j)
                    if j >= LAG:
                        after_product(e, j - LAG)
                    if j == 7 + LAG and not is_last:
                        input_high(e + 1)
                    if is_last and j >= END_STEP:
                        last_norm(j - END_STEP)

            def last_norm(t):
                act.wait_ge(y_loaded[t], 16)
                if t > 0:
                    act.wait_ge(sq3_ready, t)
                act.activation(junk2[:, :], y_end(t), ACT.Square, accum_out=sumsq[:, 2, t:t + 1]).then_inc(sq3_ready, 1)

            act.wait_ge(hn2_ready, NT)
            act.wait_ge(mix_done, NT)
            for j in range(LAG):
                split_high(0, j)
            input_high(0)
            expert(0, True, False)
            with act.Fori(1, NE - 1) as e:
                expert(e, False, False)
            expert(NE - 1, False, True)

            for t in range(UPE - END_STEP, NT):
                last_norm(t)
            act.wait_ge(sq3_ready, NT)
            act.wait_ge(sum_ready, 1)
            act.activation(junk2[:, :], x_l[:, :], ACT.Square, accum_out=sumsq[:, 3, 0:1]).then_inc(sq4_ready, 1)
            act.wait_ge(sum_ready, 2)
            act.wait_ge(sq4_ready, 1)
            act.activation(junk2[0:CAP_C, :], x_c[:, :], ACT.Square, accum_out=sumsq[0:CAP_C, 3, 1:2]).then_inc(sq4_ready, 1)

        @block.gpsimd
        def _(pool):
            steps = [0]

            def link(ins):
                ins.then_inc(pool_step, 1)
                steps[0] += 1
                pool.wait_ge(pool_step, steps[0])

            pool.memset(half[:, :], -0.5).then_inc(half_ready, 1)
            link(pool.memset(spare[:, :], 0.0))
            pool.wait_ge(half_ready, 1)

            def root(norm, t, ready, done, n=P):
                pool.wait_ge(ready, t + 1)
                x = rstd[0:n, norm, t:t + 1]
                link(pool.tensor_scalar(x, sumsq[0:n, norm, t:t + 1], 1.0 / D, EPS, ALU.mult, ALU.add))
                pool.tensor_tensor(x, x, half[0:n, :], ALU.pow).then_inc(done, 1)

            for t in range(NT):
                root(0, t, sq_ready, rstd_ready)

            pool.wait_ge(job_done, KC)
            pool.memset(w_gates[:, :, :, :, :], 0.0).then_inc(pool_step, 1)
            pool.memset(pad_l[:, :, :, :], 0.0).then_inc(pool_step, 1)
            pool.memset(pad_c[:, :, :], 0.0).then_inc(pool_step, 1)
            pool.memset(tall[:, :, :], 0.0).then_inc(pool_step, 1)
            steps[0] += 4
            pool.wait_ge(pool_step, steps[0])
            for ax, w in enumerate((w_gate_a, w_gate_x)):
                for h in range(2):
                    src = w[0].rearrange("r (k h) i j -> h i r k j", h=2)[h]
                    for r in range(2):
                        pool.dma_start(w_gates[64 * h:64 * h + 64, ax, r, :, 64 * h:64 * h + 64], src[:, r, :, :])\
                            .then_inc(small_loaded, 16)
            pool.dma_start(w_p[:, :, :], w_pool[0].rearrange("g c d -> c g d")).then_inc(small_loaded, 16)
            pool.dma_start(inv[:, :, :], inv_count.partition_broadcast(P)).then_inc(small_loaded, 16)
            pool.dma_start(chunk_no[:, :], chunk_numbers).then_inc(small_loaded, 16)
            pool.dma_start(w_r[:, :, :], w_router[0].rearrange("(k p) e -> p k e", p=P)).then_inc(small_loaded, 16)
            pool.nop().then_inc(pads_ready, 1)

            def doubling(g, first, middle, final, take, size):
                spans, a, b = [], 0, size
                for s in range(g, -1, -1):
                    spans.insert(0, (a, b))
                    h = max(1, 2 ** (s - 1))
                    a, b = a - h, b + h
                src = first
                for s, (a, b) in enumerate(spans):
                    left, right = (1, 0) if s == 0 else (2 ** (s - 1), 2 ** (s - 1))
                    dst = final if s == g else take(middle[s % 2], a, b)
                    link(pool.tensor_tensor(dst, take(src, a - left, b - left), take(src, a + right, b + right), ALU.add))
                    src = middle[s % 2]

            def along_row(buf, a, b):
                return buf[:, :, PAD + a:PAD + b]

            def along_column(buf, a, b):
                return buf[:, PAD + a:PAD + b, :]

            def along_line(buf, a, b):
                return buf[:, PAD + a:PAD + b]

            wide = [b[:, 0:GRID_H * PW].rearrange("p (r w) -> p r w", w=PW) for b in box]
            high = [b[:, :].rearrange("p (r w) -> p r w", w=GRID_W) for b in box]
            for q, g in enumerate(POOL_ORDER):
                if q > 0:
                    pool.wait_ge(pooled, q)
                pool.wait_ge(job_read, JOB[("P", g)] + 1)
                doubling(g, pad_c[:, q % 2, :], box_c, along_line(box_c[g % 2], 0, N_CTX), along_line, N_CTX)
                doubling(g, pad_l[:, q % 2, :, :], wide, tall[:, PAD:PAD + GRID_H, :], along_row, GRID_W)
                doubling(g, tall, high, along_column(high[g % 2], 0, GRID_H), along_column, GRID_H)
                pool.nop().then_inc(box_ready, 1)

            pool.wait_ge(state_kept, 1)
            pool.dma_start(new_state[0, 0].rearrange("r (k n) -> (r k) n", n=P), st_rows[:, :])\
                .then_inc(state_stored, 16)

            for s in range(NT):
                t = TILES[s]
                pool.wait_ge(x1_ready, s + 1)
                pool.dma_start(y_rows[t * P:(t + 1) * P, :], x1[:, s % 2, :]).then_inc(y_stored[s % 2], 16)
                root(1, s, sq2_ready, rstd2_ready)
                pool.wait_ge(hn2_ready, s + 1)
                pool.dma_start(h_rows[t * P:(t + 1) * P, :], hn2[:, s % 2, :]).then_inc(h_stored[s % 2], 16)
            pool.wait_ge(h_stored[0], 16 * ((NT + 1) // 2))
            pool.wait_ge(h_stored[1], 16 * (NT // 2))
            pool.wait_ge(y_stored[0], 16 * ((NT + 1) // 2))
            pool.wait_ge(y_stored[1], 16 * (NT // 2))
            pool.wait_ge(routed, 5)

            def pause(before):
                if not (isinstance(before, int) and before == 0):
                    pool.wait_ge(paused, before)
                pool.tensor_tensor(spare[:, 1:2], spare[:, 0:1], spare[:, 0:1], ALU.add).then_inc(paused, 1)

            def gather(e, paused_before):
                if not (isinstance(e, int) and e == 0):
                    pool.wait_ge(x_turned, e)
                pool.wait_ge(gi_ready, e + 1)
                pause(paused_before)
                pool.indirect_dma_start(x_l[:, :], None, h_rows, bass.IndirectOffsetOnAxis(ap=gi_lat[:, :], axis=0))\
                    .then_inc(gathered, 16)
                pool.indirect_dma_start(x_c[:, :], None, h_rows, bass.IndirectOffsetOnAxis(ap=gi_ctx[:, :], axis=0))\
                    .then_inc(gathered, 16)

            def scatter(e, paused_before):
                pool.wait_ge(out_scaled, e + 1)
                pause(paused_before)
                pool.indirect_dma_start(y_rows, bass.IndirectOffsetOnAxis(ap=si_lat[:, :], axis=0), o_l[:, :], None,
                                        compute_op=ALU.add).then_inc(scattered, 16)
                pool.indirect_dma_start(y_rows.rearrange("t (k n) -> (t k) n", n=P),
                                        bass.IndirectOffsetOnAxis(ap=si_ctx[:, :], axis=0), o_part[:, :], None,
                                        compute_op=ALU.add).then_inc(scattered, 16)
                pool.wait_ge(scattered, e * 32 + 32)

            gather(0, 0)
            gather(1, 1)
            with pool.Fori(1, NE - 1) as e:
                scatter(e - 1, 2 * e)
                gather(e + 1, 2 * e + 1)
            scatter(NE - 2, 2 * NE - 2)
            pool.wait_ge(x_turned, NE)
            pause(2 * NE - 1)
            pool.indirect_dma_start(x_l[:, :], None, y_rows, bass.IndirectOffsetOnAxis(ap=gi_lat[:, :], axis=0))\
                .then_inc(rows_back, 16)
            pool.indirect_dma_start(x_c[:, :], None, y_rows, bass.IndirectOffsetOnAxis(ap=gi_ctx[:, :], axis=0))\
                .then_inc(rows_back, 16)
            for t in range(NT):
                root(2, t, sq3_ready, rstd3_ready)
            root(3, 0, sq4_ready, rstd4_ready)
            root(3, 1, sq4_ready, rstd4_ready, CAP_C)
            pool.wait_ge(stored, 16 * NT)
            pool.wait_ge(last_ready, 1)
            pause(2 * NE)
            pool.indirect_dma_start(y_sample[0], bass.IndirectOffsetOnAxis(ap=gi_lat[:, :], axis=0), x_l[:, :], None)\
                .then_inc(last_stored, 16)
            pool.wait_ge(last_ready, 2)
            pause(2 * NE + 1)
            pool.indirect_dma_start(y_prompt[0], bass.IndirectOffsetOnAxis(ap=last_ctx[:, :], axis=0), x_c[:, :], None)\
                .then_inc(last_stored, 16)

        @block.vector
        def _(dve):
            steps = [0]

            def link(ins):
                ins.then_inc(dve_step, 1)
                steps[0] += 1
                dve.wait_ge(dve_step, steps[0])

            dve.memset(ones[:, :], 1.0).then_inc(ones_ready, 1)
            dve.wait_ge(vecs_turned, 2)
            dve.tensor_copy(vecs[:, :], ps[:, 7, 0:P]).then_inc(vecs_ready, 1)
            dve.tensor_copy(states[:, :], ps[:, 7, P:P + 8]).then_inc(vecs_ready, 1)
            dve.wait_ge(vecs_ready, 2)
            for t in range(NT):
                dve.wait_ge(rstd_ready, t + 1)
                dve.tensor_scalar(x_in[:, t, :], x_in[:, t, :], rstd[:, 0, t:t + 1], None, ALU.mult).then_inc(xn_ready, 1)

            dve.wait_ge(lam_act, 1)
            dve.tensor_scalar(lam_t[:, 2, :], lam_t[:, 1, :], 1.0, None, ALU.add).then_inc(lam_dve, 1)
            dve.wait_ge(lam_dve, 1)
            link(dve.tensor_scalar(lam_t[:, 4, :], lam_t[:, 2, :], -1.0, None, ALU.add))
            link(dve.tensor_scalar(lam_t[:, 5, :], lam_t[:, 4, :], 0.0, None, ALU.is_equal))
            link(dve.tensor_tensor(lam_t[:, 4, :], lam_t[:, 4, :], lam_t[:, 5, :], ALU.add))
            link(dve.reciprocal(lam_t[:, 4, :], lam_t[:, 4, :]))
            dve.wait_ge(lam_act, 2)
            link(dve.tensor_tensor(lam_t[:, 3, :], lam_t[:, 3, :], lam_t[:, 5, :], ALU.add))
            link(dve.tensor_tensor(lam_t[:, 3, :], lam_t[:, 3, :], lam_t[:, 4, :], ALU.mult))
            link(dve.tensor_tensor(lam_t[:, 3, :], lam_t[:, 3, :], lam_t[:, 1, :], ALU.mult))
            link(dve.tensor_scalar(lam_t[:, 0, :], vec("lam"), -1.0, 0.0, ALU.mult, ALU.max))
            link(dve.tensor_tensor(lam_t[:, 0, :], lam_t[:, 0, :], lam_t[:, 3, :], ALU.add))
            link(dve.tensor_scalar(rate[:, 0, :], lam_t[:, 0, :], 4.0, None, ALU.mult))
            dve.tensor_scalar(rate[:, 1, :], lam_t[:, 0, :], -8.0, None, ALU.mult).then_inc(rate_ready, 1)

            def add_bias(a, b):
                v = vecs[:, a:b].unsqueeze(2).broadcast_to([P, b - a, 2])
                link(dve.tensor_tensor(mod[:, a:b, :], ps[:, 6, 2 * a:2 * b].rearrange("p (k s) -> p k s", s=2), v, ALU.add))

            def one_plus_scale(a, g):
                return dve.scalar_tensor_tensor(out=scale_a[:, :, :], in0=mod[:, a:a + KC, :], scalar=1.0,
                                                in1=vec(g).unsqueeze(2).broadcast_to([P, KC, 2]),
                                                op0=ALU.add, op1=ALU.mult)

            for u in range(0, NMOD1, 2):
                dve.wait_ge(mods_done, u + 2)
                dve.tensor_copy(mod_rows[:, u * UW:(u + 2) * UW], ps[0:2, u // 2, :]).then_inc(mod_rows_ready, 1)
            dve.wait_ge(mod1_turned, 1)
            add_bias(0, 2 * NMOD1)
            one_plus_scale(SCALE1, "g_mix").then_inc(mod1_ready, 1)

            SEQS = ((UL, 0, N_LAT), (UC, N_LAT, N_CTX))

            def conv(k):
                w0 = ROWS["w_conv"][0]
                dve.wait_ge(job_read, JOB[("L", k)] + 1)
                if k >= 2:
                    dve.wait_ge(job_done, JOB[("G", k - 2, 1, 1)] + 1)
                for o, a, n in SEQS:
                    u = up[:, o - 2:o - 2 + n]
                    link(dve.tensor_scalar(xc[:, k % 2, a:a + n], u, vecs[:, w0 + k:w0 + k + 1],
                                           vec("b_conv")[:, k:k + 1], ALU.mult, ALU.add))
                for tap in range(1, CONV_W):
                    for i, (o, a, n) in enumerate(SEQS):
                        u = up[:, o - 2 + tap:o - 2 + tap + n]
                        ins = dve.scalar_tensor_tensor(out=xc[:, k % 2, a:a + n], in0=u,
                                                       scalar=vecs[:, w0 + LC * tap + k:w0 + LC * tap + k + 1],
                                                       in1=xc[:, k % 2, a:a + n], op0=ALU.mult, op1=ALU.add)
                        if tap == CONV_W - 1 and i == 1:
                            ins.then_inc(conv_done, 1)
                        elif i == 1:
                            link(ins)

            def scan(k, r):
                d = 2 * k + r
                m = r * LC + k
                dve.wait_ge(decay_ready, d + 1)
                link(dve.tensor_tensor(i_b[:, :], i_b[:, :], xc[:, k % 2, :], ALU.mult))
                link(dve.scalar_tensor_tensor(out=tau[:, :], in0=r_a[:, :], scalar=1.0, in1=tau[:, :],
                                              op0=ALU.add, op1=ALU.mult))
                link(dve.tensor_tensor(i_b[:, :], i_b[:, :], tau[:, :], ALU.mult))
                dst = y_t[:, LC + k, :] if r == 0 else tau[:, :]
                for n, (a, b) in enumerate(((0, N_LAT), (N_LAT, T))):
                    def run(x):
                        x = x[:, a:b]
                        return x if r == 0 else x[:, ::-1]
                    start = states[:, m:m + 1] if n == 0 else 0.0
                    link(dve.tensor_tensor_scan(run(dst), run(r_a[:, :]), run(i_b[:, :]), start, ALU.mult, ALU.add))
                end = T - 1 if r == 0 else N_LAT
                link(dve.tensor_copy(st_out[:, m:m + 1], dst[:, end:end + 1]))
                if r == 1:
                    dve.tensor_tensor(y_t[:, LC + k, :], y_t[:, LC + k, :], tau[:, :], ALU.add).then_inc(scan_done, 1)
                    dve.wait_ge(scan_done, d + 1)
                else:
                    dve.nop().then_inc(scan_done, 1)

            def pooling(g):
                q = POOL_ORDER.index(g)
                dve.wait_ge(small_loaded, SMALL)
                dve.wait_ge(box_ready, q + 1)
                d = y_t[:, g, 0:N_LAT].rearrange("p (r w) -> p r w", w=GRID_W)
                s = box[g % 2][:, PAD * GRID_W:(PAD + GRID_H) * GRID_W].rearrange("p (r w) -> p r w", w=GRID_W)
                by_col = inv[:, g, 0:GRID_W].unsqueeze(1).broadcast_to([P, GRID_H, GRID_W])
                by_row = inv[:, g, GRID_W:GRID_W + GRID_H].unsqueeze(2).broadcast_to([P, GRID_H, GRID_W])
                link(dve.tensor_tensor(d, s, by_col, ALU.mult))
                link(dve.tensor_tensor(d, d, by_row, ALU.mult))
                link(dve.tensor_tensor(d, d, pad_l[:, q % 2, :, PAD:PAD + GRID_W], ALU.subtract))
                dc = y_t[:, g, N_LAT:T]
                link(dve.tensor_tensor(dc, box_c[g % 2][:, PAD:PAD + N_CTX], inv[:, g, GRID_W + GRID_H:NI], ALU.mult))
                dve.tensor_tensor(dc, dc, pad_c[:, q % 2, PAD:PAD + N_CTX], ALU.subtract).then_inc(pooled, 1)

            def gated(k):
                dve.wait_ge(job_read, JOB[("E", k)] + 1)
                dve.tensor_tensor(y_t[:, LC + k, :], y_t[:, LC + k, :], gelu[:, 0:T], ALU.mult).then_inc(gelu_used, 1)

            def modulate(u):
                n = UNIT[("mod", NMOD1 + u)]
                dve.wait_ge(loaded[slot(n)], loads(n))
                if u >= 2:
                    dve.wait_ge(mods_done, NMOD1 + u - 1)
                for k in range(KC):
                    for s in range(2):
                        w, dst = raw[:, slot(n), k, :], part[:, u % 2, s, :]
                        if k == 0:
                            ins = dve.tensor_scalar(dst, w, silu_c[:, k, s:s + 1], None, ALU.mult)
                        else:
                            dve.wait_ge(dve_step, steps[0] - 1)
                            ins = dve.scalar_tensor_tensor(out=dst, in0=w, scalar=silu_c[:, k, s:s + 1], in1=dst,
                                                           op0=ALU.mult, op1=ALU.add)
                        if k == KC - 1 and s == 1:
                            dve.wait_ge(dve_step, steps[0])
                            ins.then_inc(part_ready, 1)
                        else:
                            ins.then_inc(dve_step, 1)
                            steps[0] += 1

            def out_weight_low(u):
                dve.wait_ge(w_out_hi, u + 1)
                dve.tensor_tensor(w_lo[:, u, :, :], raw[:, slot(OUT0 + u), :, :], w_hi[:, u, :, :].bitcast(f32),
                                  ALU.subtract).then_inc(w_out_lo, 1)

            modulate(0)
            modulate(1)
            dve.wait_ge(job_done, KC)
            link(dve.memset(up[:, 0:UL], 0.0))
            link(dve.memset(up[:, UL + N_LAT:UC], 0.0))
            dve.memset(up[:, UC + N_CTX:T + 6], 0.0).then_inc(up_ready, 1)
            conv(0)
            modulate(2)
            modulate(3)
            conv(1)
            scan(0, 0)
            modulate(4)
            scan(0, 1)
            modulate(5)
            scan(1, 0)
            pooling(3)
            modulate(6)
            conv(2)
            scan(1, 1)
            modulate(7)
            conv(3)
            scan(2, 0)
            modulate(8)
            pooling(2)
            scan(2, 1)
            modulate(9)
            scan(3, 0)
            pooling(1)
            modulate(10)
            gated(0)
            scan(3, 1)
            pooling(0)
            modulate(11)
            gated(1)
            modulate(12)
            modulate(13)
            gated(2)
            modulate(14)
            modulate(15)
            out_weight_low(0)
            gated(3)
            dve.wait_ge(state_turned, 1)
            dve.tensor_copy(st_rows[:, :], ps[0:8, 7, 0:P]).then_inc(state_kept, 1)

            def mixer_low(s):
                dve.wait_ge(y_out_hi, s + 1)
                dve.tensor_tensor(y_lo[:, :, tile(s)], y_t[:, :, tile(s)], y_hi[:, s % 2, :, 0:P].bitcast(f32), ALU.subtract)\
                   .then_inc(y_out_lo, 1)

            dve.wait_ge(mods_done, NMOD1 + NMOD2)
            add_bias(2 * NMOD1, 48)
            link(one_plus_scale(SCALE2, "g_ffn"))
            dve.nop().then_inc(mod2_ready, 1)
            dve.wait_ge(pooled, NG)
            for q in range(16):
                v, s, h = q // 4, q // 2 % 2, q % 2
                src = (mod[:, GATE1:GATE1 + KC, s], scale_a[:, :, s], mod[:, SHIFT2:SHIFT2 + KC, s],
                       mod[:, GATE2:GATE2 + KC, s])[v]
                if q >= 2:
                    dve.wait_ge(rows_spread, q - 1)
                dve.tensor_tensor(box[q % 2][:, PH * GRID_W - 512:].rearrange("p (k n) -> p k n", k=4),
                                  ident[:, :].unsqueeze(1).broadcast_to([P, 4, P]),
                                  src[:, 4 * h:4 * h + 4].unsqueeze(2).broadcast_to([P, 4, P]), ALU.mult)\
                   .then_inc(diag_ready, 1)
                if q == 9:
                    out_weight_low(1)
                if q == 13:
                    mixer_low(0)
            out_weight_low(2)
            out_weight_low(3)
            mixer_low(1)

            dve.wait_ge(rows_kept, 16)
            def top_round(aff, work, best, index, n, rounds):
                src = aff if n == 0 else work[(n - 1) % 2]
                link(dve.max(best[:, 8 * n:8 * n + 8], src))
                ins = dve.max_index(index[:, 8 * n:8 * n + 8], best[:, 8 * n:8 * n + 8], src)
                if n < rounds - 1:
                    link(dve.match_replace(work[n % 2], best[:, 8 * n:8 * n + 8], src, -1.0))
                else:
                    link(ins)

            ROUNDS = CAP_L // 8
            done = [0]

            def rounds(n):
                for m in range(done[0], min(done[0] + n, 2 * ROUNDS)):
                    if m < ROUNDS:
                        top_round(aff_a[:, :], [w[:, 0:TILES_A * P] for w in aff_w], top_a, top_ai, m, ROUNDS)
                    else:
                        top_round(aff_b[:, :], [w[:, 0:N_LAT - TILES_A * P] for w in aff_w], top_b, top_bi, m - ROUNDS, ROUNDS)
                    done[0] += 1

            def softmax_max(t):
                dve.wait_ge(logits_done, t + 1)
                dve.tensor_reduce(logit_max[:, t:t + 1], ps[:, 6, 0:NE], AX.X, ALU.max, negate=True).then_inc(max_ready, 1)

            def softmax_rows(t):
                dve.wait_ge(exp_ready, t + 1)
                link(dve.reciprocal(prob_inv[:, t:t + 1], prob_sum[:, t:t + 1]))
                dve.tensor_scalar(probs[:, t, :], probs[:, t, :], prob_inv[:, t:t + 1], None, ALU.mult)\
                   .then_inc(probs_ready, 1)

            def affinities(t):
                dve.wait_ge(probs_turned, t + 1)
                a = TILES[t] * P
                dst = (aff_c[:, :] if TILES[t] == CTX_TILE else aff_a[:, a:a + P] if TILES[t] < TILES_A else
                       aff_b[:, a - TILES_A * P:a - TILES_A * P + P])
                dve.tensor_copy(dst, ps[0:NE, 7, 0:P]).then_inc(aff_ready, 1)
                dve.wait_ge(aff_ready, t + 1)

            for s in range(NT + 1):
                if s < NT:
                    t = TILES[s]
                    dve.wait_ge(res_loaded[s % 2], 16 * (s // 2 + 1))
                    if s >= 2:
                        dve.wait_ge(y_stored[s % 2], 16 * (s // 2))
                        dve.wait_ge(xn2_ready, s - 1)
                    dve.wait_ge(mix_done, s + 1)
                    b = 2 * (s % 2)
                    dve.tensor_tensor(x1[:, s % 2, :], ps[:, b:b + 2, :].rearrange("p b n -> p (b n)"),
                                      bc[:, 0, stream(t), :], ALU.mult).then_inc(mix_read, 1)
                    dve.wait_ge(mix_read, s + 1)
                    dve.tensor_tensor(x1[:, s % 2, :], x1[:, s % 2, :], x_res[:, s % 2, :], ALU.add).then_inc(x1_ready, 1)
                if s >= 1:
                    softmax_max(s - 1)
                if TILES_A < s < NT:
                    rounds(1)
                if s >= 1:
                    softmax_rows(s - 1)
                if s < NT:
                    dve.wait_ge(xn2_ready, s + 1)
                    link(dve.tensor_tensor(hn2[:, s % 2, :], hn2[:, s % 2, :], bc[:, 1, stream(t), :], ALU.mult))
                    dve.tensor_tensor(hn2[:, s % 2, :], hn2[:, s % 2, :], bc[:, 2, stream(t), :], ALU.add)\
                       .then_inc(hn2_ready, 1)
                if s + 2 < NT:
                    mixer_low(s + 2)
                if s >= 1:
                    affinities(s - 1)
                if s >= TILES_A:
                    rounds(4 if s == NT - 1 else 2)
            rounds(2 * ROUNDS)
            for n in range(CAP_C // 8):
                top_round(aff_c[:, :], [w[:, 0:N_CTX] for w in aff_w], top_c, top_ci, n, CAP_C // 8)
            dve.tensor_copy(top_af[:, :], top_ai[:, :]).then_inc(top_ready, 1)
            dve.tensor_copy(rev_b[:, :], top_b[:, ::-1]).then_inc(top_ready, 1)
            link(dve.tensor_copy(rev_bf[:, :], top_bi[:, ::-1]))
            dve.tensor_scalar(rev_bf[:, :], rev_bf[:, :], float(TILES_A * P), None, ALU.add).then_inc(top_ready, 1)
            link(dve.tensor_copy(top_cf[:, :], top_ci[:, :]))
            dve.tensor_scalar(top_cf[:, :], top_cf[:, :], float(N_LAT), None, ALU.add).then_inc(top_ready, 1)
            dve.wait_ge(top_turned, 6)
            link(dve.tensor_copy(pair[:, :, :], ps[:, 4, 0:4 * NE].rearrange("p (n e) -> p n e", n=4)))
            dve.tensor_tensor(g_lat[:, :], pair[:, 0, :], pair[:, 2, :], ALU.max).then_inc(routed, 1)
            dve.tensor_tensor(pair_d[:, 0, :], pair[:, 0, :], pair[:, 2, :], ALU.is_ge).then_inc(dve_step, 1)
            dve.tensor_tensor(pair_d[:, 1, :], pair[:, 1, :], pair[:, 3, :], ALU.subtract).then_inc(dve_step, 1)
            steps[0] += 2
            dve.wait_ge(dve_step, steps[0])
            link(dve.tensor_tensor(pair_d[:, 0, :], pair_d[:, 0, :], pair_d[:, 1, :], ALU.mult))
            link(dve.tensor_tensor(pair_d[:, 0, :], pair_d[:, 0, :], pair[:, 3, :], ALU.add))
            dve.tensor_copy(i_lat[:, :], pair_d[:, 0, :]).then_inc(routed, 1)
            dve.tensor_copy(g_ctx[:, :], ps[0:CAP_C, 5, 0:NE]).then_inc(routed, 1)
            dve.tensor_copy(i_ctx[:, :], ps[0:CAP_C, 5, NE:2 * NE]).then_inc(routed, 1)
            dve.tensor_scalar(last_ctx[:, :], ps[0:CAP_C, 5, 2 * NE - 1:2 * NE], -float(N_LAT), None, ALU.add)\
               .then_inc(routed, 1)
            dve.tensor_copy(row_data[:, :], ps[0:CAP_C, 5, 0:2 * NE]).then_inc(rows_copied, 1)
            dve.tensor_copy(spread[:, :].rearrange("p (k n) -> p k n", n=CAP_C),
                            ident[0:CAP_C, 0:CAP_C].unsqueeze(1).broadcast_to([CAP_C, KC, CAP_C])).then_inc(rows_copied, 1)
            dve.tensor_copy(g2_cols[:, :].rearrange("p (k n) -> p k n", n=CAP_C),
                            mod[:, GATE2:GATE2 + KC, 1].unsqueeze(2).broadcast_to([P, KC, CAP_C])).then_inc(rows_copied, 1)
            dve.wait_ge(routed, 5)

            def column(x, e):
                return x[:, e:e + 1] if isinstance(e, int) else x[:, bass.ds(e, 1)]

            def gather_index(e):
                dve.wait_ge(routed, 5)
                dve.tensor_copy(gi_lat[:, :], column(i_lat, e))
                dve.tensor_copy(gi_ctx[:, :], column(i_ctx, e)).then_inc(gi_ready, 1)

            def split_low(e, j):
                dve.wait_ge(hi_done, e * UPE + (j + 1))
                dve.tensor_tensor(split[:, j % SPLIT, 1, :, :], raw[:, slot(MOE0 + j), :, :],
                                  split[:, j % SPLIT, 0, :, :].bitcast(f32), ALU.subtract).then_inc(lo_done, 1)

            def hidden_low(e, k):
                dve.wait_ge(hid_hi, e * 4 + (k + 1))
                dve.tensor_tensor(hid[:, 2 * k:2 * k + 2, 1, :], hid_f[:, k % 2, :, :],
                                  hid[:, 2 * k:2 * k + 2, 0, :].bitcast(f32), ALU.subtract).then_inc(hid_lo, 1)

            def after_product(e, j):
                if j < 8 and j % 2 and j > 1:
                    hidden_low(e, j // 2 - 1)
                if j < 8 and j % 2 and not (isinstance(e, int) and e == 0 and j == 1):
                    dve.wait_ge(mul_done, e * 4 + j // 2)
                k = j // 2 if j < 8 else j - 8
                b = 2 * (j % 3)
                dve.wait_ge(unit_done, e * UPE + (j + 1))
                halves = ps[:, b:b + 2, 0:2 * CAP].rearrange("p c (h n) -> p c n h", h=2)
                if j < 8:
                    dve.tensor_reduce(up_f[:, :, :] if j % 2 else gate_f[:, k % 2, :, :], halves, AX.X, ALU.add)\
                       .then_inc(psum_read, 1)
                else:
                    dve.tensor_reduce(down[:, 2 * k:2 * k + 2, :], halves[:, :, 0:CAP_L, :], AX.X, ALU.add)
                    dve.tensor_reduce(down_c[:, 2 * k:2 * k + 2, :], halves[:, :, CAP_L:CAP, :], AX.X, ALU.add)\
                       .then_inc(psum_read, 1)
                if j < 8 and j % 2:
                    dve.wait_ge(silu_done, e * 4 + (k + 1))
                    dve.wait_ge(psum_read, e * UPE + (j + 1))
                    dve.tensor_tensor(hid_f[:, k % 2, :, :], up_f[:, :, :], gate_s[:, k % 2, :, :], ALU.mult)\
                       .then_inc(mul_done, 1)
                    if k == 3:
                        hidden_low(e, 3)

            def input_c_low(e):
                dve.wait_ge(xt_c_hi, e + 1)
                dve.tensor_tensor(xt[:, :, 1, CAP_L:CAP], ps[:, 0, 0:KC * CAP_C].rearrange("p (k n) -> p k n", k=KC),
                                  xt[:, :, 0, CAP_L:CAP].bitcast(f32), ALU.subtract).then_inc(xt_c_lo, 1)

            def input_low(e):
                dve.wait_ge(xt_hi, e + 1)
                for h in range(2):
                    ins = dve.tensor_tensor(xt[:, 4 * h:4 * h + 4, 1, 0:CAP_L],
                                            ps[:, 6 + h, :].rearrange("p (k n) -> p k n", k=4),
                                            xt[:, 4 * h:4 * h + 4, 0, 0:CAP_L].bitcast(f32), ALU.subtract)
                ins.then_inc(xt_lo, 1)

            def scatter_index(e):
                dve.wait_ge(routed, 8)
                dve.tensor_copy(si_lat[:, :], column(i_lat, e))
                dve.tensor_copy(si_ctx[:, :], column(i_part, e))
                dve.tensor_copy(sg_lat[:, :], column(g_lat, e))
                dve.tensor_copy(sg_ctx[:, :], column(g_part, e)).then_inc(si_ready, 1)

            def scale_rows(e):
                dve.wait_ge(si_ready, e + 1)
                dve.wait_ge(rows_turned, e + 1)
                if isinstance(e, int) and e == NE - 1:
                    for h in range(2):
                        a, b = 512 * h, 512 * h + 512
                        ins = dve.scalar_tensor_tensor(out=o_c[:, a:b], in0=ps[0:CAP_C, 4 + h, :], scalar=g_ctx[:, e:e + 1],
                                                       in1=g2[0:CAP_C, 1, a:b], op0=ALU.mult, op1=ALU.mult)
                else:
                    ins = dve.scalar_tensor_tensor(out=o_part[:, :], in0=ps[:, 4, 0:P], scalar=sg_ctx[:, 0:1],
                                                   in1=g2_part[:, :], op0=ALU.mult, op1=ALU.mult)
                ins.then_inc(ctx_scaled, 1)
                for h in range(2):
                    a, b = 512 * h, 512 * h + 512
                    ins = dve.scalar_tensor_tensor(out=o_l[:, a:b], in0=ps[:, 6 + h, :], scalar=sg_lat[:, 0:1],
                                                   in1=g2[:, 0, a:b], op0=ALU.mult, op1=ALU.mult)
                ins.then_inc(out_scaled, 1)

            def expert(e, is_first, is_last):
                for j in range(UPE):
                    if j == 1 and not is_last:
                        gather_index(e + 1)
                    if j == 1 and not is_first:
                        scatter_index(e - 1)
                    if j == UPE - 1 and not is_first:
                        dve.wait_ge(scattered, e * 32)
                    if j >= LAG:
                        after_product(e, j - LAG)
                    elif not is_first:
                        after_product(e - 1, j - LAG + UPE)
                    if j == 7 + LAG and not is_last:
                        input_c_low(e + 1)
                    if not (is_first and j < LAG):
                        split_low(e, j)
                    if j == LAG and not is_first:
                        scale_rows(e - 1)
                    if j == 7 + LAG and not is_last:
                        input_low(e + 1)
                    if is_last and j >= END_STEP + 1:
                        last_norm(j - END_STEP - 1)

            def last_norm(t):
                dve.wait_ge(g_fin_loaded, 16)
                dve.wait_ge(rstd3_ready, t + 1)
                dve.scalar_tensor_tensor(out=y_end(t), in0=y_end(t), scalar=rstd[:, 2, t:t + 1], in1=g_fin[:, :],
                                         op0=ALU.mult, op1=ALU.mult).then_inc(end_ready, 1)

            gather_index(0)
            for j in range(LAG):
                split_low(0, j)
            dve.wait_ge(parts_spread, 2)
            dve.tensor_copy(g_part[:, :], ps[:, 4, 0:NE]).then_inc(routed, 1)
            dve.tensor_scalar(i_part[:, :], ps[:, 4, NE:2 * NE], float(KC), chunk_no[:, 0:1], ALU.mult, ALU.add)\
               .then_inc(routed, 1)
            dve.tensor_copy(g2_part[:, :], ps[:, 5, 0:P]).then_inc(routed, 1)
            input_c_low(0)
            input_low(0)
            expert(0, True, False)
            with dve.Fori(1, NE - 1) as e:
                expert(e, False, False)
            expert(NE - 1, False, True)
            for j in range(UPE - LAG, UPE):
                after_product(NE - 1, j)
                for t in range(2 * j - 15, min(2 * j - 13, NT - 1)):
                    last_norm(t)
            scatter_index(NE - 1)
            scale_rows(NE - 1)
            last_norm(NT - 1)
            dve.wait_ge(rows_back, 32)
            dve.wait_ge(out_scaled, NE)
            dve.tensor_tensor(x_l[:, :], x_l[:, :], o_l[:, :], ALU.add).then_inc(sum_ready, 1)
            dve.tensor_tensor(x_c[:, :], x_c[:, :], o_c[:, :], ALU.add).then_inc(sum_ready, 1)
            dve.wait_ge(sum_ready, 2)
            dve.wait_ge(rstd4_ready, 1)
            dve.scalar_tensor_tensor(out=x_l[:, :], in0=x_l[:, :], scalar=rstd[:, 3, 0:1], in1=g_fin[:, :],
                                     op0=ALU.mult, op1=ALU.mult).then_inc(last_ready, 1)
            dve.wait_ge(rstd4_ready, 2)
            dve.scalar_tensor_tensor(out=x_c[:, :], in0=x_c[:, :], scalar=rstd[0:CAP_C, 3, 1:2], in1=g_fin[0:CAP_C, :],
                                     op0=ALU.mult, op1=ALU.mult).then_inc(last_ready, 1)

        @block.tensor
        def _(pe):
            pe.wait_ge(ident_loaded, 16)
            pe.wait_ge(rows_loaded, 16 * (len(ROWS) + 1))
            pe.transpose(ps[:, 7, 0:P], rows_in[:, :], ident[:, :]).then_inc(vecs_turned, 1)
            pe.transpose(ps[:, 7, P:P + 8], rows_st[:, :], ident[0:8, 0:8]).then_inc(vecs_turned, 1)

            pe.wait_ge(silu_ready, 1)
            for u in range(NMOD1):
                n = UNIT[("mod", u)]
                pe.wait_ge(loaded[slot(n)], loads(n))
                for k in range(KC):
                    ins = pe.matmul(ps[0:2, u // 2, (u % 2) * UW:(u % 2 + 1) * UW], silu_c[:, k, :], raw[:, slot(n), k, :],
                                    start=(k == 0), stop=(k == KC - 1))
                ins.then_inc(mods_done, 1)
            for ch in range(2 * NMOD1):
                pe.wait_ge(mod_rows_ready, ch // 4 + 1)
                ins = pe.transpose(ps[:, 6, 2 * ch:2 * ch + 2], mod_rows[:, ch * P:(ch + 1) * P], ident[0:2, 0:2])
            ins.then_inc(mod1_turned, 1)

            def modulate(u):
                pe.wait_ge(part_ready, u + 1)
                for i in range(2):
                    for s in range(2):
                        col = 2 * (2 * (NMOD1 + u) + i) + s
                        ins = pe.matmul(ps[:, 6, col:col + 1], part[:, u % 2, s, i * P:(i + 1) * P], ones[:, 0:1],
                                        start=True, stop=True)
                ins.then_inc(mods_done, 1)

            for job in order:
                if job[0] == "M":
                    if job[1] == 1:
                        pe.wait_ge(mod1_ready, 1)
                        pe.wait_ge(ones_ready, 1)
                    if job[1] > 0:
                        modulate(job[1] - 1)
                    continue
                j = JOB[job]
                b = 3 * (j % 2)
                if j >= 2:
                    pe.wait_ge(job_read, j - 1)
                kind, k = job[0], job[1]
                if kind == "x":
                    if k == 0:
                        pe.wait_ge(xn_ready, NT)
                    for t in range(NT):
                        ins = pe.transpose(ps[:, b + t // 4, (t % 4) * P:(t % 4 + 1) * P], x_in[:, t, k * P:(k + 1) * P],
                                           ident[:, :])
                    ins.then_inc(job_done, 1)
                elif kind in IN_CHUNK:
                    ch = IN_CHUNK[kind] + k
                    n = UNIT[("in", ch // 2)]
                    if job == ("L", 0):
                        pe.wait_ge(job_read, KC)
                    pe.wait_ge(loaded[slot(n)], loads(n))
                    for kk in range(KC):
                        for seg in range(3):
                            ins = pe.matmul(ps[:, b + seg, 0:SEG], raw[:, slot(n), kk, (ch % 2) * P:(ch % 2 + 1) * P],
                                            h_t[:, kk, seg * SEG:(seg + 1) * SEG], start=(kk == 0), stop=(kk == KC - 1))
                    ins.then_inc(job_done, 1)
                elif kind == "G":
                    _, k, r, ax = job
                    pe.wait_ge(small_loaded, SMALL)
                    pe.wait_ge(conv_done, k + 1)
                    for seg in range(3):
                        ins = pe.matmul(ps[:, b + seg, 0:SEG], w_gates[:, ax, r, k, :],
                                        xc[:, k % 2, seg * SEG:(seg + 1) * SEG], start=True, stop=True)
                    ins.then_inc(job_done, 1)
                else:
                    pe.wait_ge(pooled, POOL_ORDER.index(k) + 1)
                    for seg in range(3):
                        ins = pe.matmul(ps[:, b + seg, 0:SEG], w_p[:, k, :], y_t[:, k, seg * SEG:(seg + 1) * SEG],
                                        start=True, stop=True)
                    ins.then_inc(job_done, 1)
            modulate(NMOD2 - 1)
            pe.wait_ge(scan_done, 2 * LC)
            pe.transpose(ps[0:8, 7, 0:P], st_out[:, :], ident[:, :]).then_inc(state_turned, 1)

            pe.wait_ge(mod2_ready, 1)
            pe.wait_ge(state_kept, 1)
            pe.wait_ge(ones_ready, 1)
            for q in range(16):
                pe.wait_ge(diag_ready, q + 1)
                if q >= 2:
                    pe.wait_ge(rows_kept, q - 1)
                pe.matmul(ps[:, 6 + q % 2, :], ones[:, :], box[q % 2][:, PH * GRID_W - 512:], start=True, stop=True)\
                  .then_inc(rows_spread, 1)

            pe.wait_ge(job_read, NJOBS)
            pe.wait_ge(gelu_used, LC)
            pe.wait_ge(rows_kept, 16)
            def out_product(s, half, chunks):
                for k in chunks:
                    hi, lo = y_hi[:, s % 2, k, 0:P], y_lo[:, k, tile(s)]
                    for n, (y, w) in enumerate(((hi, w_hi), (hi, w_lo), (lo, w_hi))):
                        ins = pe.matmul(ps[:, 2 * (s % 2) + half, :].rearrange("p (u n) -> p u n", u=2), y,
                                        w[:, 2 * half:2 * half + 2, k, :],
                                        start=(k == 0 and n == 0), stop=(k == KC - 1 and n == 2))
                if half == 1 and chunks[-1] == KC - 1:
                    ins.then_inc(mix_done, 1)

            for s in range(NT + 2):
                if s < NT:
                    if s >= 2:
                        pe.wait_ge(mix_read, s - 1)
                    pe.wait_ge(y_out_lo, s + 1)
                    if s == 0:
                        pe.wait_ge(w_out_lo, 2)
                    out_product(s, 0, range(KC))
                    if s == 0:
                        pe.wait_ge(w_out_lo, D // UW)
                    out_product(s, 1, range(KC - 2))
                if 0 <= s - 2 < NT:
                    t = s - 2
                    pe.wait_ge(probs_ready, t + 1)
                    if t >= 1:
                        pe.wait_ge(aff_ready, t)
                    pe.transpose(ps[0:NE, 7, 0:P], probs[:, t, :], ident[:, :]).then_inc(probs_turned, 1)
                if 0 <= s - 1 < NT:
                    t = s - 1
                    pe.wait_ge(hn2_ready, t + 1)
                    if t >= 1:
                        pe.wait_ge(hn2_t_ready, t)
                    for k in range(KC):
                        ins = pe.transpose(ps[:, 4 + k // 4, (k % 4) * P:(k % 4 + 1) * P], hn2[:, t % 2, k * P:(k + 1) * P],
                                           ident[:, :])
                    ins.then_inc(hn2_turned, 1)
                if s < NT:
                    out_product(s, 1, range(KC - 2, KC))
                if 0 <= s - 1 < NT:
                    t = s - 1
                    pe.wait_ge(hn2_t_ready, t + 1)
                    if t >= 1:
                        pe.wait_ge(exp_ready, t)
                    for k in range(KC):
                        ins = pe.matmul(ps[:, 6, 0:NE], hn2_t[:, t % 2, k, :], w_r[:, k, :],
                                        start=(k == 0), stop=(k == KC - 1))
                    ins.then_inc(logits_done, 1)

            pe.wait_ge(top_ready, 4)
            for n, best in enumerate((top_a, top_af, rev_b, rev_bf)):
                pe.transpose(ps[:, 4, n * NE:(n + 1) * NE], best[:, :], ident[0:NE, 0:NE]).then_inc(top_turned, 1)
            for n, best in enumerate((top_c, top_cf)):
                pe.transpose(ps[0:CAP_C, 5, n * NE:(n + 1) * NE], best[:, :], ident[0:NE, 0:NE]).then_inc(top_turned, 1)

            pe.wait_ge(routed, 5)
            pe.wait_ge(rows_copied, 3)
            pe.matmul(ps[:, 4, 0:2 * NE], spread[:, :], row_data[:, :], start=True, stop=True).then_inc(parts_spread, 1)
            pe.transpose(ps[:, 5, 0:P], g2_cols[:, :], ident[:, :]).then_inc(parts_spread, 1)

            def turn_input(e):
                pe.wait_ge(gathered, e * 32 + 32)
                if not (isinstance(e, int) and e == 0):
                    pe.wait_ge(psum_read, e * UPE - 5)
                    if not (isinstance(e, int) and e == 1):
                        pe.wait_ge(out_scaled, e - 1)
                for k in range(KC):
                    pe.transpose(ps[:, 6 + k // 4, (k % 4) * P:(k % 4 + 1) * P], x_l[:, k * P:(k + 1) * P], ident[:, :])
                for k in range(KC):
                    ins = pe.transpose(ps[:, 0, k * CAP_C:(k + 1) * CAP_C], x_c[:, k * P:(k + 1) * P],
                                       ident[0:CAP_C, 0:CAP_C])
                ins.then_inc(x_turned, 1)

            def turn_rows(e):
                pe.wait_ge(psum_read, e * UPE + UPE)
                if isinstance(e, int) and e == NE - 1:
                    pe.wait_ge(out_scaled, e)
                else:
                    pe.wait_ge(xt_lo, e + 2)
                for k in range(KC):
                    pe.transpose(ps[:, 6 + k // 4, (k % 4) * P:(k % 4 + 1) * P], down[:, k, :], ident[:, :])
                if isinstance(e, int) and e == NE - 1:
                    for k in range(KC):
                        ins = pe.transpose(ps[0:CAP_C, 4 + k // 4, (k % 4) * P:(k % 4 + 1) * P], down_c[:, k, :],
                                           ident[:, :])
                else:
                    ins = pe.transpose(ps[:, 4, 0:P], down_c[:, :, :].rearrange("p k n -> p (k n)"), ident[:, :])
                ins.then_inc(rows_turned, 1)

            def product(e, j, is_last):
                pe.wait_ge(lo_done, e * UPE + (j + 1))
                some = not (isinstance(e, int) and e == 0)
                if some or j >= 3:
                    pe.wait_ge(psum_read, e * UPE + (j - 2))
                if j == 0:
                    pe.wait_ge(xt_lo, e + 1)
                if j == 2 and some:
                    pe.wait_ge(ctx_scaled, e)
                if j == 8:
                    pe.wait_ge(hid_lo, e * 4 + 3)
                if j == 9 and not is_last:
                    pe.wait_ge(xt_c_lo, e + 2)
                src = xt if j < 8 else hid
                for i in range(2):
                    out = ps[:, 2 * (j % 3) + i, :]
                    for c in range(KC):
                        if j == 8 and i == 0 and c == KC - 2:
                            pe.wait_ge(hid_lo, e * 4 + 4)
                        pe.matmul(out[:, 0:2 * CAP], split[:, j % SPLIT, 0, c, i * P:(i + 1) * P],
                                  src[:, c, :, :].rearrange("p h n -> p (h n)"), start=(c == 0), stop=False)
                        ins = pe.matmul(out[:, 0:CAP], split[:, j % SPLIT, 1, c, i * P:(i + 1) * P], src[:, c, 0, :],
                                        start=False, stop=(c == KC - 1))
                ins.then_inc(unit_done, 1)

            def expert(e, is_first, is_last):
                for j in range(UPE):
                    product(e, j, is_last)
                    if j == 0 and not is_first:
                        turn_rows(e - 1)
                    if j == 7 and not is_last:
                        turn_input(e + 1)

            pe.wait_ge(routed, 5)
            turn_input(0)
            expert(0, True, False)
            with pe.Fori(1, NE - 1) as e:
                expert(e, False, False)
            expert(NE - 1, False, True)
            turn_rows(NE - 1)


_INS = ["x_prompt", "x_sample", "state_rglru", "c", "c_ctx", "w_mod", "b_mod", "g_norm_mix", "g_norm_ffn", "w_in",
        "w_pool", "pool_scale", "w_conv", "b_conv", "w_gate_a", "b_gate_a", "w_gate_x", "b_gate_x", "lru_lambda",
        "w_out", "w_router", "w_exp_gate", "w_exp_up", "w_exp_down", "g_final"]
_OUTS = [((1, N_CTX, D), "float32"), ((1, N_LAT, D), "float32"), ((1, 1, 2, LC * P), "float32")]


def window_counts():
    out = np.zeros((NG, GRID_W + GRID_H + N_CTX), np.float32)
    for g in range(NG):
        w, at = 2 ** (g + 1), 0
        for n in (GRID_W, GRID_H, N_CTX):
            t = np.arange(n)
            count = np.minimum(t + w - w // 2, n) - np.maximum(t - w // 2, 0)
            out[g, at:at + n] = 1.0 / count
            at += n
    return out


def kernel(**inputs):
    import concourse.bacc as _bacc
    from concourse import mybir as _mybir
    from concourse.bass_utils import run_bass_kernel_spmd as _run

    nc = _bacc.Bacc("TRN2", target_bir_lowering=False, num_devices=1)
    arrays, args = {}, []
    consts = {"identity": np.eye(P, dtype=np.float32), "inv_count": window_counts(),
              "chunk_numbers": np.repeat(np.arange(KC, dtype=np.float32), CAP_C).reshape(P, 1)}
    for name in _INS + list(consts):
        a = np.ascontiguousarray(inputs[name] if name in inputs else consts[name])
        arrays[f"in_{name}_dram"] = a
        args.append(nc.dram_tensor(f"in_{name}_dram", a.shape, _mybir.dt.from_np(a.dtype), kind="ExternalInput").ap())
    for i, (shape, dtype) in enumerate(_OUTS):
        args.append(nc.dram_tensor(f"out_{i}_dram", shape, _mybir.dt.from_np(np.dtype(dtype)),
                                   kind="ExternalOutput").ap())
    hybrid_step_kernel(nc, *args)
    r = _run(nc, [arrays], core_ids=[0])
    return tuple(r.results[0][f"out_{i}_dram"] for i in range(len(_OUTS)))
```
